# Optimizing a Trainium2 kernel written in Bass

```python
import math
import jax, jax.numpy as jnp
from jax import lax
import numpy as np

D_MODEL = 1024
BATCH = 1
SEQ = 512
DEPTH = 1
DEC_BATCH = 8
DEC_SEQ = 4
PAST_LEN = 256
PAGE_SIZE = 128

HEAD_DIM = 64
H_A = 6
H_B = 6
C_GROUPS = 4
C_GROUP_DIM = 64
W_A = H_A * HEAD_DIM
W_B = H_B * HEAD_DIM
W_C = C_GROUPS * C_GROUP_DIM
MIX_WIDTH = W_A + W_B + W_C
IN_WIDTH = 3 * W_A + 3 * W_B + 2 * W_C
MOBA_BLOCK = 256
MOBA_TOPK = 3
MOBA_QBLOCK = 64
SB_QBLOCK = 128
CHUNK = 128
D_FF = 4 * D_MODEL
DEEPNORM_ALPHA = (2 * DEPTH) ** 0.25
DEEPNORM_BETA = (8 * DEPTH) ** -0.25
LN_EPS = 1e-5

kernel_name = 'hymba_moba_stickbreak_gmlp_deepnorm_step'

def layer_norm(x, g, b):
    xf = x.astype(jnp.float32)
    mu = xf.mean(-1, keepdims=True)
    var = jnp.square(xf - mu).mean(-1, keepdims=True)
    return ((xf - mu) * lax.rsqrt(var + LN_EPS) * g + b).astype(x.dtype)

def alibi_slopes(n):
    def pow2(m):
        start = 2.0 ** (-8.0 / m)
        return [start ** (i + 1) for i in range(m)]
    p = 2 ** int(math.floor(math.log2(n)))
    s = pow2(p)
    if p < n:
        s = s + pow2(2 * p)[0::2][: n - p]
    return jnp.asarray(np.array(s, dtype=np.float32))

def moba_attention(q, k, v, q_pos, slopes, q_block):
    Bn, H, Q, D = q.shape
    L = k.shape[2]
    n_blk = -(-L // MOBA_BLOCK)
    pad = n_blk * MOBA_BLOCK - L
    k = jnp.pad(k, ((0, 0), (0, 0), (0, pad), (0, 0)))
    v = jnp.pad(v, ((0, 0), (0, 0), (0, pad), (0, 0)))
    kb = k.reshape(Bn, H, n_blk, MOBA_BLOCK, D)
    vb = v.reshape(Bn, H, n_blk, MOBA_BLOCK, D)
    k_mean = kb.astype(jnp.float32).mean(3)
    k_sel = min(MOBA_TOPK, n_blk)
    scale = HEAD_DIM ** -0.5
    blk_ids = jnp.arange(n_blk)
    offs = jnp.arange(MOBA_BLOCK)
    bi = jnp.arange(Bn)[:, None, None]
    hi = jnp.arange(H)[None, :, None]

    def attend(args):
        qc, pc = args
        qb = pc.shape[0]
        cur = pc // MOBA_BLOCK
        gate = jnp.einsum('bhqd,bhnd->bhqn', qc.astype(jnp.float32), k_mean)
        gate = jnp.where(blk_ids[None, :] < cur[:, None], gate, -jnp.inf)
        _, top = lax.top_k(gate, k_sel)
        sel_ok = top < cur[:, None]
        cur_b = jnp.broadcast_to(cur[:, None], (Bn, H, qb, 1))
        blocks = jnp.concatenate([top, cur_b], -1)
        ok = jnp.concatenate([sel_ok, jnp.ones(cur_b.shape, bool)], -1)
        ns = blocks.shape[-1]
        flat = blocks.reshape(Bn, H, qb * ns)
        kg = kb[bi, hi, flat].reshape(Bn, H, qb, ns, MOBA_BLOCK, D)
        vg = vb[bi, hi, flat].reshape(Bn, H, qb, ns, MOBA_BLOCK, D)
        kpos = blocks[..., None] * MOBA_BLOCK + offs
        s = jnp.einsum('bhqd,bhqnsd->bhqns', qc, kg).astype(jnp.float32) * scale
        dist = (pc[:, None, None] - kpos).astype(jnp.float32)
        s = s - slopes[:, None, None, None] * dist
        mask = ok[..., None] & (kpos <= pc[:, None, None])
        s = jnp.where(mask, s, -jnp.inf)
        p = jax.nn.softmax(s.reshape(Bn, H, qb, ns * MOBA_BLOCK), axis=-1)
        p = p.reshape(Bn, H, qb, ns, MOBA_BLOCK).astype(v.dtype)
        return jnp.einsum('bhqns,bhqnsd->bhqd', p, vg)

    nq = Q // q_block
    qs = q.reshape(Bn, H, nq, q_block, D).transpose(2, 0, 1, 3, 4)
    ps = q_pos.reshape(nq, q_block)
    out = lax.map(attend, (qs, ps))
    return out.transpose(1, 2, 0, 3, 4).reshape(Bn, H, Q, D)

def stick_breaking_attention(q, k, v, q_pos, q_block):
    Bn, H, Q, D = q.shape
    L = k.shape[2]
    kpos = jnp.arange(L)
    scale = HEAD_DIM ** -0.5

    def attend(args):
        qc, pc = args
        z = jnp.einsum('bhqd,bhld->bhql', qc, k).astype(jnp.float32) * scale
        before = kpos[None, :] < pc[:, None]
        log_keep = jnp.where(before, jax.nn.log_sigmoid(-z), 0.0)
        after = lax.cumsum(log_keep, axis=3, reverse=True) - log_keep
        a = jnp.where(before, jnp.exp(jax.nn.log_sigmoid(z) + after), 0.0)
        return jnp.einsum('bhql,bhld->bhqd', a.astype(v.dtype), v)

    nq = Q // q_block
    qs = q.reshape(Bn, H, nq, q_block, D).transpose(2, 0, 1, 3, 4)
    ps = q_pos.reshape(nq, q_block)
    out = lax.map(attend, (qs, ps))
    return out.transpose(1, 2, 0, 3, 4).reshape(Bn, H, Q, D)

def chunk_spatial_gating(u, v, w_s, b_s):
    Bn, T, G, gd = v.shape
    n = min(T, CHUNK)
    w = jnp.tril(w_s[:, :n, :n])
    vc = v.reshape(Bn, T // n, n, G, gd)
    mix = jnp.einsum('gts,bcsgd->bctgd', w, vc) + jnp.transpose(b_s[:, :n])[:, :, None]
    return u * mix.reshape(Bn, T, G, gd)

def gather_pages(cache_l, page_table):
    g = cache_l[page_table]
    return g.reshape(g.shape[0], g.shape[1] * g.shape[2], g.shape[3], g.shape[4])

def hybrid_layer(h, past, q_pos, moba_qb, sb_qb, slopes, w_in, w_out, w_s, b_s,
                 lnc_g, lnc_b, ln1_g, ln1_b, w_ff1, w_ff2, ln2_g, ln2_b):
    Bn, T, _ = h.shape
    z = h @ w_in
    sizes = (W_A, W_A, W_A, W_B, W_B, W_B, W_C, W_C)
    splits = [sum(sizes[: i + 1]) for i in range(len(sizes) - 1)]
    qa, ka, va, qb, kb, vb, uc, vc = jnp.split(z, splits, axis=-1)
    qa = qa.reshape(Bn, T, H_A, HEAD_DIM)
    ka = ka.reshape(Bn, T, H_A, HEAD_DIM)
    va = va.reshape(Bn, T, H_A, HEAD_DIM)
    qb = qb.reshape(Bn, T, H_B, HEAD_DIM)
    kb = kb.reshape(Bn, T, H_B, HEAD_DIM)
    vb = vb.reshape(Bn, T, H_B, HEAD_DIM)
    if past is None:
        fka, fva, fkb, fvb = ka, va, kb, vb
    else:
        pka, pva, pkb, pvb = past
        fka = jnp.concatenate([pka, ka], axis=1)
        fva = jnp.concatenate([pva, va], axis=1)
        fkb = jnp.concatenate([pkb, kb], axis=1)
        fvb = jnp.concatenate([pvb, vb], axis=1)
    bhld = lambda t: t.transpose(0, 2, 1, 3)
    o_a = moba_attention(bhld(qa), bhld(fka), bhld(fva), q_pos, slopes, moba_qb)
    o_b = stick_breaking_attention(bhld(qb), bhld(fkb), bhld(fvb), q_pos, sb_qb)
    uc = jax.nn.gelu(uc).reshape(Bn, T, C_GROUPS, C_GROUP_DIM)
    vc = layer_norm(jax.nn.gelu(vc).reshape(Bn, T, C_GROUPS, C_GROUP_DIM), lnc_g, lnc_b)
    o_c = chunk_spatial_gating(uc, vc, w_s, b_s)
    mixed = jnp.concatenate([
        o_a.transpose(0, 2, 1, 3).reshape(Bn, T, W_A),
        o_b.transpose(0, 2, 1, 3).reshape(Bn, T, W_B),
        o_c.reshape(Bn, T, W_C)], axis=-1)
    h = layer_norm(DEEPNORM_ALPHA * h + mixed @ w_out, ln1_g, ln1_b)
    f = jnp.square(jax.nn.relu(h @ w_ff1)) @ w_ff2
    h = layer_norm(DEEPNORM_ALPHA * h + f, ln2_g, ln2_b)
    return h, (ka, va, kb, vb, vc.reshape(Bn, T, W_C))

def setup_inputs(seed: int = 0) -> dict:
    key = jax.random.key(seed)
    ks = jax.random.split(key, 24)
    n_pages = PAST_LEN // PAGE_SIZE
    n_used = DEC_BATCH * n_pages
    n_pool = n_used + n_used // 4
    f32 = jnp.float32
    nrm = lambda k, shape, s: jax.random.normal(k, shape, f32) * s
    cshape = (DEPTH, n_pool, PAGE_SIZE, H_A, HEAD_DIM)
    cshape_b = (DEPTH, n_pool, PAGE_SIZE, H_B, HEAD_DIM)
    page_table = jax.random.permutation(ks[6], n_pool)[:n_used].astype(jnp.int32).reshape(DEC_BATCH, n_pages)
    w_in = nrm(ks[7], (DEPTH, D_MODEL, IN_WIDTH), D_MODEL ** -0.5)
    col = jnp.arange(IN_WIDTH)
    is_value = ((col >= 2 * W_A) & (col < 3 * W_A)) | ((col >= 3 * W_A + 2 * W_B) & (col < 3 * W_A + 3 * W_B))
    w_in = w_in * jnp.where(is_value, DEEPNORM_BETA, 1.0).astype(f32)
    return {
        'x_prompt': nrm(ks[0], (BATCH, SEQ, D_MODEL), 1.0),
        'x_sample': nrm(ks[1], (DEC_BATCH, DEC_SEQ, D_MODEL), 1.0),
        'cache_k_a': nrm(ks[2], cshape, 1.0),
        'cache_v_a': nrm(ks[3], cshape, 1.0),
        'cache_k_b': nrm(ks[4], cshape_b, 1.0),
        'cache_v_b': nrm(ks[5], cshape_b, 1.0),
        'page_table': page_table,
        'ln_in_g': 1.0 + nrm(ks[8], (D_MODEL,), 0.02),
        'ln_in_b': nrm(ks[9], (D_MODEL,), 0.02),
        'w_in': w_in,
        'w_out': nrm(ks[10], (DEPTH, MIX_WIDTH, D_MODEL), MIX_WIDTH ** -0.5 * DEEPNORM_BETA),
        'w_spatial': nrm(ks[11], (DEPTH, C_GROUPS, CHUNK, CHUNK), CHUNK ** -0.5),
        'b_spatial': 1.0 + nrm(ks[12], (DEPTH, C_GROUPS, CHUNK), 0.1),
        'ln_c_g': 1.0 + nrm(ks[13], (DEPTH, C_GROUPS, C_GROUP_DIM), 0.02),
        'ln_c_b': nrm(ks[14], (DEPTH, C_GROUPS, C_GROUP_DIM), 0.02),
        'ln1_g': 1.0 + nrm(ks[15], (DEPTH, D_MODEL), 0.02),
        'ln1_b': nrm(ks[16], (DEPTH, D_MODEL), 0.02),
        'w_ff1': nrm(ks[17], (DEPTH, D_MODEL, D_FF), D_MODEL ** -0.5 * DEEPNORM_BETA),
        'w_ff2': nrm(ks[18], (DEPTH, D_FF, D_MODEL), D_FF ** -0.5 * DEEPNORM_BETA),
        'ln2_g': 1.0 + nrm(ks[19], (DEPTH, D_MODEL), 0.02),
        'ln2_b': nrm(ks[20], (DEPTH, D_MODEL), 0.02),
    }

def reference(x_prompt, x_sample, cache_k_a, cache_v_a, cache_k_b, cache_v_b, page_table,
              ln_in_g, ln_in_b, w_in, w_out, w_spatial, b_spatial, ln_c_g, ln_c_b,
              ln1_g, ln1_b, w_ff1, w_ff2, ln2_g, ln2_b):
    slopes = alibi_slopes(H_A)
    hp = layer_norm(x_prompt, ln_in_g, ln_in_b)
    hs = layer_norm(x_sample, ln_in_g, ln_in_b)
    pos_p = jnp.arange(SEQ, dtype=jnp.int32)
    pos_s = PAST_LEN + jnp.arange(DEC_SEQ, dtype=jnp.int32)
    st_p = []
    st_s = []
    for l in range(DEPTH):
        params = (w_in[l], w_out[l], w_spatial[l], b_spatial[l], ln_c_g[l], ln_c_b[l],
                  ln1_g[l], ln1_b[l], w_ff1[l], w_ff2[l], ln2_g[l], ln2_b[l])
        hp, sp = hybrid_layer(hp, None, pos_p, min(MOBA_QBLOCK, SEQ), min(SB_QBLOCK, SEQ), slopes, *params)
        past = (gather_pages(cache_k_a[l], page_table), gather_pages(cache_v_a[l], page_table),
                gather_pages(cache_k_b[l], page_table), gather_pages(cache_v_b[l], page_table))
        hs, ss = hybrid_layer(hs, past, pos_s, 1, DEC_SEQ, slopes, *params)
        st_p.append(sp)
        st_s.append(ss)
    k_a_prompt = jnp.stack([s[0] for s in st_p])
    v_a_prompt = jnp.stack([s[1] for s in st_p])
    k_b_prompt = jnp.stack([s[2] for s in st_p])
    v_b_prompt = jnp.stack([s[3] for s in st_p])
    k_a_sample = jnp.stack([s[0] for s in st_s])
    v_a_sample = jnp.stack([s[1] for s in st_s])
    k_b_sample = jnp.stack([s[2] for s in st_s])
    v_b_sample = jnp.stack([s[3] for s in st_s])
    v_c_sample = jnp.stack([s[4] for s in st_s])
    return (hp, hs, k_a_prompt, v_a_prompt, k_b_prompt, v_b_prompt,
            k_a_sample, v_a_sample, k_b_sample, v_b_sample, v_c_sample)


_drawn_inputs = setup_inputs


def setup_inputs(seed=0):
    import zlib

    import numpy as np

    out = dict(_drawn_inputs(seed))
    spreads = {}
    factors = {'b_spatial': 2.86,
     'ln_c_b': 2.917,
     'ln1_g': 7.824,
     'ln1_b': 7.8,
     'ln2_g': 8.055,
     'ln2_b': 8.361}
    for name, (base, spread) in spreads.items():
        noise = np.random.default_rng([zlib.crc32(name.encode()), seed]).standard_normal(out[name].shape)
        drawn = base * np.exp(spread * noise) if base else spread * noise
        out[name] = __import__('jax').numpy.asarray(drawn.astype(out[name].dtype))
    for name, factor in factors.items():
        out[name] = (out[name] * factor).astype(out[name].dtype)
    return out
```

```python
from contextlib import ExitStack

import numpy as np

import concourse.bass as bass
from concourse import mybir

ALU = mybir.AluOpType
ACT = mybir.ActivationFunctionType
AX_X = mybir.AxisListType.X
F32 = mybir.dt.float32
F32R = mybir.dt.float32r
I32 = mybir.dt.int32

P = 128
D_MODEL = 1024
KT = D_MODEL // P
SEQ = 512
NB = 8
NQ = 4
NS = NB * NQ
T = SEQ + NS
HALF = T // 2
QT = SEQ // P
HD = 64
H = 6
PAIRS = H // 2
W_ATT = H * HD
GROUPS = 4
W_C = GROUPS * HD
PAST = 256
PAGE = 128
PAGES = PAST // PAGE
CHUNK = 128
D_FF = 4 * D_MODEL
SCALE = HD ** -0.5
ALPHA = 2 ** 0.25
EPS = 1e-5
MOBA_BLOCK = 256
MOBA_TOPK = 3
assert max(SEQ, PAST + NQ) <= 2 * MOBA_BLOCK and MOBA_TOPK >= 2
SLOPES = [0.25, 0.0625, 0.015625, 0.00390625, 0.5, 0.125]
NEG = -1e30
SK = PAST + NS

IN_UNITS = 22
OUT_UNITS = D_MODEL // P
FG = 4
NG = D_FF // (P * FG)
FF_UNITS = 2 * NG * FG
UNITS = IN_UNITS + OUT_UNITS + FF_UNITS
STAGE = 2
RING = 4

def _pack(*sizes):
    at, out = 0, {}
    for name, cols in sizes:
        out[name] = (at, cols)
        at += cols
    return out, at


CONST, CONSTS = _pack(("ident", P), ("dist", SEQ), ("below", P), ("below_neg", P), ("upto", P), ("mean", P))
S_CONST, S_CONSTS = _pack(("s_bias", 2 * SK), ("s_keep", 2 * SK), ("s_neg", 2 * SK), ("s_head", W_ATT),
                          ("s_pick", 16), ("s_chunk", NS))


def hybrid_layer(nc, x_prompt, x_sample, weights, cache_k_a, cache_v_a, cache_k_b, cache_v_b,
                 page_table, ln_cols, w_spatial, b_spatial, lnc_g, lnc_b, ln2_g, ln2_b, consts, s_consts,
                 y_prompt, y_sample, k_a_prompt, v_a_prompt, k_b_prompt, v_b_prompt,
                 k_a_sample, v_a_sample, k_b_sample, v_b_sample, v_c_sample):
    n_pool = cache_k_a.shape[1]
    caches = [[c.rearrange("l n p h d -> (l n) p (h d)") for c in kv]
              for kv in ((cache_k_a, cache_v_a), (cache_k_b, cache_v_b))]
    x_rows = [x_prompt[0, t * P:(t + 1) * P, :] for t in range(QT)]
    x_rows.append(x_sample.rearrange("b t d -> (b t) d"))
    kv_prompt = [[o.rearrange("l b (t p) h d -> p (l b t) (h d)", p=P) for o in kv]
                 for kv in ((k_a_prompt, v_a_prompt), (k_b_prompt, v_b_prompt))]
    kv_sample = [[o.rearrange("l b t h d -> (l b t) (h d)") for o in kv]
                 for kv in ((k_a_sample, v_a_sample), (k_b_sample, v_b_sample))]
    rows = [P] * QT + [NS]

    with ExitStack() as ctx:
        def sb(name, shape, dt=F32, to=None):
            return (to or ctx).enter_context(nc.sbuf_tensor(name, shape, dt))

        def sem(name):
            return ctx.enter_context(nc.semaphore(name))

        cst = sb("cst", [P, CONSTS])
        h_hi = sb("h_hi", [P, KT, T], F32R)
        h_lo = sb("h_lo", [P, KT, T], F32R)
        res = sb("res", [P, KT, T])
        m_hi = sb("m_hi", [P, KT, T], F32R)
        m_lo = sb("m_lo", [P, KT, T], F32R)
        w_raw = sb("w_raw", [P, STAGE, KT * P])
        w_hi = sb("w_hi", [P, RING, KT * P], F32R)
        w_lo = sb("w_lo", [P, RING, KT * P], F32R)
        lnp = sb("lnp", [P, 4, KT])
        eps = sb("eps", [P, 1])

        ph = ExitStack()
        xin = sb("xin", [P, QT + 1, D_MODEL], to=ph)
        x_st = sb("x_st", [P, QT + 1, 12], to=ph)
        x_mv = sb("x_mv", [P, QT + 1, 2], to=ph)
        x_sd = sb("x_sd", [P, QT + 1], to=ph)
        x_rs = sb("x_rs", [P, QT + 1], to=ph)
        ph.close()

        after_x = ExitStack()
        z_c = sb("z_c", [P, 4, T], to=after_x)
        qbd = [sb(f"qbd{y}", [P, NB, PAIRS, 32], to=after_x) for y in range(2)]
        k_new = [sb(f"k_new{y}", [P, PAIRS, NS], to=after_x) for y in range(2)]
        kv_new = [sb(f"kv_new{y}", [NS, 2, W_ATT], to=after_x) for y in range(2)]

        pr = ExitStack()
        z = [sb(f"z{y}", [P, 3, T], to=pr) for y in range(2)]
        strip = sb("strip", [P, H, SEQ], to=pr)
        k_tok = [sb(f"k_tok{y}", [P, QT, P], to=pr) for y in range(2)]
        v_tok = [sb(f"v_tok{y}", [P, QT, P], to=pr) for y in range(2)]
        wk = [sb(f"wk{j}", [P, 2, SEQ], to=pr) for j in range(2)]
        prob = sb("prob", [P, 2, SEQ], to=pr)
        prob_t = [sb(f"prob_t{h}", [P, QT * (QT + 1) // 2, P], to=pr) for h in range(2)]
        mx = sb("mx", [P, 2], to=pr)
        nmx = sb("nmx", [P, 2], to=pr)
        rsum = sb("rsum", [P, 2], to=pr)
        rinv = sb("rinv", [P, 2], to=pr)
        pr.close()

        sa = ExitStack()
        s_cst = sb("s_cst", [P, S_CONSTS], to=sa)
        vt = sb("vt", [P, QT + 1, W_C], to=sa)
        vsq = sb("vsq", [P, QT + 1, W_C], to=sa)
        v_s = sb("v_s", [P, 4, (QT + 1) * GROUPS], to=sa)
        lnc = sb("lnc", [P, 2, W_C], to=sa)
        wsp = sb("wsp", [P, GROUPS, CHUNK], to=sa)
        wbd = sb("wbd", [NS, GROUPS, NS], to=sa)
        bsp = sb("bsp", [P, 2, CHUNK], to=sa)
        ptab = sb("ptab", [1, NB * PAGES], I32, to=sa)
        k_pg = sb("k_pg", [P, 2, PAGES, W_ATT], to=sa)
        v_pg = sb("v_pg", [P, 4, PAGES, W_ATT], to=sa)
        k_t = [sb(f"k_t{j}", [P, PAIRS, SK], to=sa) for j in range(2)]
        sw = [sb(f"sw{j}", [P, SK], to=sa) for j in range(2)]
        s_prob = sb("s_prob", [P, SK], to=sa)
        s_pt = sb("s_pt", [P, 3, P], to=sa)
        s_om = sb("s_om", [P, W_ATT], to=sa)
        s_st = sb("s_st", [P, 4], to=sa)
        sa.close()
        after_x.close()

        ff = ExitStack()
        mean_b = sb("mean_b", [P, T], to=ff)
        sd_b = sb("sd_b", [P, T], to=ff)
        rstd_b = sb("rstd_b", [P, T], to=ff)
        sq = sb("sq", [P, 2, T], to=ff)
        relu = sb("relu", [P, 2, T], to=ff)
        hid = sb("hid", [P, 2, T], to=ff)
        ln2 = sb("ln2", [P, 2, D_MODEL], to=ff)
        y_n = sb("y_n", [P, 2, D_MODEL], to=ff)
        y_st = sb("y_st", [P, QT + 1, 12], to=ff)
        y_mv = sb("y_mv", [P, QT + 1, 2], to=ff)
        y_sd = sb("y_sd", [P, QT + 1], to=ff)
        y_rs = sb("y_rs", [P, QT + 1], to=ff)
        ff.close()

        acc = ctx.enter_context(nc.psum_tensor("acc", [P, 4, 512], F32))
        s_bank = [ctx.enter_context(nc.psum_tensor(f"s_bank{j}", [P, 512], F32)) for j in range(2)]
        t_bank = ctx.enter_context(nc.psum_tensor("t_bank", [P, 512], F32))
        o_bank = ctx.enter_context(nc.psum_tensor("o_bank", [P, 512], F32))

        def c_(name, r=P, lo=0, hi=None):
            where, t = (CONST, cst) if name in CONST else (S_CONST, s_cst)
            at, n = where[name]
            return t[0:r, at + lo:at + (n if hi is None else hi)]

        def ident(r):
            return c_("ident", r, 0, r)

        x_loaded = [sem(f"x_loaded{t}") for t in range(QT + 1)]
        const_loaded = sem("const_loaded")
        row_loaded = sem("row_loaded")
        w_loaded = [sem(f"w_loaded{j}") for j in range(STAGE)]
        hi_done, lo_done = sem("hi_done"), sem("lo_done")
        half_done = sem("half_done")
        acc_act, acc_dve = sem("acc_act"), sem("acc_dve")
        x_stat, x_std, x_norm = sem("x_stat"), sem("x_std"), sem("x_norm")
        xt_ready, res_ready, hhi_ready, h_ready = sem("xt_ready"), sem("res_ready"), sem("hhi_ready"), sem("h_ready")
        init = sem("init")
        z_copied, q_copied = sem("z_copied"), sem("q_copied")
        kv_t, kv_act, kv_dve = sem("kv_t"), sem("kv_act"), sem("kv_dve")
        kv_out = [sem(f"kv_out{y}") for y in range(2)]
        s_ready, s_read = sem("s_ready"), sem("s_read")
        st1, st2, st3, st4 = sem("st1"), sem("st2"), sem("st3"), sem("st4")
        softplus_e, softplus = sem("softplus_e"), sem("softplus")
        d1, d2, d3, d4, d5 = sem("d1"), sem("d2"), sem("d3"), sem("d4"), sem("d5")
        p_written, p_scaled, p_sum = sem("p_written"), sem("p_scaled"), sem("p_sum")
        pt_ready, pt_read = sem("pt_ready"), sem("pt_read")
        o_ready, mhi_ready, m_ready = sem("o_ready"), sem("mhi_ready"), sem("m_ready")
        gelu_done, vt_ready, vt_read, v_chain, v_sq = sem("gelu_done"), sem("vt_ready"), sem("vt_read"), sem("v_chain"), sem("v_sq")
        mix_ready, mix_dve, mix_hi, mix_lo = sem("mix_ready"), sem("mix_dve"), sem("mix_hi"), sem("mix_lo")
        wsp_ready, g_loaded = sem("wsp_ready"), sem("g_loaded")
        pt_loaded = sem("pt_loaded")
        kp_loaded = [sem(f"kp_loaded{j}") for j in range(2)]
        vp_loaded = [sem(f"vp_loaded{j}") for j in range(4)]
        kt_pe, kt_act, kt_dve, sc_pe = sem("kt_pe"), sem("kt_act"), sem("kt_dve"), sem("sc_pe")
        tail_done = sem("tail_done")
        ss_read, e1, e2, e3, sp_written = sem("ss_read"), sem("e1"), sem("e2"), sem("e3"), sem("sp_written")
        st_pe, st_act, pv_pe, om_done, ot_pe, ot_hi, ot_lo = (sem(n) for n in ("st_pe", "st_act", "pv_pe", "om_done", "ot_pe", "ot_hi", "ot_lo"))
        r_ready, mean_pe, mean_sb, cent, sq_done, sq_pe, std_done, rstd_done = (sem(n) for n in ("r_ready", "mean_pe", "mean_sb", "cent", "sq_done", "sq_pe", "std_done", "rstd_done"))
        nrm, x1_done, h1_hi, h1_lo, res_a = (sem(n) for n in ("nrm", "x1_done", "h1_hi", "h1_lo", "res_a"))
        relu_act, relu_dve, sq_h, hid_hi, hid_lo = (sem(n) for n in ("relu_act", "relu_dve", "sq_h", "hid_hi", "hid_lo"))
        yt_pe, yt_read, y_c, y_std, y_nrm, y_g, y_b, ln2_loaded = (sem(n) for n in ("yt_pe", "yt_read", "y_c", "y_std", "y_nrm", "y_g", "y_b", "ln2_loaded"))
        y_out = [sem(f"y_out{j}") for j in range(2)]
        out_s = sem("out_s")
        d0, e4, y_rec = sem("d0"), sem("e4"), sem("y_rec")

        def y_banks(t):
            return ((acc[:, 0, :], acc[:, 1, :]), (acc[:, 2, :], acc[:, 3, :]),
                    (s_bank[0][:, :], s_bank[1][:, :]), (t_bank[:, :], o_bank[:, :]))[t % 4]

        block = ctx.enter_context(nc.Block())

        MLP_HEAD = [("up", 0), ("up", 1), ("down", 0)]
        MLP_BODY = [("up", 2), ("down", 1), ("up", 3), ("down", 2)]
        MLP_ROUNDS = (NG - 2) // 2
        MLP_TAIL = [("down", NG - 1)]
        UPS, DOWNS = FG, KT
        FF0 = IN_UNITS + OUT_UNITS

        def act_reads(n):
            return min(n, IN_UNITS)

        def dve_reads(n):
            return min(n, IN_UNITS) + 2 * max(0, n - IN_UNITS)

        ACT0, DVE0 = act_reads(FF0), dve_reads(FF0)

        def mlp(eng, segment):
            up = {"unit": FG, "tile": UPS, "act": UPS, "dve": UPS, "up": 1, "down": 0}
            down = {"unit": FG, "tile": DOWNS, "act": 0, "dve": 2 * DOWNS, "up": 0, "down": 1}
            before = ["down"]

            def run(c, segments):
                for kind, g in segments:
                    segment(kind, g % 2, before[0], c)
                    before[0] = kind
                    c = {k: c[k] + (up if kind == "up" else down)[k] for k in c}
                return c

            c = run({"unit": FF0, "tile": FF0, "act": ACT0, "dve": DVE0, "up": 0, "down": 0}, MLP_HEAD)
            with eng.Fori(0, MLP_ROUNDS) as i:
                run({k: i * (2 * up[k] + 2 * down[k]) + c[k] for k in c}, MLP_BODY)
            run({k: c[k] + MLP_ROUNDS * (2 * up[k] + 2 * down[k]) for k in c}, MLP_TAIL)

        @block.sync
        def _(sp):
            sp.dma_start(cst[:, :], consts).then_inc(const_loaded, 16)
            sp.dma_start(lnp[:, :, :], ln_cols).then_inc(const_loaded, 16)
            for t in range(QT + 1):
                sp.dma_start(xin[0:rows[t], t, :], x_rows[t]).then_inc(x_loaded[t], 16)

            def load_unit(u, slot, count):
                if count is not None:
                    sp.wait_ge(lo_done, count)
                sp.dma_start(w_raw[:, slot, :], weights[u]).then_inc(w_loaded[slot], 16)

            for u in range(IN_UNITS + STAGE):
                load_unit(u, u % STAGE, u - STAGE + 1 if u >= STAGE else None)
            sp.wait_ge(m_ready, 6)
            sp.wait_ge(kv_out[0], 16 * 6)
            sp.wait_ge(kv_out[1], 16 * 6)
            sp.dma_start(ptab[:, :], page_table.rearrange("(a b) p -> a (b p)", a=1)).then_inc(pt_loaded, 16)
            sp.dma_start(s_cst[:, :], s_consts).then_inc(g_loaded, 16)
            for j, row in enumerate((lnc_g, lnc_b)):
                sp.dma_start(lnc[:, j, :], row.to_broadcast([P, W_C])).then_inc(g_loaded, 16)
            sp.dma_start(wsp[:, :, :], w_spatial).then_inc(g_loaded, 16)
            for g in range(GROUPS):
                j, g2 = divmod(g, 2)
                sp.dma_start(bsp[HD * g2:HD * (g2 + 1), j, :],
                             b_spatial[g:g + 1, :].to_broadcast([HD, CHUNK])).then_inc(g_loaded, 16)
            sp.wait_ge(init, 11)
            for b in range(NB):
                sp.dma_start(wbd[NQ * b:NQ * (b + 1), :, NQ * b:NQ * (b + 1)],
                             w_spatial[0:NQ, :, 0:NQ]).then_inc(g_loaded, 16)
            sp.wait_ge(pt_loaded, 16)
            pages = [sp.value_load(ptab[0:1, n:n + 1], min_val=0, max_val=n_pool - 1)
                     for n in range(NB * PAGES)]
            for y in range(2):
                for grp in range(2):
                    gi = 2 * y + grp
                    for b4 in range(4):
                        n = 4 * gi + b4
                        if n >= 2:
                            sp.wait_ge(kt_pe, n - 1)
                        for pg in range(PAGES):
                            src = caches[y][0][pages[PAGES * (4 * grp + b4) + pg]]
                            sp.dma_start(k_pg[:, n % 2, pg, :], src).then_inc(kp_loaded[n % 2], 16)
                    if gi:
                        sp.wait_ge(pv_pe, gi)
                    for b4 in range(4):
                        for pg in range(PAGES):
                            src = caches[y][1][pages[PAGES * (4 * grp + b4) + pg]]
                            sp.dma_start(v_pg[:, b4, pg, :], src).then_inc(vp_loaded[b4], 16)
            for u in range(IN_UNITS + STAGE, FF0):
                load_unit(u, u % STAGE, u - STAGE + 1)

            def segment(kind, par, prev, c):
                for j in range(FG):
                    load_unit(c["unit"] + j, (FF0 + j) % STAGE, c["unit"] + (j - STAGE + 1))
            mlp(sp, segment)
            sp.wait_ge(res_a, KT)
            for j, row in enumerate((ln2_g, ln2_b)):
                sp.dma_start(ln2[:, j, :], row.to_broadcast([P, D_MODEL])).then_inc(ln2_loaded, 16)
            for t in range(QT + 1):
                sp.wait_ge(y_b, t + 1)
                dst = y_prompt[0, P * t:P * (t + 1), :] if t < QT else y_sample.rearrange("b t d -> (b t) d")
                sp.dma_start(dst, y_n[0:rows[t], t % 2, :]).then_inc(y_out[t % 2], 16)
            for t in range(2):
                sp.wait_ge(y_out[t], 16 * ((QT + 2 - t) // 2))
                sp.wait_ge(kv_out[t], 16 * 6)
            sp.wait_ge(out_s, 16 * 5)

        @block.gpsimd
        def _(pool):
            def lo_part(slot, stage, u):
                pool.wait_ge(hi_done, u + 1)
                pool.tensor_tensor(w_lo[:, slot, :], w_raw[:, stage, :],
                                   w_hi[:, slot, :].bitcast(F32), ALU.subtract).then_inc(lo_done, 1)

            pool.memset(eps[:, :], EPS).then_inc(init, 1)
            for k in range(KT):
                pool.wait_ge(hhi_ready, k + 1)
                pool.tensor_tensor(h_lo[:, k, :], res[:, k, :], h_hi[:, k, :].bitcast(F32),
                                   ALU.subtract).then_inc(h_ready, 1)
                if k < 3:
                    lo_part(k, k % STAGE, k)
            pool.wait_ge(xt_ready, KT)
            for y in range(2):
                pool.memset(qbd[y][:, :, :, :], 0.0).then_inc(init, 1)
            for h in range(H):
                pool.tensor_scalar(strip[:, h, :], c_("dist"), SLOPES[h], None, ALU.mult).then_inc(init, 1)
            pool.wait_ge(init, 3)
            for u in range(3, IN_UNITS):
                lo_part(u % RING, u % STAGE, u)
                if u >= 5 and (u - 5) % 3 == 0:
                    i = (u - 5) // 3
                    y, p = i % 2, i // 2
                    pool.wait_ge(acc_act, 3 * i + 3)
                    pool.wait_ge(acc_dve, 3 * i + 3)
                    pool.wait_ge(lo_done, u + 1)
                    for h in range(2):
                        r = slice(HD * h, HD * (h + 1))
                        pool.tensor_copy(qbd[y][r, :, p, 8 * p + NQ * h:8 * p + NQ * (h + 1)],
                                         z[y][r, 0, SEQ:T].rearrange("d (b q) -> d b q", q=NQ)).then_inc(q_copied, 1)
                        pool.wait_ge(q_copied, 2 * i + h + 1)
                    pool.tensor_copy(k_new[y][:, p, :], z[y][:, 1, SEQ:T]).then_inc(z_copied, 1)
            pool.wait_ge(m_ready, 6)
            pool.wait_ge(kv_out[0], 16 * 6)
            pool.wait_ge(kv_out[1], 16 * 6)
            pool.memset(vt[:, QT, :], 0.0).then_inc(init, 1)
            pool.memset(wbd[:, :, :], 0.0).then_inc(init, 1)
            pool.wait_ge(g_loaded, 16 * (4 + GROUPS + NB))
            for g in range(GROUPS):
                pool.tensor_tensor(wsp[:, g, :], wsp[:, g, :], c_("upto"), ALU.mult).then_inc(wsp_ready, 1)
                pool.tensor_tensor(wbd[:, g, :], wbd[:, g, :], c_("s_chunk", NS), ALU.mult).then_inc(wsp_ready, 1)
            for j in range(2):
                pool.tensor_copy(k_t[j][:, :, PAST:SK], k_new[0][:, :, :]).then_inc(tail_done, 1)
            for u in range(IN_UNITS, IN_UNITS + STAGE):
                lo_part(u % RING, u % STAGE, u)
            for j in range(2):
                pool.wait_ge(sc_pe, NB - 1 + j)
                pool.tensor_copy(k_t[j][:, :, PAST:SK], k_new[1][:, :, :]).then_inc(tail_done, 1)
            for u in range(IN_UNITS + STAGE, FF0 + RING):
                lo_part(u % RING, u % STAGE, u)
            for k in range(KT):
                pool.wait_ge(h1_lo, k + 1)
                pool.tensor_scalar(res[:, k, :], res[:, k, :], ALPHA, None, ALU.mult).then_inc(res_a, 1)

            first = [True]

            def segment(kind, par, prev, c):
                if first[0]:
                    first[0] = False
                    return
                for j in range(FG):
                    lo_part((FF0 + j) % RING, (FF0 + j) % STAGE, c["unit"] + j)
            mlp(pool, segment)

            pool.wait_ge(ln2_loaded, 32)
            for t in range(QT + 1):
                pool.wait_ge(y_g, t + 1)
                pool.tensor_tensor(y_n[0:rows[t], t % 2, :], y_n[0:rows[t], t % 2, :],
                                   ln2[0:rows[t], 1, :], ALU.add).then_inc(y_b, 1)

        @block.scalar
        def _(act):
            def hi_part(slot, stage, u, used, loaded):
                if used is not None:
                    act.wait_ge(half_done, used)
                act.wait_ge(w_loaded[stage], loaded)
                act.activation(w_hi[:, slot, :], w_raw[:, stage, :], ACT.Copy).then_inc(hi_done, 1)

            def hi_unit(u):
                hi_part(u % RING, u % STAGE, u, 2 * (u - RING + 1) if u >= RING else None, 16 * (u // STAGE + 1))

            hi_unit(0)
            act.wait_ge(init, 1)
            act.wait_ge(x_stat, 3 * (QT + 1))
            act.activation(x_sd[:, :], x_mv[:, :, 1], ACT.Sqrt, bias=eps[:, 0:1]).then_inc(x_std, 1)
            for k in range(KT):
                act.wait_ge(res_ready, 2 * (k + 1))
                act.activation(h_hi[:, k, :], res[:, k, :], ACT.Copy).then_inc(hhi_ready, 1)
                if k < 2:
                    hi_unit(1 + k)
            hi_unit(3)

            def read_half(u):
                i, j = divmod(u, 3)
                act.wait_ge(half_done, 2 * u + 1)
                if u < 18:
                    y = i % 2
                    if i >= 2 and j == 0:
                        act.wait_ge(z_copied, i - 1)
                    dst = z[y][:, j, 0:HALF]
                else:
                    dst = z_c[:, u - 18, 0:HALF]
                act.activation(dst, acc[:, 2 * (u % 2), 0:HALF], ACT.Copy,
                               scale=SCALE if (u < 18 and j == 0) else 1.0).then_inc(acc_act, 1)
                if u + RING < IN_UNITS + STAGE:
                    hi_unit(u + RING)

            for u in range(3):
                read_half(u)

            def item(i, s):
                return s // 2, s % 2, s % 2, 8 * i + s

            for i in range(6):
                y, p = i % 2, i // 2
                for dst, bank, w in ((k_tok, t_bank, 1), (v_tok, o_bank, 2)):
                    act.wait_ge(kv_t, 3 * i + w)
                    if i >= 2:
                        act.wait_ge(kv_out[y], 32 * (i // 2))
                    act.activation(dst[y][:, :, :], bank[:, :], ACT.Copy).then_inc(kv_act, 1)
                act.wait_ge(kv_act, 2 * i + 2)
                act.dma_start(kv_prompt[y][0][:, :, P * p:P * (p + 1)], k_tok[y][:, :, :]).then_inc(kv_out[y], 16)
                act.dma_start(kv_prompt[y][1][:, :, P * p:P * (p + 1)], v_tok[y][:, :, :]).then_inc(kv_out[y], 16)

                def exp_a(s):
                    t, h, b, n = item(i, s)
                    L = P * (t + 1)
                    act.wait_ge(st2, 8 * (i // 2) + s + 1)
                    if n >= 2:
                        act.wait_ge(pt_ready, n - 1)
                    act.activation(prob[:, b, 0:L], wk[0][:, b, 0:L], ACT.Exp, bias=nmx[:, b:b + 1],
                                   accum_out=rsum[:, b:b + 1]).then_inc(p_written, 1)

                def softplus_b(s):
                    t, h, b, n = item(i, s)
                    L = P * (t + 1)
                    a = 8 * (i // 2) + s
                    act.wait_ge(s_ready, n + 1)
                    act.wait_ge(p_written, n - 1)
                    act.activation(wk[0][:, b, 0:L], s_bank[b][:, 0:L], ACT.Abs).then_inc(d1, 1)
                    act.wait_ge(d1, a + 1)
                    act.activation(wk[0][:, b, 0:L], wk[0][:, b, 0:L], ACT.Exp, scale=-1.0).then_inc(softplus_e, 1)
                    act.wait_ge(softplus_e, a + 1)
                    act.activation(wk[0][:, b, 0:L], wk[0][:, b, 0:L], ACT.Ln, bias=1.0).then_inc(softplus, 1)

                def exp_b(s):
                    t, h, b, n = item(i, s)
                    L = P * (t + 1)
                    act.wait_ge(d5, 8 * (i // 2) + s + 1)
                    if n >= 2:
                        act.wait_ge(pt_ready, n - 1)
                    act.activation(prob[:, b, 0:L], wk[1][:, b, 0:L], ACT.Exp).then_inc(p_written, 1)

                def keep_t(s):
                    t, h, b, n = item(i, s)
                    act.wait_ge(pt_ready, n + 1)
                    if s == 0 and i:
                        act.wait_ge(o_ready, i)
                    act.activation(prob_t[h][:, t * (t + 1) // 2:(t + 1) * (t + 2) // 2, :],
                                   t_bank[:, 0:P * (t + 1)].rearrange("p (k q) -> p k q", q=P),
                                   ACT.Copy).then_inc(pt_read, 1)

                for s in range(10):
                    if s < 8:
                        exp_a(s) if y == 0 else softplus_b(s)
                    if y == 1 and 1 <= s <= 8:
                        exp_b(s - 1)
                    if s >= 2:
                        keep_t(s - 2)
                    if s in (2, 5, 8):
                        read_half(3 * (i + 1) + s // 3)
                act.wait_ge(o_ready, i + 1)
                act.activation(m_hi[:, 3 * y + p, 0:SEQ], o_bank[:, :], ACT.Copy).then_inc(mhi_ready, 1)
            read_half(21)

            act.wait_ge(acc_act, IN_UNITS)
            act.wait_ge(acc_dve, IN_UNITS)
            act.activation(z_c[:, 2:4, :], z_c[:, 2:4, :], ACT.Gelu_apprx_tanh).then_inc(gelu_done, 1)
            act.activation(z_c[:, 0:2, :], z_c[:, 0:2, :], ACT.Gelu_apprx_tanh).then_inc(gelu_done, 1)
            act.wait_ge(vt_ready, 1)
            act.wait_ge(init, 10)
            for j in range(2):
                act.activation(vt[:, 2 * j:2 * j + 2, :], acc[:, j, :], ACT.Copy).then_inc(vt_read, 1)
            act.activation(vt[0:NS, QT, :], acc[0:NS, 2, 0:W_C], ACT.Copy).then_inc(vt_read, 1)
            act.wait_ge(v_chain, 3)
            act.activation(vsq[:, :, :], vt[:, :, :], ACT.Square).then_inc(v_sq, 1)
            act.wait_ge(v_chain, 4)
            act.activation(v_s[:, 2, :], v_s[:, 1, :], ACT.Sqrt, bias=eps[:, 0:1], scale=1.0 / HD).then_inc(v_sq, 1)
            act.wait_ge(v_chain, 8)
            act.dma_start(v_c_sample.rearrange("l b t c -> (l b t) c"), vt[0:NS, QT, :]).then_inc(out_s, 16)
            for y in range(2):
                for w in range(2):
                    act.dma_start(kv_sample[y][w], kv_new[y][:, w, :]).then_inc(out_s, 16)
            act.wait_ge(mix_dve, 8)
            act.activation(m_hi[:, 6:8, :], z_c[:, 0:2, :], ACT.Copy).then_inc(mix_hi, 1)

            for y in range(2):
                for grp in range(2):
                    gi = 2 * y + grp
                    for b4 in range(4):
                        n = 4 * gi + b4
                        act.wait_ge(kt_pe, n + 1)
                        if n >= 2:
                            act.wait_ge(sc_pe, n - 1)
                        act.activation(k_t[n % 2][:, :, 0:PAGE],
                                       s_bank[0][:, 0:W_ATT].rearrange("p (h k) -> p h k", k=PAGE),
                                       ACT.Copy).then_inc(kt_act, 1)
                    if y == 0:
                        act.wait_ge(e2, gi + 1)
                        if gi:
                            act.wait_ge(st_pe, gi)
                        act.activation(s_prob[:, :], sw[0][:, :], ACT.Exp, bias=s_st[:, 1:2],
                                       accum_out=s_st[:, 2:3]).then_inc(sp_written, 1)
                    else:
                        act.wait_ge(sc_pe, 4 * gi + 4)
                        act.wait_ge(ss_read, gi)
                        act.activation(sw[0][:, :], t_bank[:, 0:SK], ACT.Abs).then_inc(e1, 1)
                        act.wait_ge(e1, grp + 1)
                        act.activation(sw[0][:, :], sw[0][:, :], ACT.Exp, scale=-1.0).then_inc(softplus_e, 1)
                        act.wait_ge(softplus_e, 24 + grp + 1)
                        act.activation(sw[0][:, :], sw[0][:, :], ACT.Ln, bias=1.0).then_inc(softplus, 1)
                        act.wait_ge(e2, gi + 1)
                        act.wait_ge(st_pe, gi)
                        act.activation(s_prob[:, :], sw[1][:, :], ACT.Exp).then_inc(sp_written, 1)
                    act.wait_ge(st_pe, gi + 1)
                    if gi:
                        act.wait_ge(pv_pe, gi)
                    act.activation(s_pt[:, 0:2, :], o_bank[:, 0:2 * P], ACT.Copy).then_inc(st_act, 1)
                    act.activation(s_pt[0:NS, 2, :], o_bank[0:NS, 2 * P:3 * P], ACT.Copy).then_inc(st_act, 1)
                    act.wait_ge(ot_pe, gi + 1)
                    act.activation(m_hi[:, 3 * y:3 * y + 3, SEQ + 16 * grp:SEQ + 16 * (grp + 1)],
                                   o_bank[:, 0:48].rearrange("p (t c) -> p t c", c=16), ACT.Copy).then_inc(ot_hi, 1)

            for u in range(IN_UNITS + STAGE, FF0 + RING):
                hi_unit(u)

            act.wait_ge(out_s, 16 * 5)
            act.wait_ge(mean_pe, 1)
            for hf in range(2):
                act.activation(mean_b[:, HALF * hf:HALF * (hf + 1)], s_bank[hf][:, 0:HALF], ACT.Copy).then_inc(mean_sb, 1)
            for k in range(KT):
                act.wait_ge(cent, k + 1)
                if k >= 2:
                    act.wait_ge(sq_pe, k - 1)
                act.activation(sq[:, k % 2, :], res[:, k, :], ACT.Square).then_inc(sq_done, 1)
            act.wait_ge(sq_pe, KT)
            act.activation(sd_b[:, 0:HALF], t_bank[:, 0:HALF], ACT.Sqrt, bias=eps[:, 0:1]).then_inc(std_done, 1)
            act.activation(sd_b[:, HALF:T], o_bank[:, 0:HALF], ACT.Sqrt, bias=eps[:, 0:1]).then_inc(std_done, 1)
            for k in range(KT):
                act.wait_ge(nrm, k + 1)
                act.activation(res[:, k, :], res[:, k, :], ACT.Identity, bias=lnp[:, 3, k:k + 1],
                               scale=lnp[:, 2, k:k + 1]).then_inc(x1_done, 1)
                act.wait_ge(x1_done, k + 1)
                act.activation(h_hi[:, k, :], res[:, k, :], ACT.Copy).then_inc(h1_hi, 1)

            def segment(kind, par, prev, c):
                for j in range(FG):
                    if kind == "up":
                        act.wait_ge(half_done, (c["tile"] + j) * 2 + 1)
                        if not (isinstance(c["up"], int) and FG * c["up"] + j < 2):
                            act.wait_ge(sq_h, c["up"] * FG + (j - 1))
                        act.activation(relu[:, j % 2, 0:HALF], acc[:, 2 * (j % 2), 0:HALF],
                                       ACT.Relu).then_inc(acc_act, 1)
                    u = c["unit"] + j
                    if isinstance(u, int) and u + RING >= UNITS:
                        continue
                    used = 2 * (j + 1) if kind == "up" else 4 * (j + 1)
                    hi_part((FF0 + j) % RING, (FF0 + j) % STAGE, u + RING, c["tile"] * 2 + used,
                            c["unit"] * (16 // STAGE) + 16 * ((j + RING) // STAGE + 1))
            mlp(act, segment)

            for t in range(QT + 1):
                r = rows[t]
                act.wait_ge(y_c, 3 * (t + 1))
                act.activation(y_sd[0:r, t:t + 1], y_mv[0:r, t, 1:2], ACT.Sqrt, bias=eps[0:r, 0:1]).then_inc(y_std, 1)

        @block.vector
        def _(dve):
            dve.memset(x_mv[:, :, :], 1.0).then_inc(d0, 1)
            dve.wait_ge(d0, 1)
            for t in range(QT + 1):
                r = rows[t]
                dve.wait_ge(x_loaded[t], 16)
                for j in range(2):
                    dve.bn_stats(x_st[0:r, t, 6 * j:6 * j + 6],
                                 xin[0:r, t, 512 * j:512 * (j + 1)]).then_inc(x_stat, 1)
                dve.wait_ge(x_stat, 3 * t + 2)
                dve.bn_aggr(x_mv[0:r, t, :], x_st[0:r, t, :]).then_inc(x_stat, 1)
            dve.wait_ge(x_std, 1)
            dve.reciprocal(x_rs[:, :], x_sd[:, :]).then_inc(x_std, 1)
            dve.wait_ge(x_std, 2)
            for t in range(QT + 1):
                r = rows[t]
                dve.tensor_scalar(xin[0:r, t, :], xin[0:r, t, :], x_mv[0:r, t, 0:1], x_rs[0:r, t:t + 1],
                                  ALU.subtract, ALU.mult).then_inc(x_norm, 1)
            dve.wait_ge(const_loaded, 32)
            for k in range(KT):
                dve.wait_ge(xt_ready, k + 1)
                for dst, bank, n in ((slice(0, SEQ), 0, SEQ), (slice(SEQ, T), 1, NS)):
                    dve.tensor_scalar(res[:, k, dst], acc[:, 2 * (k % 2) + bank, 0:n], lnp[:, 0, k:k + 1],
                                      lnp[:, 1, k:k + 1], ALU.mult, ALU.add).then_inc(res_ready, 1)

            def read_half(u):
                i, j = divmod(u, 3)
                dve.wait_ge(half_done, 2 * u + 2)
                if u < 18:
                    if i >= 2 and j == 0:
                        dve.wait_ge(z_copied, i - 1)
                    dst = z[i % 2][:, j, HALF:T]
                else:
                    dst = z_c[:, u - 18, HALF:T]
                dve.tensor_scalar(dst, acc[:, 2 * (u % 2) + 1, 0:HALF], SCALE if (u < 18 and j == 0) else 1.0,
                                  None, ALU.mult).then_inc(acc_dve, 1)

            for u in range(3):
                read_half(u)
            dve.wait_ge(init, 9)
            for i in range(6):
                y, p = i % 2, i // 2
                dve.wait_ge(kv_t, 3 * i + 3)
                dve.tensor_copy(kv_new[y][:, :, P * p:P * (p + 1)],
                                s_bank[1][0:NS, 0:2 * P].rearrange("t (w c) -> t w c", w=2)).then_inc(s_read, 1)

                def scores_a(s):
                    t, h, b, n = s // 2, s % 2, s % 2, 8 * i + s
                    L = P * (t + 1)
                    dve.wait_ge(s_ready, n + 1)
                    if n >= 2:
                        dve.wait_ge(p_written, n - 1)
                    dve.tensor_tensor_reduce(wk[0][:, b, 0:L], s_bank[b][:, 0:L],
                                             strip[:, 2 * p + h, SEQ - L:SEQ], 1.0, -3e38,
                                             ALU.add, ALU.max, mx[:, b:b + 1]).then_inc(s_read, 1)
                    dve.wait_ge(s_read, 9 * i + 2 + s)
                    dve.tensor_scalar(nmx[:, b:b + 1], mx[:, b:b + 1], -1.0, None, ALU.mult).then_inc(st2, 1)

                def scale_a(s):
                    t, h, b, n = s // 2, s % 2, s % 2, 8 * i + s
                    L = P * (t + 1)
                    dve.wait_ge(p_written, n + 1)
                    dve.reciprocal(rinv[:, b:b + 1], rsum[:, b:b + 1]).then_inc(st3, 1)
                    dve.wait_ge(st3, 8 * (i // 2) + s + 1)
                    dve.tensor_scalar(prob[:, b, 0:L], prob[:, b, 0:L], rinv[:, b:b + 1], None,
                                      ALU.mult).then_inc(p_scaled, 1)

                def stick_b(s):
                    t, h, b, n = s // 2, s % 2, s % 2, 8 * i + s
                    L, a = P * (t + 1), 8 * (i // 2) + s + 1
                    diag = slice(L - P, L)
                    dve.wait_ge(softplus, a)
                    dve.wait_ge(p_written, n - 1)
                    dve.scalar_tensor_tensor(wk[1][:, b, 0:L], s_bank[b][:, 0:L], 0.0, wk[0][:, b, 0:L],
                                             ALU.max, ALU.add).then_inc(d2, 1)
                    dve.wait_ge(d2, a)
                    dve.tensor_tensor(wk[1][:, b, diag], wk[1][:, b, diag], c_("below"), ALU.mult).then_inc(d3, 1)
                    dve.wait_ge(d3, a)
                    back = wk[1][:, b, 0:L][:, ::-1]
                    dve.tensor_tensor_scan(wk[0][:, b, 0:L][:, ::-1], back, back, 0.0, ALU.add, ALU.max).then_inc(d4, 1)
                    dve.wait_ge(d4, a)
                    dve.tensor_tensor(wk[1][:, b, 0:L], s_bank[b][:, 0:L], wk[0][:, b, 0:L],
                                      ALU.subtract).then_inc(s_read, 1)
                    dve.wait_ge(s_read, 9 * i + 2 + s)
                    dve.tensor_tensor(wk[1][:, b, diag], wk[1][:, b, diag], c_("below_neg"), ALU.add).then_inc(d5, 1)

                for s in range(9):
                    if s < 8 and y == 0:
                        scores_a(s)
                    if s >= 1:
                        scale_a(s - 1) if y == 0 else stick_b(s - 1)
                    if s in (2, 5, 8):
                        read_half(3 * (i + 1) + s // 3)
                dve.wait_ge(mhi_ready, i + 1)
                dve.tensor_tensor(m_lo[:, 3 * y + p, 0:SEQ], o_bank[:, :], m_hi[:, 3 * y + p, 0:SEQ].bitcast(F32),
                                  ALU.subtract).then_inc(m_ready, 1)
            read_half(21)

            def bc(j):
                return v_s[:, j, :].rearrange("p (a o) -> p a o", o=1).to_broadcast([P, (QT + 1) * GROUPS, HD])
            vg = vt[:, :, :].rearrange("p t (g d) -> p (t g) d", d=HD)
            vall = vsq[:, :, :].rearrange("p t (g d) -> p (t g) d", d=HD)
            dve.wait_ge(vt_read, 3)
            dve.tensor_reduce(v_s[:, 0, :], vg, AX_X, ALU.add).then_inc(v_chain, 1)
            dve.wait_ge(v_chain, 1)
            dve.tensor_scalar(v_s[:, 1, :], v_s[:, 0, :], 1.0 / HD, None, ALU.mult).then_inc(v_chain, 1)
            dve.wait_ge(v_chain, 2)
            dve.tensor_tensor(vg, vg, bc(1), ALU.subtract).then_inc(v_chain, 1)
            dve.wait_ge(v_sq, 1)
            dve.tensor_reduce(v_s[:, 1, :], vall, AX_X, ALU.add).then_inc(v_chain, 1)
            dve.wait_ge(v_sq, 2)
            dve.reciprocal(v_s[:, 3, :], v_s[:, 2, :]).then_inc(v_chain, 1)
            dve.wait_ge(v_chain, 5)
            dve.tensor_tensor(vg, vg, bc(3), ALU.mult).then_inc(v_chain, 1)
            dve.wait_ge(g_loaded, 16 * (4 + GROUPS + NB))
            for j, op in enumerate((ALU.mult, ALU.add)):
                dve.wait_ge(v_chain, 6 + j)
                row = lnc[:, j, :].rearrange("p (o c) -> p o c", o=1).to_broadcast([P, QT + 1, W_C])
                dve.tensor_tensor(vt[:, :, :], vt[:, :, :], row, op).then_inc(v_chain, 1)
            tmp = vsq[:, :, :].rearrange("p t c -> p (t c)")
            done = 0
            for j in range(2):
                dve.wait_ge(mix_ready, j + 1)
                tj = tmp[:, SEQ * j:SEQ * (j + 1)].rearrange("p (c t) -> p c t", t=CHUNK)
                row = bsp[:, j, :].rearrange("p (o t) -> p o t", o=1).to_broadcast([P, QT, CHUNK])
                dve.tensor_tensor(tj, acc[:, j, :].rearrange("p (c t) -> p c t", t=CHUNK), row,
                                  ALU.add).then_inc(mix_dve, 1)
                dve.wait_ge(mix_dve, done + 1)
                dve.tensor_tensor(z_c[:, j, 0:SEQ], z_c[:, j, 0:SEQ], tmp[:, SEQ * j:SEQ * (j + 1)],
                                  ALU.mult).then_inc(mix_dve, 1)
                done += 2
            dve.wait_ge(mix_ready, 3)
            for j in range(2):
                at = 2 * SEQ + NS * j
                tj = tmp[:, at:at + NS].rearrange("p (b t) -> p b t", t=NQ)
                row = bsp[:, j, 0:NQ].rearrange("p (o t) -> p o t", o=1).to_broadcast([P, NB, NQ])
                dve.tensor_tensor(tj, acc[:, 2, NS * j:NS * (j + 1)].rearrange("p (b t) -> p b t", t=NQ), row,
                                  ALU.add).then_inc(mix_dve, 1)
                dve.wait_ge(mix_dve, done + 1)
                dve.tensor_tensor(z_c[:, j, SEQ:T], z_c[:, j, SEQ:T], tmp[:, at:at + NS],
                                  ALU.mult).then_inc(mix_dve, 1)
                done += 2
            dve.wait_ge(mix_hi, 1)
            dve.tensor_tensor(m_lo[:, 6:8, :], z_c[:, 0:2, :], m_hi[:, 6:8, :].bitcast(F32),
                              ALU.subtract).then_inc(mix_lo, 1)

            for y in range(2):
                for grp in range(2):
                    gi = 2 * y + grp
                    for b4 in range(4):
                        n = 4 * gi + b4
                        dve.wait_ge(kt_pe, n + 1)
                        if n >= 2:
                            dve.wait_ge(sc_pe, n - 1)
                        dve.tensor_copy(k_t[n % 2][:, :, PAGE:PAST],
                                        s_bank[1][:, 0:W_ATT].rearrange("p (h k) -> p h k", k=PAGE)).then_inc(kt_dve, 1)
                    dve.wait_ge(sc_pe, 4 * gi + 4)
                    if gi:
                        dve.wait_ge(sp_written, gi)
                    S = t_bank[:, 0:SK]
                    if y == 0:
                        dve.tensor_tensor_reduce(sw[0][:, :], S, c_("s_bias", P, SK * grp, SK * (grp + 1)), 1.0, -3e38, ALU.add, ALU.max,
                                                 s_st[:, 0:1]).then_inc(ss_read, 1)
                        dve.wait_ge(ss_read, gi + 1)
                        dve.tensor_scalar(s_st[:, 1:2], s_st[:, 0:1], -1.0, None, ALU.mult).then_inc(e2, 1)
                        dve.wait_ge(sp_written, gi + 1)
                        dve.reciprocal(s_st[:, 3:4], s_st[:, 2:3]).then_inc(e3, 1)
                    else:
                        dve.wait_ge(softplus, 24 + grp + 1)
                        dve.scalar_tensor_tensor(sw[1][:, :], S, 0.0, sw[0][:, :], ALU.max, ALU.add).then_inc(e4, 1)
                        dve.wait_ge(e4, 3 * grp + 1)
                        dve.tensor_tensor(sw[1][:, :], sw[1][:, :], c_("s_keep", P, SK * grp, SK * (grp + 1)), ALU.mult).then_inc(e4, 1)
                        dve.wait_ge(e4, 3 * grp + 2)
                        back = sw[1][:, ::-1]
                        dve.tensor_tensor_scan(sw[0][:, ::-1], back, back, 0.0, ALU.add, ALU.max).then_inc(e4, 1)
                        dve.wait_ge(e4, 3 * grp + 3)
                        dve.tensor_tensor(sw[1][:, :], S, sw[0][:, :], ALU.subtract).then_inc(ss_read, 1)
                        dve.wait_ge(ss_read, gi + 1)
                        dve.tensor_tensor(sw[1][:, :], sw[1][:, :], c_("s_neg", P, SK * grp, SK * (grp + 1)), ALU.add).then_inc(e2, 1)
                    dve.wait_ge(pv_pe, gi + 1)
                    if y == 0:
                        dve.wait_ge(e3, gi + 1)
                    if gi:
                        dve.wait_ge(ot_pe, gi)
                    dve.scalar_tensor_tensor(s_om[:, :], o_bank[:, 0:W_ATT], s_st[:, 3:4] if y == 0 else 1.0,
                                             c_("s_head"), ALU.mult, ALU.mult).then_inc(om_done, 1)
                    dve.wait_ge(ot_hi, gi + 1)
                    dst = slice(SEQ + 16 * grp, SEQ + 16 * (grp + 1))
                    dve.tensor_tensor(m_lo[:, 3 * y:3 * y + 3, dst], o_bank[:, 0:48].rearrange("p (t c) -> p t c", c=16),
                                      m_hi[:, 3 * y:3 * y + 3, dst].bitcast(F32), ALU.subtract).then_inc(ot_lo, 1)

            def halves(hf):
                return slice(HALF * hf, HALF * (hf + 1))
            for m in range(KT):
                u = IN_UNITS + m
                for hf in range(2):
                    dve.wait_ge(half_done, 2 * u + hf + 1)
                    dve.scalar_tensor_tensor(res[:, m, halves(hf)], res[:, m, halves(hf)], ALPHA,
                                             acc[:, 2 * (u % 2) + hf, 0:HALF], ALU.mult, ALU.add).then_inc(acc_dve, 1)
            dve.wait_ge(out_s, 16 * 5)
            dve.wait_ge(mean_sb, 2)
            for k in range(KT):
                dve.tensor_tensor(res[:, k, :], res[:, k, :], mean_b[:, :], ALU.subtract).then_inc(cent, 1)
            dve.wait_ge(std_done, 2)
            dve.reciprocal(rstd_b[:, :], sd_b[:, :]).then_inc(rstd_done, 1)
            dve.wait_ge(rstd_done, 1)
            for k in range(KT + 2):
                if k < KT:
                    dve.tensor_tensor(res[:, k, :], res[:, k, :], rstd_b[:, :], ALU.mult).then_inc(nrm, 1)
                if k >= 2:
                    dve.wait_ge(h1_hi, k - 1)
                    dve.tensor_tensor(h_lo[:, k - 2, :], res[:, k - 2, :], h_hi[:, k - 2, :].bitcast(F32),
                                      ALU.subtract).then_inc(h1_lo, 1)

            def segment(kind, par, prev, c):
                if kind == "up":
                    for j in range(UPS):
                        done = c["up"] * FG + (j + 1)
                        dve.wait_ge(half_done, (c["tile"] + j) * 2 + 2)
                        dve.tensor_scalar(relu[:, j % 2, HALF:T], acc[:, 2 * (j % 2) + 1, 0:HALF], 0.0, None,
                                          ALU.max).then_inc(acc_dve, 1)
                        dve.wait_ge(acc_act, c["act"] + (j + 1))
                        dve.wait_ge(acc_dve, c["dve"] + (j + 1))
                        dve.tensor_tensor(hid[:, j % 2, :], relu[:, j % 2, :], relu[:, j % 2, :], ALU.mult).then_inc(sq_h, 1)
                        dve.wait_ge(sq_h, done)
                        dve.tensor_copy(m_hi[:, FG * par + j, :], hid[:, j % 2, :]).then_inc(hid_hi, 1)
                        dve.wait_ge(hid_hi, done)
                        dve.tensor_tensor(m_lo[:, FG * par + j, :], hid[:, j % 2, :],
                                          m_hi[:, FG * par + j, :].bitcast(F32), ALU.subtract).then_inc(hid_lo, 1)
                else:
                    for m in range(DOWNS):
                        for hf in range(2):
                            dve.wait_ge(half_done, (c["tile"] + m) * 2 + (hf + 1))
                            if m == 0 and hf == 0:
                                dve.wait_ge(res_a, KT)
                            dve.tensor_tensor(res[:, m, halves(hf)], res[:, m, halves(hf)],
                                              acc[:, 2 * (m % 2) + hf, 0:HALF], ALU.add).then_inc(acc_dve, 1)
            mlp(dve, segment)

            for t in range(QT + 1):
                r = rows[t]
                banks = y_banks(t)
                dve.wait_ge(yt_pe, t + 1)
                for j in range(2):
                    dve.bn_stats(y_st[0:r, t, 6 * j:6 * j + 6], banks[j][0:r, :]).then_inc(y_c, 1)
                dve.wait_ge(y_c, 3 * t + 2)
                dve.bn_aggr(y_mv[0:r, t, :], y_st[0:r, t, :]).then_inc(y_c, 1)
                dve.wait_ge(y_std, t + 1)
                dve.reciprocal(y_rs[0:r, t:t + 1], y_sd[0:r, t:t + 1]).then_inc(y_rec, 1)
                dve.wait_ge(y_rec, t + 1)
                if t >= 2:
                    dve.wait_ge(y_out[t % 2], 16 * (t // 2))
                for j in range(2):
                    dve.tensor_scalar(y_n[0:r, t % 2, 512 * j:512 * (j + 1)], banks[j][0:r, :],
                                      y_mv[0:r, t, 0:1], y_rs[0:r, t:t + 1], ALU.subtract, ALU.mult).then_inc(yt_read, 1)
                dve.wait_ge(yt_read, 2 * (t + 1))
                if t == 0:
                    dve.wait_ge(ln2_loaded, 32)
                dve.tensor_tensor(y_n[0:r, t % 2, :], y_n[0:r, t % 2, :], ln2[0:r, 0, :], ALU.mult).then_inc(y_g, 1)

        @block.tensor
        def _(pe):
            pe.wait_ge(const_loaded, 32)
            for k in range(KT):
                if k >= 2:
                    pe.wait_ge(res_ready, 2 * (k - 1))
                for t in range(QT):
                    if k == 0:
                        pe.wait_ge(x_norm, t + 1)
                    pe.transpose(acc[:, 2 * (k % 2), P * t:P * (t + 1)], xin[:, t, P * k:P * (k + 1)], ident(P))
                if k == 0:
                    pe.wait_ge(x_norm, QT + 1)
                pe.transpose(acc[:, 2 * (k % 2) + 1, 0:NS], xin[0:NS, QT, P * k:P * (k + 1)],
                             ident(NS)).then_inc(xt_ready, 1)

            def halves(hf):
                return slice(HALF * hf, HALF * (hf + 1))

            def product(slot, cols, hi, lo, ks, out, chunk=None):
                work = [(hf, k, pas) for hf in range(2) for k in range(len(ks)) for pas in range(3)]
                part = work if chunk is None else work[len(work) // 3 * chunk:len(work) // 3 * (chunk + 1)]
                for hf, k, pas in part:
                    w = (w_hi, w_hi, w_lo)[pas]
                    x = (hi, lo, hi)[pas]
                    last = k == len(ks) - 1 and pas == 2
                    mm = pe.matmul(out[hf], w[:, slot, cols(k)], x[:, ks[k], halves(hf)],
                                   start=(k == 0 and pas == 0), stop=last)
                    if last:
                        mm.then_inc(half_done, 1)

            def cols(k):
                return slice(P * k, P * (k + 1))

            def unit(u, hi, lo, chunk=None):
                if chunk in (None, 0):
                    pe.wait_ge(lo_done, u + 1)
                    if u >= 2 and u != IN_UNITS and u != IN_UNITS + 1:
                        pe.wait_ge(acc_act, act_reads(u - 1))
                        pe.wait_ge(acc_dve, dve_reads(u - 1))
                b = 2 * (u % 2)
                product(u % RING, cols, hi, lo, range(KT), [acc[:, b + hf, 0:HALF] for hf in range(2)], chunk)

            pe.wait_ge(h_ready, KT)
            for u in range(3):
                unit(u, h_hi, h_lo)
            for i in range(6):
                y, p = i % 2, i // 2
                zq = z[y]
                pe.wait_ge(acc_act, 3 * i + 3)
                pe.wait_ge(acc_dve, 3 * i + 3)
                pe.wait_ge(pt_read, 8 * i) if i else None
                for t in range(QT):
                    mm = pe.transpose(t_bank[:, P * t:P * (t + 1)], zq[:, 1, P * t:P * (t + 1)], ident(P))
                mm.then_inc(kv_t, 1)
                pe.wait_ge(m_ready, i) if i else None
                for t in range(QT):
                    mm = pe.transpose(o_bank[:, P * t:P * (t + 1)], zq[:, 2, P * t:P * (t + 1)], ident(P))
                mm.then_inc(kv_t, 1)
                pe.wait_ge(s_read, 9 * i) if i else None
                for w in range(2):
                    mm = pe.transpose(s_bank[1][0:NS, P * w:P * (w + 1)], zq[:, 1 + w, SEQ:T], ident(P))
                mm.then_inc(kv_t, 1)
                for s in range(10):
                    if s < 8:
                        t, h = s // 2, s % 2
                        L = P * (t + 1)
                        if 9 * i + s - (s == 0) > 0:
                            pe.wait_ge(s_read, 9 * i + s - (s == 0))
                        r = slice(HD * h, HD * (h + 1))
                        pe.matmul(s_bank[s % 2][:, 0:L], zq[r, 0, P * t:P * (t + 1)], zq[r, 1, 0:L],
                                  start=True, stop=True).then_inc(s_ready, 1)
                    if s < 9:
                        unit(3 * (i + 1) + s // 3, h_hi, h_lo, s % 3)
                    if s >= 2:
                        n = 8 * i + s - 2
                        t, h, b = (s - 2) // 2, s % 2, s % 2
                        if y == 0:
                            pe.wait_ge(p_scaled, 8 * (i // 2) + s - 1)
                        else:
                            pe.wait_ge(p_written, n + 1)
                        if s == 2:
                            pe.wait_ge(kv_act, 2 * i + 1)
                        else:
                            pe.wait_ge(pt_read, n)
                        for kb in range(t + 1):
                            mm = pe.transpose(t_bank[:, P * kb:P * (kb + 1)], prob[:, b, P * kb:P * (kb + 1)], ident(P))
                        mm.then_inc(pt_ready, 1)
                pe.wait_ge(pt_read, 8 * i + 8)
                pe.wait_ge(kv_act, 2 * i + 2)
                for t in range(QT):
                    for kb in range(t + 1):
                        for h in range(2):
                            r = slice(HD * h, HD * (h + 1))
                            mm = pe.matmul(o_bank[r, P * t:P * (t + 1)], v_tok[y][:, kb, r],
                                           prob_t[h][:, t * (t + 1) // 2 + kb, :], start=(kb == 0), stop=(kb == t))
                mm.then_inc(o_ready, 1)
            unit(21, h_hi, h_lo)

            pe.wait_ge(gelu_done, 1)
            for t in range(QT + 1):
                for ct in range(2):
                    if t < QT:
                        out = acc[:, t // 2, W_C * (t % 2) + P * ct:W_C * (t % 2) + P * (ct + 1)]
                        src = z_c[:, 2 + ct, P * t:P * (t + 1)]
                    else:
                        out, src = acc[0:NS, 2, P * ct:P * (ct + 1)], z_c[:, 2 + ct, SEQ:T]
                    mm = pe.transpose(out, src, ident(P))
            mm.then_inc(vt_ready, 1)
            pe.wait_ge(v_chain, 8)
            pe.wait_ge(wsp_ready, 2 * GROUPS)
            for j in range(2):
                for ch in range(QT):
                    for g2 in range(2):
                        g = 2 * j + g2
                        mm = pe.matmul(acc[HD * g2:HD * (g2 + 1), j, CHUNK * ch:CHUNK * (ch + 1)],
                                       vt[:, ch, HD * g:HD * (g + 1)], wsp[:, g, :], start=True, stop=True)
                mm.then_inc(mix_ready, 1)
            for j in range(2):
                for g2 in range(2):
                    g = 2 * j + g2
                    mm = pe.matmul(acc[HD * g2:HD * (g2 + 1), 2, NS * j:NS * (j + 1)],
                                   vt[0:NS, QT, HD * g:HD * (g + 1)], wbd[:, g, :], start=True, stop=True)
            mm.then_inc(mix_ready, 1)

            def turn_pages(n):
                pe.wait_ge(kp_loaded[n % 2], 16 * PAGES * (n // 2 + 1))
                if n:
                    pe.wait_ge(kt_act, n)
                    pe.wait_ge(kt_dve, n)
                for pg in range(PAGES):
                    for p in range(PAIRS):
                        mm = pe.transpose(s_bank[pg][:, P * p:P * (p + 1)], k_pg[:, n % 2, pg, P * p:P * (p + 1)], ident(P))
                mm.then_inc(kt_pe, 1)

            pe.wait_ge(m_ready, 6)
            pe.wait_ge(z_copied, 6)
            turn_pages(0)
            for y in range(2):
                for grp in range(2):
                    gi = 2 * y + grp
                    for b4 in range(4):
                        n = 4 * gi + b4
                        if n + 1 < 2 * NB:
                            turn_pages(n + 1)
                        pe.wait_ge(kt_act, n + 1)
                        pe.wait_ge(kt_dve, n + 1)
                        pe.wait_ge(tail_done, 2 if y == 0 else 3 + n % 2)
                        if b4 == 0 and gi:
                            pe.wait_ge(ss_read, gi)
                        for p in range(PAIRS):
                            mm = pe.matmul(t_bank[32 * b4:32 * (b4 + 1), 0:SK], qbd[y][:, 4 * grp + b4, p, :],
                                           k_t[n % 2][:, p, :], start=(p == 0), stop=(p == PAIRS - 1),
                                           tile_position=(0, 32 * b4))
                        mm.then_inc(sc_pe, 1)
                    pe.wait_ge(sp_written, gi + 1)
                    if gi:
                        pe.wait_ge(ot_lo, gi)
                    pe.transpose(o_bank[:, 0:P], s_prob[:, 0:P], ident(P))
                    pe.transpose(o_bank[:, P:2 * P], s_prob[:, P:2 * P], ident(P))
                    pe.transpose(o_bank[0:NS, 2 * P:3 * P], s_prob[:, 2 * P:SK], ident(P)).then_inc(st_pe, 1)
                    pe.wait_ge(st_act, 2 * (gi + 1))
                    for b4 in range(4):
                        pe.wait_ge(vp_loaded[b4], 16 * PAGES * (gi + 1))
                        r = slice(32 * b4, 32 * (b4 + 1))
                        for pg in range(PAGES):
                            pe.matmul(o_bank[r, 0:W_ATT], s_pt[:, pg, r], v_pg[:, b4, pg, :], start=(pg == 0),
                                      stop=False, tile_position=(0, 32 * b4))
                        mm = pe.matmul(o_bank[r, 0:W_ATT], s_pt[0:NS, 2, r], kv_new[y][:, 1, :], start=False,
                                       stop=True, tile_position=(0, 32 * b4))
                    mm.then_inc(pv_pe, 1)
                    pe.wait_ge(om_done, gi + 1)
                    for p in range(PAIRS):
                        mm = pe.matmul(o_bank[:, 16 * p:16 * (p + 1)], s_om[:, P * p:P * (p + 1)], c_("s_pick"),
                                       start=True, stop=True)
                    mm.then_inc(ot_pe, 1)

            pe.wait_ge(ot_lo, 4)
            pe.wait_ge(mix_lo, 1)

            def mean_step(k):
                pe.wait_ge(acc_dve, dve_reads(IN_UNITS + k + 1))
                for hf in range(2):
                    mm = pe.matmul(s_bank[hf][:, 0:HALF], c_("mean"), res[:, k, halves(hf)],
                                   start=(k == 0), stop=(k == KT - 1))
                if k == KT - 1:
                    mm.then_inc(mean_pe, 1)
            for m in range(KT):
                unit(IN_UNITS + m, m_hi, m_lo)
                if m:
                    mean_step(m - 1)
            mean_step(KT - 1)
            for k in range(KT):
                pe.wait_ge(sq_done, k + 1)
                for hf, bank in enumerate((t_bank, o_bank)):
                    mm = pe.matmul(bank[:, 0:HALF], c_("mean"), sq[:, k % 2, halves(hf)],
                                   start=(k == 0), stop=(k == KT - 1))
                mm.then_inc(sq_pe, 1)

            pe.wait_ge(h1_lo, KT)

            def segment(kind, par, prev, c):
                first = (0, 2) if prev == "down" else (1, 1)
                if kind == "up":
                    for j in range(UPS):
                        pe.wait_ge(lo_done, c["unit"] + (j + 1))
                        a, d = (j - 1, j - 1) if j else (-first[0], -first[1])
                        pe.wait_ge(acc_act, c["act"] + a)
                        pe.wait_ge(acc_dve, c["dve"] + d)
                        b = 2 * (j % 2)
                        product((FF0 + j) % RING, cols, h_hi, h_lo, range(KT),
                                [acc[:, b + hf, 0:HALF] for hf in range(2)])
                else:
                    pe.wait_ge(hid_lo, (c["down"] + 1) * FG)
                    for j in range(FG):
                        pe.wait_ge(lo_done, c["unit"] + (j + 1))
                        for mj in range(2):
                            m = 2 * j + mj
                            a, d = (0, 2 * (m - 1)) if m else (-first[0], -first[1])
                            pe.wait_ge(acc_act, c["act"] + a)
                            pe.wait_ge(acc_dve, c["dve"] + d)
                            b = 2 * (m % 2)
                            product((FF0 + j) % RING, lambda f: slice(2 * P * f + P * mj, 2 * P * f + P * (mj + 1)),
                                    m_hi, m_lo, [FG * par + f for f in range(FG)],
                                    [acc[:, b + hf, 0:HALF] for hf in range(2)])
            mlp(pe, segment)

            pe.wait_ge(acc_dve, DVE0 + NG * (UPS + 2 * DOWNS))
            for t in range(QT + 1):
                r = rows[t]
                banks = y_banks(t)
                if t == QT:
                    pe.wait_ge(yt_read, 2)
                for m in range(KT):
                    mm = pe.transpose(banks[m // 4][0:r, P * (m % 4):P * (m % 4 + 1)], res[:, m, P * t:P * t + r], ident(P))
                mm.then_inc(yt_pe, 1)


def constants():
    c = np.zeros((P, CONSTS), np.float32)
    s = np.zeros((P, S_CONSTS), np.float32)

    def put(name, a):
        to, where = (c, CONST) if name in CONST else (s, S_CONST)
        at, n = where[name]
        to[:a.shape[0], at:at + n] = a
    i = np.arange(P)[:, None]
    put("ident", np.eye(P))
    j = np.arange(SEQ)[None, :] - (SEQ - P)
    put("dist", np.where(j <= i, j - i, NEG))
    j = np.arange(P)[None, :]
    put("below", j < i)
    put("below_neg", np.where(j < i, 0.0, NEG))
    put("upto", i <= j)
    b, hq = i // 32, i % 32
    h, q = hq // NQ, hq % NQ
    slope = np.array(SLOPES + [0.0, 0.0])[h]
    key = np.arange(SK)[None, :]
    new = key - PAST
    rel = new % NQ - q
    for grp in range(2):
        at = np.arange(grp * SK, (grp + 1) * SK)
        own = (new >= 0) & (new // NQ == 4 * grp + b)
        for name, a in (("s_bias", np.where(key < PAST, slope * (new - q), np.where(own & (rel <= 0), slope * rel, NEG))),
                        ("s_keep", (key < PAST) | (own & (rel < 0))),
                        ("s_neg", np.where((key < PAST) | (own & (rel < 0)), 0.0, NEG))):
            s[:, S_CONST[name][0] + at] = a
    put("mean", np.full((P, P), 1.0 / D_MODEL))
    put("s_head", (np.arange(W_ATT)[None, :] // HD == h))
    bb = np.arange(16)[None, :]
    put("s_pick", (bb // NQ == b) & (bb % NQ == q) & (h < H))
    a, d = np.arange(NS)[:, None], np.arange(NS)[None, :]
    put("s_chunk", (a // NQ == d // NQ) & (a % NQ <= d % NQ))
    return c, s


def split_units(w_in, w_out, w_ff1, w_ff2):
    def columns(w, at, n=P):
        return w[:, at:at + n].reshape(-1, P, n).transpose(1, 0, 2).reshape(P, -1)
    units = []
    for p in range(PAIRS):
        for y in range(2):
            units += [columns(w_in, (3 * y + s) * W_ATT + P * p) for s in range(3)]
    units += [columns(w_in, 6 * W_ATT + P * j) for j in range(4)]
    units += [columns(w_out, P * m) for m in range(OUT_UNITS)]

    def up(g):
        return [columns(w_ff1, P * (FG * g + j)) for j in range(FG)]

    def down(g):
        rows = w_ff2[P * FG * g:P * FG * (g + 1)]
        return [columns(rows, 2 * P * j, 2 * P) for j in range(FG)]
    units += up(0)
    for g in range(1, NG):
        units += up(g) + down(g - 1)
    return np.stack(units + down(NG - 1))


_OUTS = [("y_prompt", (1, SEQ, D_MODEL)), ("y_sample", (NB, NQ, D_MODEL)),
         ("k_a_prompt", (1, 1, SEQ, H, HD)), ("v_a_prompt", (1, 1, SEQ, H, HD)),
         ("k_b_prompt", (1, 1, SEQ, H, HD)), ("v_b_prompt", (1, 1, SEQ, H, HD)),
         ("k_a_sample", (1, NB, NQ, H, HD)), ("v_a_sample", (1, NB, NQ, H, HD)),
         ("k_b_sample", (1, NB, NQ, H, HD)), ("v_b_sample", (1, NB, NQ, H, HD)),
         ("v_c_sample", (1, NB, NQ, W_C))]


def kernel(x_prompt, x_sample, cache_k_a, cache_v_a, cache_k_b, cache_v_b, page_table, ln_in_g,
           ln_in_b, w_in, w_out, w_spatial, b_spatial, ln_c_g, ln_c_b, ln1_g, ln1_b, w_ff1, w_ff2,
           ln2_g, ln2_b):
    import concourse.bacc as bacc
    from concourse.bass_utils import run_bass_kernel_spmd

    a = {k: np.asarray(v) for k, v in locals().items()
         if k not in ("bacc", "run_bass_kernel_spmd")}
    arrays = {
        "x_prompt": a["x_prompt"], "x_sample": a["x_sample"],
        "weights": split_units(a["w_in"][0], a["w_out"][0], a["w_ff1"][0], a["w_ff2"][0]),
        "cache_k_a": a["cache_k_a"], "cache_v_a": a["cache_v_a"],
        "cache_k_b": a["cache_k_b"], "cache_v_b": a["cache_v_b"],
        "page_table": a["page_table"],
        "ln_cols": np.stack([v.reshape(KT, P).T for v in
                             (a["ln_in_g"], a["ln_in_b"], a["ln1_g"][0], a["ln1_b"][0])], axis=1),
        "w_spatial": a["w_spatial"][0].transpose(2, 0, 1),
        "b_spatial": a["b_spatial"][0],
        "lnc_g": a["ln_c_g"].reshape(1, W_C), "lnc_b": a["ln_c_b"].reshape(1, W_C),
        "ln2_g": a["ln2_g"].reshape(1, D_MODEL), "ln2_b": a["ln2_b"].reshape(1, D_MODEL),
        "consts": constants()[0], "s_consts": constants()[1],
    }
    nc = bacc.Bacc("TRN2", target_bir_lowering=False, num_devices=1)
    args = []
    for name, v in arrays.items():
        arrays[name] = v = np.ascontiguousarray(v)
        args.append(nc.dram_tensor(name, v.shape, mybir.dt.from_np(v.dtype), kind="ExternalInput").ap())
    for name, shape in _OUTS:
        args.append(nc.dram_tensor(name, shape, F32, kind="ExternalOutput").ap())
    hybrid_layer(nc, *args)
    r = run_bass_kernel_spmd(nc, [arrays], core_ids=[0]).results[0]
    return tuple(r[name] for name, _ in _OUTS)
```

```python
from contextlib import ExitStack

import numpy as np

import concourse.bass as bass
from concourse import mybir

ALU = mybir.AluOpType
ACT = mybir.ActivationFunctionType
AX_X = mybir.AxisListType.X
F32 = mybir.dt.float32
F32R = mybir.dt.float32r
I32 = mybir.dt.int32

P = 128
D_MODEL = 1024
KT = D_MODEL // P
SEQ = 512
NB = 8
NQ = 4
NS = NB * NQ
T = SEQ + NS
HALF = T // 2
QT = SEQ // P
HD = 64
H = 6
PAIRS = H // 2
W_ATT = H * HD
GROUPS = 4
W_C = GROUPS * HD
PAST = 256
PAGE = 128
PAGES = PAST // PAGE
CHUNK = 128
D_FF = 4 * D_MODEL
SCALE = HD ** -0.5
ALPHA = 2 ** 0.25
EPS = 1e-5
MOBA_BLOCK = 256
MOBA_TOPK = 3
assert max(SEQ, PAST + NQ) <= 2 * MOBA_BLOCK and MOBA_TOPK >= 2
SLOPES = [0.25, 0.0625, 0.015625, 0.00390625, 0.5, 0.125]
NEG = -1e30
SK = PAST + NS

IN_UNITS = 22
OUT_UNITS = D_MODEL // P
FG = 4
NG = D_FF // (P * FG)
FF_UNITS = 2 * NG * FG
UNITS = IN_UNITS + OUT_UNITS + FF_UNITS
STAGE = 2
RING = 4
ITEMS = 2 * PAIRS * QT * 2
C_TILE = (2, 3, 0, 1)

def _pack(*sizes):
    at, out = 0, {}
    for name, cols in sizes:
        out[name] = (at, cols)
        at += cols
    return out, at


CONST, CONSTS = _pack(("ident", P), ("dist", SEQ), ("below_neg", P), ("upto", P), ("mean", P))
S_CONST, S_CONSTS = _pack(("s_bias", 2 * SK), ("s_neg", 2 * SK), ("s_head", W_ATT),
                          ("s_pick", 16), ("s_chunk", NS))


def hybrid_layer(nc, x_prompt, x_sample, weights, cache_k_a, cache_v_a, cache_k_b, cache_v_b,
                 page_table, ln_cols, w_spatial, b_spatial, lnc_g, lnc_b, ln2_g, ln2_b, consts, s_consts,
                 y_prompt, y_sample, k_a_prompt, v_a_prompt, k_b_prompt, v_b_prompt,
                 k_a_sample, v_a_sample, k_b_sample, v_b_sample, v_c_sample):
    n_pool = cache_k_a.shape[1]
    caches = [[c.rearrange("l n p h d -> (l n) p (h d)") for c in kv]
              for kv in ((cache_k_a, cache_v_a), (cache_k_b, cache_v_b))]
    x_rows = [x_prompt[0, t * P:(t + 1) * P, :] for t in range(QT)]
    x_rows.append(x_sample.rearrange("b t d -> (b t) d"))
    kv_prompt = [[o.rearrange("l b (t p) h d -> p (l b t) (h d)", p=P) for o in kv]
                 for kv in ((k_a_prompt, v_a_prompt), (k_b_prompt, v_b_prompt))]
    kv_sample = [[o.rearrange("l b t h d -> (l b t) (h d)") for o in kv]
                 for kv in ((k_a_sample, v_a_sample), (k_b_sample, v_b_sample))]
    rows = [P] * QT + [NS]

    with ExitStack() as ctx:
        def sb(name, shape, dt=F32, to=None):
            return (to or ctx).enter_context(nc.sbuf_tensor(name, shape, dt))

        def sem(name):
            return ctx.enter_context(nc.semaphore(name))

        cst = sb("cst", [P, CONSTS])
        h_hi = sb("h_hi", [P, KT, T], F32R)
        h_lo = sb("h_lo", [P, KT, T], F32R)
        m_hi = sb("m_hi", [P, KT, T], F32R)
        m_lo = sb("m_lo", [P, KT, T], F32R)
        w_raw = sb("w_raw", [P, STAGE, KT * P])
        w_hi = sb("w_hi", [P, RING, KT * P], F32R)
        w_lo = sb("w_lo", [P, RING, KT * P], F32R)
        lnp = sb("lnp", [P, 4, KT])
        eps = sb("eps", [P, 1])
        qbd = [sb(f"qbd{y}", [P, NB, PAIRS, 32]) for y in range(2)]
        dist_r = sb("dist_r", [P, SEQ], F32R)
        sid_r = sb("sid_r", [P, H, P], F32R)
        id_r = sb("id_r", [P, P], F32R)
        below_r = sb("below_r", [P, P], F32R)

        early = ExitStack()
        s_cst = sb("s_cst", [P, S_CONSTS], to=early)
        sb_r = sb("sb_r", [P, 4, SK], F32R, to=early)
        k_pg = sb("k_pg", [P, 2, PAGES, W_ATT], to=early)
        ptab = sb("ptab", [1, NB * PAGES], I32, to=early)
        early.close()
        res = sb("res", [P, KT, T])

        ph = ExitStack()
        xin = sb("xin", [P, QT + 1, D_MODEL], to=ph)
        x_n = sb("x_n", [P, KT, T], to=ph)
        x_st = sb("x_st", [P, QT + 1, 12], to=ph)
        x_mv = sb("x_mv", [P, QT + 1, 2], to=ph)
        x_sd = sb("x_sd", [P, QT + 1], to=ph)
        x_rs = sb("x_rs", [P, QT + 1], to=ph)
        ph.close()

        after_x = ExitStack()
        z_c = sb("z_c", [P, 4, T], to=after_x)
        k_new = [sb(f"k_new{y}", [P, PAIRS, NS], to=after_x) for y in range(2)]
        kv_new = [sb(f"kv_new{y}", [NS, 2, W_ATT], to=after_x) for y in range(2)]

        pr = ExitStack()
        k_tok = [sb(f"k_tok{j}", [P, QT, P], to=pr) for j in range(2)]
        v_tok = [sb(f"v_tok{j}", [P, QT, P], to=pr) for j in range(2)]
        keep = sb("keep", [P, 2, SEQ], to=pr)
        left = sb("left", [P, 2, SEQ], to=pr)
        prob = sb("prob", [P, 3, SEQ], to=pr)
        prob_t = [sb(f"prob_t{h}", [P, QT * (QT + 1) // 2, P], to=pr) for h in range(2)]
        mx = sb("mx", [P, 2], to=pr)
        nmx = sb("nmx", [P, 2], to=pr)
        rsum = sb("rsum", [P, 2], to=pr)
        rinv = sb("rinv", [P, 2], to=pr)
        z_q = [sb(f"z_q{j}", [P, 2, T], to=pr) for j in range(2)]
        z_kv = [sb(f"z_kv{j}", [P, 2, T], to=pr) for j in range(2)]
        pr.close()

        sa = ExitStack()
        vt = sb("vt", [P, QT + 1, W_C], to=sa)
        vsq = sb("vsq", [P, QT + 1, W_C], to=sa)
        v_s = sb("v_s", [P, 4, (QT + 1) * GROUPS], to=sa)
        lnc = sb("lnc", [P, 2, W_C], to=sa)
        wsp = sb("wsp", [P, GROUPS, CHUNK], to=sa)
        wbd = sb("wbd", [NS, GROUPS, NS], to=sa)
        bsp = sb("bsp", [P, 2, CHUNK], to=sa)
        v_pg = sb("v_pg", [P, 4, PAGES, W_ATT], to=sa)
        k_t = sb("k_t", [P, 4, PAIRS, PAST], to=sa)
        sw = [sb(f"sw{j}", [P, SK], to=sa) for j in range(2)]
        s_prob = sb("s_prob", [P, SK], to=sa)
        s_pt = sb("s_pt", [P, 3, P], to=sa)
        s_om = sb("s_om", [P, W_ATT], to=sa)
        s_st = sb("s_st", [P, 4], to=sa)
        sa.close()
        after_x.close()

        ff = ExitStack()
        mean_b = sb("mean_b", [P, T], to=ff)
        sd_b = sb("sd_b", [P, T], to=ff)
        rstd_b = sb("rstd_b", [P, T], to=ff)
        sq = sb("sq", [P, 2, T], to=ff)
        relu = sb("relu", [P, 2, T], to=ff)
        hid = sb("hid", [P, 2, T], to=ff)
        ln2 = sb("ln2", [P, 2, D_MODEL], to=ff)
        y_n = sb("y_n", [P, 2, D_MODEL], to=ff)
        y_st = sb("y_st", [P, QT + 1, 12], to=ff)
        y_mv = sb("y_mv", [P, QT + 1, 2], to=ff)
        y_sd = sb("y_sd", [P, QT + 1], to=ff)
        y_rs = sb("y_rs", [P, QT + 1], to=ff)
        ff.close()

        acc = ctx.enter_context(nc.psum_tensor("acc", [P, 4, 512], F32))
        s_bank = [ctx.enter_context(nc.psum_tensor(f"s_bank{j}", [P, 512], F32)) for j in range(2)]
        t_bank = ctx.enter_context(nc.psum_tensor("t_bank", [P, 512], F32))
        o_bank = ctx.enter_context(nc.psum_tensor("o_bank", [P, 512], F32))

        def c_(name, r=P, lo=0, hi=None):
            where, t = (CONST, cst) if name in CONST else (S_CONST, s_cst)
            at, n = where[name]
            return t[0:r, at + lo:at + (n if hi is None else hi)]

        def ident(r):
            return c_("ident", r, 0, r)

        x_loaded = [sem(f"x_loaded{t}") for t in range(QT + 1)]
        const_loaded = sem("const_loaded")
        const2_loaded, s_const_loaded = sem("const2_loaded"), sem("s_const_loaded")
        bias_ready, sb_ready = sem("bias_ready"), sem("sb_ready")
        vt_zero, wbd_zero, max_ready, s_scaled, stream = (sem(n) for n in ("vt_zero", "wbd_zero", "max_ready", "s_scaled", "stream"))
        w_loaded = [sem(f"w_loaded{j}") for j in range(STAGE)]
        hi_done, lo_done = sem("hi_done"), sem("lo_done")
        half_done = sem("half_done")
        acc_act, acc_dve = sem("acc_act"), sem("acc_dve")
        x_stat, x_std, x_norm = sem("x_stat"), sem("x_std"), sem("x_norm")
        xt_ready, res_ready, hhi_ready, h_ready = sem("xt_ready"), sem("res_ready"), sem("hhi_ready"), sem("h_ready")
        init = sem("init")
        z_copied, q_copied = sem("z_copied"), sem("q_copied")
        kv_t, kv_act, kv_dve = sem("kv_t"), sem("kv_act"), sem("kv_dve")
        kv_out = [sem(f"kv_out{y}") for y in range(2)]
        s_ready, s_read = sem("s_ready"), sem("s_read")
        st1, st2, st3, st4 = sem("st1"), sem("st2"), sem("st3"), sem("st4")
        softplus_e, softplus = sem("softplus_e"), sem("softplus")
        d1, d2, d3, d4, d5 = sem("d1"), sem("d2"), sem("d3"), sem("d4"), sem("d5")
        p_written, p_scaled, p_sum = sem("p_written"), sem("p_scaled"), sem("p_sum")
        pt_ready, pt_read = sem("pt_ready"), sem("pt_read")
        o_ready, mhi_ready, m_ready = sem("o_ready"), sem("mhi_ready"), sem("m_ready")
        gelu_done, vt_ready, vt_read, v_chain, v_sq = sem("gelu_done"), sem("vt_ready"), sem("vt_read"), sem("v_chain"), sem("v_sq")
        mix_ready, mix_dve, mix_hi, mix_lo = sem("mix_ready"), sem("mix_dve"), sem("mix_hi"), sem("mix_lo")
        wsp_ready, g_loaded = sem("wsp_ready"), sem("g_loaded")
        pt_loaded = sem("pt_loaded")
        kp_loaded = [sem(f"kp_loaded{j}") for j in range(2)]
        vp_loaded = [sem(f"vp_loaded{j}") for j in range(4)]
        kt_pe, kt_act, kt_dve, sc_pe = sem("kt_pe"), sem("kt_act"), sem("kt_dve"), sem("sc_pe")
        tail_done = sem("tail_done")
        ss_read, e1, e2, e3, sp_written = sem("ss_read"), sem("e1"), sem("e2"), sem("e3"), sem("sp_written")
        st_pe, st_act, pv_pe, om_done, ot_pe, ot_hi, ot_lo = (sem(n) for n in ("st_pe", "st_act", "pv_pe", "om_done", "ot_pe", "ot_hi", "ot_lo"))
        r_ready, mean_pe, mean_sb, cent, sq_done, sq_pe, std_done, rstd_done = (sem(n) for n in ("r_ready", "mean_pe", "mean_sb", "cent", "sq_done", "sq_pe", "std_done", "rstd_done"))
        nrm, x1_done, h1_hi, h1_lo, res_a = (sem(n) for n in ("nrm", "x1_done", "h1_hi", "h1_lo", "res_a"))
        relu_act, relu_dve, sq_h, hid_hi, hid_lo = (sem(n) for n in ("relu_act", "relu_dve", "sq_h", "hid_hi", "hid_lo"))
        yt_pe, yt_read, y_c, y_std, y_nrm, y_g, y_b, ln2_loaded = (sem(n) for n in ("yt_pe", "yt_read", "y_c", "y_std", "y_nrm", "y_g", "y_b", "ln2_loaded"))
        y_out = [sem(f"y_out{j}") for j in range(2)]
        out_s = sem("out_s")
        d0, e4, y_rec = sem("d0"), sem("e4"), sem("y_rec")

        def x_rows_sb(t):
            return xin[0:rows[t], t, :]

        def item(n):
            i, s = divmod(n, 8)
            return i, s, s // 2, s % 2, P * (s // 2 + 1)

        def pt_bank(n):
            return t_bank[:, :] if n % 2 == 0 else acc[:, 2, :]

        def page_bank(q):
            return (s_bank[0][:, :], s_bank[1][:, :], acc[:, 3, :])[q % 3]

        def y_banks(t):
            return ((acc[:, 0, :], acc[:, 1, :]), (acc[:, 2, :], acc[:, 3, :]),
                    (s_bank[0][:, :], s_bank[1][:, :]), (t_bank[:, :], o_bank[:, :]))[t % 4]

        block = ctx.enter_context(nc.Block())

        MLP_HEAD = [("up", 0), ("up", 1), ("down", 0)]
        MLP_BODY = [("up", 2), ("down", 1), ("up", 3), ("down", 2)]
        MLP_ROUNDS = (NG - 2) // 2
        MLP_TAIL = [("down", NG - 1)]
        UPS, DOWNS = FG, KT
        FF0 = IN_UNITS + OUT_UNITS

        def act_reads(n):
            return min(n, IN_UNITS)

        def dve_reads(n):
            return min(n, IN_UNITS) + 2 * max(0, n - IN_UNITS)

        ACT0, DVE0 = act_reads(FF0), dve_reads(FF0)

        def mlp(eng, segment):
            up = {"unit": FG, "tile": UPS, "act": UPS, "dve": UPS, "up": 1, "down": 0}
            down = {"unit": FG, "tile": DOWNS, "act": 0, "dve": 2 * DOWNS, "up": 0, "down": 1}
            before = ["down"]

            def run(c, segments):
                for kind, g in segments:
                    segment(kind, g % 2, before[0], c)
                    before[0] = kind
                    c = {k: c[k] + (up if kind == "up" else down)[k] for k in c}
                return c

            c = run({"unit": FF0, "tile": FF0, "act": ACT0, "dve": DVE0, "up": 0, "down": 0}, MLP_HEAD)
            with eng.Fori(0, MLP_ROUNDS) as i:
                run({k: i * (2 * up[k] + 2 * down[k]) + c[k] for k in c}, MLP_BODY)
            run({k: c[k] + MLP_ROUNDS * (2 * up[k] + 2 * down[k]) for k in c}, MLP_TAIL)

        @block.sync
        def _(sp):
            at, n = CONST["ident"]
            sp.dma_start(x_rows_sb(0), x_rows[0]).then_inc(x_loaded[0], 16)
            sp.dma_start(cst[:, at:at + n], consts[:, at:at + n]).then_inc(const_loaded, 16)
            sp.dma_start(lnp[:, :, :], ln_cols).then_inc(const_loaded, 16)
            for t in range(1, QT + 1):
                sp.dma_start(x_rows_sb(t), x_rows[t]).then_inc(x_loaded[t], 16)

            def load_unit(u, slot, count):
                if count is not None:
                    sp.wait_ge(lo_done, count)
                sp.dma_start(w_raw[:, slot, :], weights[u]).then_inc(w_loaded[slot], 16)

            def load_first(u):
                load_unit(u, u % STAGE, u - STAGE + 1 if u >= STAGE else None)

            def load_keys(n):
                y, b = divmod(n, NB)
                for pg in range(PAGES):
                    sp.dma_start(k_pg[:, n % 2, pg, :], caches[y][0][pages[PAGES * b + pg]]).then_inc(kp_loaded[n % 2], 16)

            for u in range(STAGE):
                load_first(u)
            sp.dma_start(cst[:, at + n:CONSTS], consts[:, at + n:CONSTS]).then_inc(const2_loaded, 16)
            sp.dma_start(ptab[:, :], page_table.rearrange("(a b) p -> a (b p)", a=1)).then_inc(pt_loaded, 16)
            for u in range(STAGE, 8):
                load_first(u)
            sp.dma_start(s_cst[:, :], s_consts).then_inc(s_const_loaded, 16)
            sp.wait_ge(pt_loaded, 16)
            pages = [sp.value_load(ptab[0:1, n:n + 1], min_val=0, max_val=n_pool - 1)
                     for n in range(NB * PAGES)]
            for n in range(2):
                load_keys(n)
            for u in range(8, IN_UNITS + RING):
                load_first(u)

            sp.wait_ge(m_ready, 6)
            sp.wait_ge(kv_out[0], 16 * 6)
            sp.wait_ge(kv_out[1], 16 * 6)
            for j, row in enumerate((lnc_g, lnc_b)):
                sp.dma_start(lnc[:, j, :], row.to_broadcast([P, W_C])).then_inc(g_loaded, 16)
            sp.dma_start(wsp[:, :, :], w_spatial).then_inc(g_loaded, 16)
            for g in range(GROUPS):
                j, g2 = divmod(g, 2)
                sp.dma_start(bsp[HD * g2:HD * (g2 + 1), j, :],
                             b_spatial[g:g + 1, :].to_broadcast([HD, CHUNK])).then_inc(g_loaded, 16)
            sp.wait_ge(wbd_zero, 1)
            for b in range(NB):
                sp.dma_start(wbd[NQ * b:NQ * (b + 1), :, NQ * b:NQ * (b + 1)],
                             w_spatial[0:NQ, :, 0:NQ]).then_inc(g_loaded, 16)
            for gi in range(4):
                y, grp = divmod(gi, 2)
                for n in range(max(2, 4 * gi), 4 * gi + 4):
                    sp.wait_ge(kt_pe, 2 * (n - 1))
                    load_keys(n)
                if gi:
                    sp.wait_ge(pv_pe, gi)
                for b4 in range(4):
                    for pg in range(PAGES):
                        src = caches[y][1][pages[PAGES * (4 * grp + b4) + pg]]
                        sp.dma_start(v_pg[:, b4, pg, :], src).then_inc(vp_loaded[b4], 16)
            for u in range(IN_UNITS + RING, FF0):
                load_first(u)

            def segment(kind, par, prev, c):
                for j in range(FG):
                    load_unit(c["unit"] + j, (FF0 + j) % STAGE, c["unit"] + (j - STAGE + 1))
            mlp(sp, segment)
            sp.wait_ge(res_a, KT)
            for j, row in enumerate((ln2_g, ln2_b)):
                sp.dma_start(ln2[:, j, :], row.to_broadcast([P, D_MODEL])).then_inc(ln2_loaded, 16)
            for t in range(QT + 1):
                sp.wait_ge(y_b, t + 1)
                dst = y_prompt[0, P * t:P * (t + 1), :] if t < QT else y_sample.rearrange("b t d -> (b t) d")
                sp.dma_start(dst, y_n[0:rows[t], t % 2, :]).then_inc(y_out[t % 2], 16)
            for t in range(2):
                sp.wait_ge(y_out[t], 16 * ((QT + 2 - t) // 2))
                sp.wait_ge(kv_out[t], 16 * 6)
            sp.wait_ge(out_s, 16 * 5)

        @block.gpsimd
        def _(pool):
            def lo_part(slot, stage, u):
                pool.wait_ge(hi_done, u + 1)
                pool.tensor_tensor(w_lo[:, slot, :], w_raw[:, stage, :],
                                   w_hi[:, slot, :].bitcast(F32), ALU.subtract).then_inc(lo_done, 1)

            pool.memset(eps[:, :], EPS).then_inc(init, 1)
            for j in range(2):
                pool.memset(z_q[j][:, :, :], 0.0).then_inc(init, 1)
            for y in range(2):
                pool.memset(qbd[y][:, :, :, :], 0.0).then_inc(init, 1)
            for u in range(2):
                lo_part(u, u % STAGE, u)
            for k in range(0, KT, 2):
                pool.wait_ge(hhi_ready, k + 1)
                pool.tensor_tensor(h_lo[:, k, :], x_n[:, k, :], h_hi[:, k, :].bitcast(F32),
                                   ALU.subtract).then_inc(h_ready, 1)
            lo_part(2, 2 % STAGE, 2)
            pool.wait_ge(const2_loaded, 16)
            pool.tensor_copy(dist_r[:, :], c_("dist")).then_inc(bias_ready, 1)
            for h in range(H):
                pool.tensor_scalar(sid_r[:, h, :], c_("ident"), SLOPES[h], None, ALU.mult).then_inc(bias_ready, 1)
            lo_part(3, 3 % STAGE, 3)
            pool.tensor_copy(id_r[:, :], c_("ident")).then_inc(bias_ready, 1)
            pool.tensor_copy(below_r[:, :], c_("below_neg")).then_inc(bias_ready, 1)

            def keep_samples(i):
                y, p = divmod(i, PAIRS)
                pool.wait_ge(acc_act, 3 * i + 3)
                pool.wait_ge(acc_dve, 3 * i + 3)
                for h in range(2):
                    r = slice(HD * h, HD * (h + 1))
                    pool.tensor_copy(qbd[y][r, :, p, 8 * p + NQ * h:8 * p + NQ * (h + 1)],
                                     z_q[i % 2][r, h, SEQ:T].rearrange("d (b q) -> d b q", q=NQ)).then_inc(q_copied, 1)
                    pool.wait_ge(q_copied, 2 * i + h + 1)
                pool.tensor_copy(k_new[y][:, p, :], z_kv[i % 2][:, 0, SEQ:T]).then_inc(z_copied, 1)

            for u in range(4, IN_UNITS + RING):
                lo_part(u % RING, u % STAGE, u)
                if u in (10, 12):
                    pool.wait_ge(s_const_loaded, 16)
                    a = 2 * ((u - 10) // 2)
                    pool.tensor_copy(sb_r[:, a:a + 2, :],
                                     c_("s_bias" if a == 0 else "s_neg").rearrange("p (g k) -> p g k", k=SK)).then_inc(sb_ready, 1)
                if u >= 7 and (u - 7) % 3 == 0 and (u - 7) // 3 < 6:
                    pool.wait_ge(lo_done, u + 1)
                    keep_samples((u - 7) // 3)
            pool.wait_ge(m_ready, 6)
            pool.wait_ge(kv_out[0], 16 * 6)
            pool.wait_ge(kv_out[1], 16 * 6)
            pool.memset(vt[:, QT, :], 0.0).then_inc(vt_zero, 1)
            pool.wait_ge(vt_zero, 1)
            pool.memset(wbd[:, :, :], 0.0).then_inc(wbd_zero, 1)
            pool.wait_ge(g_loaded, 16 * (3 + GROUPS + NB))
            for g in range(GROUPS):
                pool.tensor_tensor(wsp[:, g, :], wsp[:, g, :], c_("upto"), ALU.mult).then_inc(wsp_ready, 1)
                pool.tensor_tensor(wbd[:, g, :], wbd[:, g, :], c_("s_chunk", NS), ALU.mult).then_inc(wsp_ready, 1)
            for u in range(IN_UNITS + RING, FF0 + RING):
                lo_part(u % RING, u % STAGE, u)
            for k in range(KT):
                pool.wait_ge(h1_lo, k + 1)
                pool.tensor_scalar(res[:, k, :], res[:, k, :], ALPHA, None, ALU.mult).then_inc(res_a, 1)

            first = [True]

            def segment(kind, par, prev, c):
                if first[0]:
                    first[0] = False
                    return
                for j in range(FG):
                    lo_part((FF0 + j) % RING, (FF0 + j) % STAGE, c["unit"] + j)
            mlp(pool, segment)

            pool.wait_ge(ln2_loaded, 32)
            for t in range(QT + 1):
                pool.wait_ge(y_g, t + 1)
                pool.tensor_tensor(y_n[0:rows[t], t % 2, :], y_n[0:rows[t], t % 2, :],
                                   ln2[0:rows[t], 1, :], ALU.add).then_inc(y_b, 1)

        @block.scalar
        def _(act):
            def hi_part(slot, stage, u, used, loaded):
                if used is not None:
                    act.wait_ge(half_done, used)
                act.wait_ge(w_loaded[stage], loaded)
                act.activation(w_hi[:, slot, :], w_raw[:, stage, :], ACT.Copy).then_inc(hi_done, 1)

            def hi_unit(u):
                hi_part(u % RING, u % STAGE, u, 2 * (u - RING + 1) if u >= RING else None, 16 * (u // STAGE + 1))

            act.wait_ge(init, 1)
            act.wait_ge(x_stat, 3 * (QT + 1))
            act.activation(x_sd[:, :], x_mv[:, :, 1], ACT.Sqrt, bias=eps[:, 0:1]).then_inc(x_std, 1)
            for u in range(2):
                hi_unit(u)
            for k in range(KT):
                act.wait_ge(res_ready, 2 * (k + 1))
                act.activation(h_hi[:, k, :], x_n[:, k, :], ACT.Copy).then_inc(hhi_ready, 1)
            hi_unit(2)
            hi_unit(3)
            act.wait_ge(init, 5)

            def read_half(u):
                i, j = divmod(u, 3)
                act.wait_ge(half_done, 2 * u + 1)
                src, scale = acc[:, 0, 0:HALF], 1.0
                if u >= 18:
                    act.activation(z_c[:, C_TILE[u - 18], 0:HALF], src, ACT.Copy).then_inc(acc_act, 1)
                    return
                if i >= 2 and j == 0:
                    act.wait_ge(z_copied, i - 1)
                if j == 0:
                    for h in range(2):
                        r = slice(HD * h, HD * (h + 1))
                        op = act.activation(z_q[i % 2][r, h, 0:HALF], acc[r, 0, 0:HALF], ACT.Copy, scale=SCALE)
                    op.then_inc(acc_act, 1)
                else:
                    act.activation(z_kv[i % 2][:, j - 1, 0:HALF], src, ACT.Copy).then_inc(acc_act, 1)

            for u in range(3):
                read_half(u)
                hi_unit(u + RING)

            def probs(n):
                i, s, t, h, L = item(n)
                b = n % 2
                if i < PAIRS:
                    act.wait_ge(max_ready, n + 1)
                else:
                    act.wait_ge(s_ready, n + 1)
                    act.wait_ge(p_scaled, n - 1)
                    act.activation(keep[:, b, 0:L], s_bank[b][:, 0:L], ACT.Sigmoid, scale=-1.0)
                if n >= 3:
                    act.wait_ge(pt_ready, n - 2)
                if i < PAIRS:
                    act.activation(prob[:, n % 3, 0:L], s_bank[b][:, 0:L], ACT.Exp, bias=nmx[:, b:b + 1],
                                   accum_out=rsum[:, b:b + 1]).then_inc(p_written, 1)
                else:
                    act.activation(prob[:, n % 3, 0:L], s_bank[b][:, 0:L], ACT.Sigmoid).then_inc(p_written, 1)

            def keep_turned(n):
                i, s, t, h, L = item(n)
                act.wait_ge(pt_ready, n + 1)
                act.activation(prob_t[h][:, t * (t + 1) // 2:(t + 1) * (t + 2) // 2, :],
                               pt_bank(n)[:, 0:L].rearrange("p (k q) -> p k q", q=P), ACT.Copy).then_inc(pt_read, 1)

            for n in range(ITEMS + 4):
                i, s = divmod(n, 8)
                if n < ITEMS:
                    probs(n)
                if n < ITEMS and s < 2:
                    act.wait_ge(kv_t, 3 * i + s + 1)
                    if i >= 2:
                        act.wait_ge(kv_out[i % 2], 32 * (i // 2))
                    y, p = divmod(i, PAIRS)
                    dst = (k_tok, v_tok)[s][i % 2]
                    act.activation(dst[:, :, :], acc[:, 3, :], ACT.Copy).then_inc(kv_act, 1)
                    act.wait_ge(kv_act, 2 * i + s + 1)
                    act.dma_start(kv_prompt[y][s][:, :, P * p:P * (p + 1)], dst[:, :, :]).then_inc(kv_out[i % 2], 16)
                if 2 <= n < ITEMS + 2:
                    keep_turned(n - 2)
                if i >= 1 and s == 3:
                    act.wait_ge(o_ready, 4 * i)
                    act.activation(m_hi[:, i - 1, 0:SEQ], o_bank[:, :], ACT.Copy).then_inc(mhi_ready, 1)
                if n < ITEMS:
                    if s in (1, 3, 6):
                        read_half(3 * (i + 1) + (1, 3, 6).index(s))
                    if s in (2, 5, 7):
                        u = 3 * (i + 1) + (2, 5, 7).index(s)
                        hi_unit(u + RING)
            read_half(21)
            hi_unit(21 + RING)

            def page(q):
                act.wait_ge(kt_pe, q + 1)
                act.wait_ge(sc_pe, q // 8) if q >= 8 else None
                act.activation(k_t[:, (q // 2) % 4, :, 0:PAGE], page_bank(q)[:, 0:W_ATT].rearrange("p (h k) -> p h k", k=PAGE),
                               ACT.Copy).then_inc(kt_act, 1)

            act.wait_ge(m_ready, 6)
            act.wait_ge(acc_act, IN_UNITS)
            act.wait_ge(acc_dve, IN_UNITS)
            act.activation(z_c[:, 2:4, :], z_c[:, 2:4, :], ACT.Gelu_apprx_tanh).then_inc(gelu_done, 1)
            page(0)
            act.wait_ge(vt_zero, 1)
            act.wait_ge(vt_ready, 1)
            for j in range(2):
                act.activation(vt[:, 2 * j:2 * j + 2, :], acc[:, j, :], ACT.Copy).then_inc(vt_read, 1)
            page(2)
            act.wait_ge(vt_ready, 2)
            act.activation(vt[0:NS, QT, :], acc[0:NS, 0, 0:W_C], ACT.Copy).then_inc(vt_read, 1)
            act.activation(z_c[:, 0:2, :], z_c[:, 0:2, :], ACT.Gelu_apprx_tanh).then_inc(gelu_done, 1)
            act.wait_ge(v_chain, 3)
            act.activation(vsq[:, :, :], vt[:, :, :], ACT.Square).then_inc(v_sq, 1)
            page(4)
            page(6)
            act.wait_ge(v_chain, 4)
            act.activation(v_s[:, 2, :], v_s[:, 1, :], ACT.Sqrt, bias=eps[:, 0:1], scale=1.0 / HD).then_inc(v_sq, 1)

            for gi in range(1, 5):
                g, q0 = gi - 1, 8 * gi
                y, grp = divmod(g, 2)
                if g:
                    act.wait_ge(st_pe, g)
                if y == 0:
                    act.wait_ge(e2, g + 1)
                    act.activation(s_prob[:, :], t_bank[:, 0:SK], ACT.Exp, bias=s_st[:, 1:2],
                                   accum_out=s_st[:, 2:3]).then_inc(sp_written, 1)
                else:
                    act.wait_ge(sc_pe, g + 1)
                    act.wait_ge(s_scaled, g)
                    act.activation(sw[0][:, :], t_bank[:, 0:SK], ACT.Sigmoid, scale=-1.0)
                    act.activation(s_prob[:, :], t_bank[:, 0:SK], ACT.Sigmoid).then_inc(sp_written, 1)
                if gi == 1:
                    act.wait_ge(v_chain, 8)
                    act.dma_start(v_c_sample.rearrange("l b t c -> (l b t) c"), vt[0:NS, QT, :]).then_inc(out_s, 16)
                    act.wait_ge(s_read, 6)
                    for yy in range(2):
                        for w in range(2):
                            act.dma_start(kv_sample[yy][w], kv_new[yy][:, w, :]).then_inc(out_s, 16)
                if gi < 4:
                    page(q0)
                    page(q0 + 2)
                act.wait_ge(st_pe, g + 1)
                act.activation(s_pt[:, 0:2, :], o_bank[:, 0:2 * P], ACT.Copy).then_inc(st_act, 1)
                act.activation(s_pt[0:NS, 2, :], o_bank[0:NS, 2 * P:3 * P], ACT.Copy).then_inc(st_act, 1)
                if gi < 4:
                    page(q0 + 4)
                    page(q0 + 6)
                act.wait_ge(ot_pe, g + 1)
                act.activation(m_hi[:, 3 * y:3 * y + 3, SEQ + 16 * grp:SEQ + 16 * (grp + 1)],
                               o_bank[:, 0:48].rearrange("p (t c) -> p t c", c=16), ACT.Copy).then_inc(ot_hi, 1)
                if gi == 3:
                    act.wait_ge(mix_dve, 8)
                    act.activation(m_hi[:, 6:8, :], z_c[:, 0:2, :], ACT.Copy).then_inc(mix_hi, 1)

            for u in range(IN_UNITS + RING, FF0 + RING):
                hi_unit(u)

            act.wait_ge(out_s, 16 * 5)
            act.wait_ge(mean_pe, 1)
            for hf in range(2):
                act.activation(mean_b[:, HALF * hf:HALF * (hf + 1)], s_bank[hf][:, 0:HALF], ACT.Copy).then_inc(mean_sb, 1)
            for k in range(KT):
                act.wait_ge(cent, k + 1)
                if k >= 2:
                    act.wait_ge(sq_pe, k - 1)
                act.activation(sq[:, k % 2, :], res[:, k, :], ACT.Square).then_inc(sq_done, 1)
            act.wait_ge(sq_pe, KT)
            act.activation(sd_b[:, 0:HALF], t_bank[:, 0:HALF], ACT.Sqrt, bias=eps[:, 0:1]).then_inc(std_done, 1)
            act.activation(sd_b[:, HALF:T], o_bank[:, 0:HALF], ACT.Sqrt, bias=eps[:, 0:1]).then_inc(std_done, 1)
            for k in range(KT):
                act.wait_ge(nrm, k + 1)
                act.activation(res[:, k, :], res[:, k, :], ACT.Identity, bias=lnp[:, 3, k:k + 1],
                               scale=lnp[:, 2, k:k + 1]).then_inc(x1_done, 1)
                act.wait_ge(x1_done, k + 1)
                act.activation(h_hi[:, k, :], res[:, k, :], ACT.Copy).then_inc(h1_hi, 1)

            def segment(kind, par, prev, c):
                for j in range(FG):
                    if kind == "up":
                        act.wait_ge(half_done, (c["tile"] + j) * 2 + 1)
                        if not (isinstance(c["up"], int) and FG * c["up"] + j < 2):
                            act.wait_ge(sq_h, c["up"] * FG + (j - 1))
                        act.activation(relu[:, j % 2, 0:HALF], acc[:, 2 * (j % 2), 0:HALF],
                                       ACT.Relu).then_inc(acc_act, 1)
                    u = c["unit"] + j
                    if isinstance(u, int) and u + RING >= UNITS:
                        continue
                    used = 2 * (j + 1) if kind == "up" else 4 * (j + 1)
                    hi_part((FF0 + j) % RING, (FF0 + j) % STAGE, u + RING, c["tile"] * 2 + used,
                            c["unit"] * (16 // STAGE) + 16 * ((j + RING) // STAGE + 1))
            mlp(act, segment)

            for t in range(QT + 1):
                r = rows[t]
                act.wait_ge(y_c, 3 * (t + 1))
                act.activation(y_sd[0:r, t:t + 1], y_mv[0:r, t, 1:2], ACT.Sqrt, bias=eps[0:r, 0:1]).then_inc(y_std, 1)

        @block.vector
        def _(dve):
            dve.memset(x_mv[:, :, :], 1.0).then_inc(d0, 1)
            dve.wait_ge(d0, 1)
            for t in range(QT + 1):
                r = rows[t]
                dve.wait_ge(x_loaded[t], 16)
                for j in range(2):
                    dve.bn_stats(x_st[0:r, t, 6 * j:6 * j + 6],
                                 xin[0:r, t, 512 * j:512 * (j + 1)]).then_inc(x_stat, 1)
                dve.wait_ge(x_stat, 3 * t + 2)
                dve.bn_aggr(x_mv[0:r, t, :], x_st[0:r, t, :]).then_inc(x_stat, 1)
            dve.wait_ge(x_std, 1)
            dve.reciprocal(x_rs[:, :], x_sd[:, :]).then_inc(x_std, 1)
            dve.wait_ge(x_std, 2)
            for t in range(QT + 1):
                r = rows[t]
                dve.tensor_scalar(xin[0:r, t, :], xin[0:r, t, :], x_mv[0:r, t, 0:1], x_rs[0:r, t:t + 1],
                                  ALU.subtract, ALU.mult).then_inc(x_norm, 1)
            dve.wait_ge(const_loaded, 32)

            def lo_odd(k):
                dve.wait_ge(hhi_ready, k + 1)
                dve.tensor_tensor(h_lo[:, k, :], x_n[:, k, :], h_hi[:, k, :].bitcast(F32),
                                  ALU.subtract).then_inc(h_ready, 1)
            for k in range(KT):
                dve.wait_ge(xt_ready, k + 1)
                for dst, bank, n in ((slice(0, SEQ), 0, SEQ), (slice(SEQ, T), 1, NS)):
                    dve.tensor_scalar(x_n[:, k, dst], acc[:, 2 * (k % 2) + bank, 0:n], lnp[:, 0, k:k + 1],
                                      lnp[:, 1, k:k + 1], ALU.mult, ALU.add).then_inc(res_ready, 1)
                if k >= 3 and k % 2:
                    lo_odd(k - 2)
            lo_odd(KT - 1)
            dve.wait_ge(init, 5)

            def read_half(u):
                i, j = divmod(u, 3)
                dve.wait_ge(half_done, 2 * u + 2)
                src = acc[:, 1, 0:HALF]
                if u >= 18:
                    dve.tensor_copy(z_c[:, C_TILE[u - 18], HALF:T], src).then_inc(acc_dve, 1)
                    return
                if i >= 2 and j == 0:
                    dve.wait_ge(z_copied, i - 1)
                if j == 0:
                    for h in range(2):
                        r = slice(HD * h, HD * (h + 1))
                        op = dve.tensor_scalar(z_q[i % 2][r, h, HALF:T], acc[r, 1, 0:HALF], SCALE, None, ALU.mult)
                    op.then_inc(acc_dve, 1)
                else:
                    dve.tensor_copy(z_kv[i % 2][:, j - 1, HALF:T], src).then_inc(acc_dve, 1)

            for u in range(3):
                read_half(u)

            def row_max(n):
                i, s, t, h, L = item(n)
                b = n % 2
                dve.wait_ge(s_ready, n + 1)
                dve.tensor_reduce(mx[:, b:b + 1], s_bank[b][:, 0:L], AX_X, ALU.max).then_inc(d1, 1)
                dve.wait_ge(d1, n + 1)
                dve.tensor_scalar(nmx[:, b:b + 1], mx[:, b:b + 1], -1.0, None, ALU.mult).then_inc(max_ready, 1)

            def normalise(n):
                i, s, t, h, L = item(n)
                b = n % 2
                dve.wait_ge(p_written, n + 1)
                dve.reciprocal(rinv[:, b:b + 1], rsum[:, b:b + 1]).then_inc(d2, 1)
                dve.wait_ge(d2, n + 1)
                dve.tensor_scalar(prob[:, n % 3, 0:L], prob[:, n % 3, 0:L], rinv[:, b:b + 1], None,
                                  ALU.mult).then_inc(p_scaled, 1)

            def stick(n):
                i, s, t, h, L = item(n)
                b = n % 2
                dve.wait_ge(p_written, n + 1)
                back = keep[:, b, 0:L][:, ::-1]
                dve.tensor_tensor_scan(left[:, b, 0:L][:, ::-1], back, back, 1.0, ALU.mult, ALU.min).then_inc(d3, 1)
                dve.wait_ge(d3, n - 8 * PAIRS + 1)
                dve.tensor_tensor(prob[:, n % 3, 0:L - 1], prob[:, n % 3, 0:L - 1], left[:, b, 1:L],
                                  ALU.mult).then_inc(p_scaled, 1)

            dve.wait_ge(const2_loaded, 16)
            for n in range(ITEMS + 4):
                i, s = divmod(n, 8)
                if n < 8 * PAIRS:
                    row_max(n)
                if 1 <= n <= ITEMS:
                    normalise(n - 1) if n - 1 < 8 * PAIRS else stick(n - 1)
                if n < ITEMS and s == 2:
                    y, p = divmod(i, PAIRS)
                    dve.wait_ge(kv_t, 3 * i + 3)
                    dve.tensor_copy(kv_new[y][:, :, P * p:P * (p + 1)],
                                    acc[0:NS, 3, 0:2 * P].rearrange("t (w c) -> t w c", w=2)).then_inc(s_read, 1)
                if i >= 1 and s == 3:
                    dve.wait_ge(mhi_ready, i)
                    dve.tensor_tensor(m_lo[:, i - 1, 0:SEQ], o_bank[:, :], m_hi[:, i - 1, 0:SEQ].bitcast(F32),
                                      ALU.subtract).then_inc(m_ready, 1)
                if n < ITEMS and s in (2, 5, 7):
                    read_half(3 * (i + 1) + (2, 5, 7).index(s))
            read_half(21)

            def page(q):
                dve.wait_ge(kt_pe, q + 1)
                dve.wait_ge(sc_pe, q // 8) if q >= 8 else None
                dve.tensor_copy(k_t[:, (q // 2) % 4, :, PAGE:PAST],
                                page_bank(q)[:, 0:W_ATT].rearrange("p (h k) -> p h k", k=PAGE)).then_inc(kt_dve, 1)

            def bc(j):
                return v_s[:, j, :].rearrange("p (a o) -> p a o", o=1).to_broadcast([P, (QT + 1) * GROUPS, HD])
            vg = vt[:, :, :].rearrange("p t (g d) -> p (t g) d", d=HD)
            vall = vsq[:, :, :].rearrange("p t (g d) -> p (t g) d", d=HD)
            page(1)
            page(3)
            dve.wait_ge(vt_read, 3)
            dve.tensor_reduce(v_s[:, 0, :], vg, AX_X, ALU.add).then_inc(v_chain, 1)
            dve.wait_ge(v_chain, 1)
            dve.tensor_scalar(v_s[:, 1, :], v_s[:, 0, :], 1.0 / HD, None, ALU.mult).then_inc(v_chain, 1)
            dve.wait_ge(v_chain, 2)
            dve.tensor_tensor(vg, vg, bc(1), ALU.subtract).then_inc(v_chain, 1)
            page(5)
            dve.wait_ge(v_sq, 1)
            dve.tensor_reduce(v_s[:, 1, :], vall, AX_X, ALU.add).then_inc(v_chain, 1)
            page(7)
            dve.wait_ge(v_sq, 2)
            dve.reciprocal(v_s[:, 3, :], v_s[:, 2, :]).then_inc(v_chain, 1)
            dve.wait_ge(v_chain, 5)
            dve.tensor_tensor(vg, vg, bc(3), ALU.mult).then_inc(v_chain, 1)
            dve.wait_ge(g_loaded, 16 * (3 + GROUPS + NB))
            for j, op in enumerate((ALU.mult, ALU.add)):
                dve.wait_ge(v_chain, 6 + j)
                row = lnc[:, j, :].rearrange("p (o c) -> p o c", o=1).to_broadcast([P, QT + 1, W_C])
                dve.tensor_tensor(vt[:, :, :], vt[:, :, :], row, op).then_inc(v_chain, 1)

            tmp = vsq[:, :, :].rearrange("p t c -> p (t c)")

            def mix(j, cols, src, at, parts, width):
                done = 2 * (j + (2 if at >= 2 * SEQ else 0))
                n = parts * width
                tj = tmp[:, at:at + n].rearrange("p (c t) -> p c t", t=width)
                row = bsp[:, j, 0:width].rearrange("p (o t) -> p o t", o=1).to_broadcast([P, parts, width])
                dve.tensor_tensor(tj, src.rearrange("p (c t) -> p c t", t=width), row, ALU.add).then_inc(mix_dve, 1)
                dve.wait_ge(mix_dve, done + 1)
                dve.tensor_tensor(z_c[:, j, cols], z_c[:, j, cols], tmp[:, at:at + n], ALU.mult).then_inc(mix_dve, 1)

            S = t_bank[:, 0:SK]
            for gi in range(1, 5):
                g, q0 = gi - 1, 8 * gi
                y, grp = divmod(g, 2)
                if y == 0:
                    dve.wait_ge(sc_pe, g + 1)
                    dve.tensor_reduce(s_st[:, 0:1], S, AX_X, ALU.max).then_inc(e1, 1)
                    dve.wait_ge(e1, g + 1)
                    dve.tensor_scalar(s_st[:, 1:2], s_st[:, 0:1], -1.0, None, ALU.mult).then_inc(e2, 1)
                if gi < 4:
                    page(q0 + 1)
                dve.wait_ge(sp_written, g + 1)
                if y == 0:
                    dve.reciprocal(s_st[:, 3:4], s_st[:, 2:3]).then_inc(s_scaled, 1)
                else:
                    back = sw[0][:, ::-1]
                    dve.tensor_tensor_scan(sw[1][:, ::-1], back, back, 1.0, ALU.mult, ALU.min).then_inc(e4, 1)
                    dve.wait_ge(e4, grp + 1)
                    dve.tensor_tensor(s_prob[:, 0:SK - 1], s_prob[:, 0:SK - 1], sw[1][:, 1:SK], ALU.mult).then_inc(s_scaled, 1)
                if gi == 1:
                    dve.wait_ge(gelu_done, 2)
                    for j in range(2):
                        dve.wait_ge(mix_ready, j + 1)
                        mix(j, slice(0, SEQ), acc[:, j, :], SEQ * j, QT, CHUNK)
                if gi < 4:
                    page(q0 + 3)
                    page(q0 + 5)
                dve.wait_ge(pv_pe, g + 1)
                dve.wait_ge(s_scaled, g + 1)
                dve.scalar_tensor_tensor(s_om[:, :], acc[:, 2, 0:W_ATT], s_st[:, 3:4] if y == 0 else 1.0,
                                         c_("s_head"), ALU.mult, ALU.mult).then_inc(om_done, 1)
                if gi == 2:
                    dve.wait_ge(mix_ready, 3)
                    for j in range(2):
                        mix(j, slice(SEQ, T), acc[:, 0, NS * j:NS * (j + 1)], 2 * SEQ + NS * j, NB, NQ)
                if gi < 4:
                    page(q0 + 7)
                dve.wait_ge(ot_hi, g + 1)
                dst = slice(SEQ + 16 * grp, SEQ + 16 * (grp + 1))
                dve.tensor_tensor(m_lo[:, 3 * y:3 * y + 3, dst], o_bank[:, 0:48].rearrange("p (t c) -> p t c", c=16),
                                  m_hi[:, 3 * y:3 * y + 3, dst].bitcast(F32), ALU.subtract).then_inc(ot_lo, 1)
                if gi == 3:
                    dve.wait_ge(mix_hi, 1)
                    dve.tensor_tensor(m_lo[:, 6:8, :], z_c[:, 0:2, :], m_hi[:, 6:8, :].bitcast(F32),
                                      ALU.subtract).then_inc(mix_lo, 1)

            def halves(hf):
                return slice(HALF * hf, HALF * (hf + 1))
            for m in range(KT):
                u = IN_UNITS + m
                if m == 0:
                    dve.wait_ge(ot_lo, 4)
                dve.tensor_tensor(res[:, m, :], h_hi[:, m, :].bitcast(F32), h_lo[:, m, :].bitcast(F32), ALU.add).then_inc(stream, 1)
                dve.wait_ge(stream, m + 1)
                for hf in range(2):
                    dve.wait_ge(half_done, 2 * u + hf + 1)
                    dve.scalar_tensor_tensor(res[:, m, halves(hf)], res[:, m, halves(hf)], ALPHA,
                                             acc[:, 2 * (u % 2) + hf, 0:HALF], ALU.mult, ALU.add).then_inc(acc_dve, 1)
            dve.wait_ge(out_s, 16 * 5)
            dve.wait_ge(mean_sb, 2)
            for k in range(KT):
                dve.tensor_tensor(res[:, k, :], res[:, k, :], mean_b[:, :], ALU.subtract).then_inc(cent, 1)
            dve.wait_ge(std_done, 2)
            dve.reciprocal(rstd_b[:, :], sd_b[:, :]).then_inc(rstd_done, 1)
            dve.wait_ge(rstd_done, 1)
            for k in range(KT + 2):
                if k < KT:
                    dve.tensor_tensor(res[:, k, :], res[:, k, :], rstd_b[:, :], ALU.mult).then_inc(nrm, 1)
                if k >= 2:
                    dve.wait_ge(h1_hi, k - 1)
                    dve.tensor_tensor(h_lo[:, k - 2, :], res[:, k - 2, :], h_hi[:, k - 2, :].bitcast(F32),
                                      ALU.subtract).then_inc(h1_lo, 1)

            def segment(kind, par, prev, c):
                if kind == "up":
                    for j in range(UPS):
                        done = c["up"] * FG + (j + 1)
                        dve.wait_ge(half_done, (c["tile"] + j) * 2 + 2)
                        dve.tensor_scalar(relu[:, j % 2, HALF:T], acc[:, 2 * (j % 2) + 1, 0:HALF], 0.0, None,
                                          ALU.max).then_inc(acc_dve, 1)
                        dve.wait_ge(acc_act, c["act"] + (j + 1))
                        dve.wait_ge(acc_dve, c["dve"] + (j + 1))
                        dve.tensor_tensor(hid[:, j % 2, :], relu[:, j % 2, :], relu[:, j % 2, :], ALU.mult).then_inc(sq_h, 1)
                        dve.wait_ge(sq_h, done)
                        dve.tensor_copy(m_hi[:, FG * par + j, :], hid[:, j % 2, :]).then_inc(hid_hi, 1)
                        dve.wait_ge(hid_hi, done)
                        dve.tensor_tensor(m_lo[:, FG * par + j, :], hid[:, j % 2, :],
                                          m_hi[:, FG * par + j, :].bitcast(F32), ALU.subtract).then_inc(hid_lo, 1)
                else:
                    for m in range(DOWNS):
                        for hf in range(2):
                            dve.wait_ge(half_done, (c["tile"] + m) * 2 + (hf + 1))
                            if m == 0 and hf == 0:
                                dve.wait_ge(res_a, KT)
                            dve.tensor_tensor(res[:, m, halves(hf)], res[:, m, halves(hf)],
                                              acc[:, 2 * (m % 2) + hf, 0:HALF], ALU.add).then_inc(acc_dve, 1)
            mlp(dve, segment)

            for t in range(QT + 1):
                r = rows[t]
                banks = y_banks(t)
                dve.wait_ge(yt_pe, t + 1)
                for j in range(2):
                    dve.bn_stats(y_st[0:r, t, 6 * j:6 * j + 6], banks[j][0:r, :]).then_inc(y_c, 1)
                dve.wait_ge(y_c, 3 * t + 2)
                dve.bn_aggr(y_mv[0:r, t, :], y_st[0:r, t, :]).then_inc(y_c, 1)
                dve.wait_ge(y_std, t + 1)
                dve.reciprocal(y_rs[0:r, t:t + 1], y_sd[0:r, t:t + 1]).then_inc(y_rec, 1)
                dve.wait_ge(y_rec, t + 1)
                if t >= 2:
                    dve.wait_ge(y_out[t % 2], 16 * (t // 2))
                for j in range(2):
                    dve.tensor_scalar(y_n[0:r, t % 2, 512 * j:512 * (j + 1)], banks[j][0:r, :],
                                      y_mv[0:r, t, 0:1], y_rs[0:r, t:t + 1], ALU.subtract, ALU.mult).then_inc(yt_read, 1)
                dve.wait_ge(yt_read, 2 * (t + 1))
                if t == 0:
                    dve.wait_ge(ln2_loaded, 32)
                dve.tensor_tensor(y_n[0:r, t % 2, :], y_n[0:r, t % 2, :], ln2[0:r, 0, :], ALU.mult).then_inc(y_g, 1)

        @block.tensor
        def _(pe):
            pe.wait_ge(const_loaded, 32)
            for k in range(KT):
                if k >= 2:
                    pe.wait_ge(res_ready, 2 * (k - 1))
                for t in range(QT):
                    if k == 0:
                        pe.wait_ge(x_norm, t + 1)
                    pe.transpose(acc[:, 2 * (k % 2), P * t:P * (t + 1)], xin[:, t, P * k:P * (k + 1)], ident(P))
                if k == 0:
                    pe.wait_ge(x_norm, QT + 1)
                pe.transpose(acc[:, 2 * (k % 2) + 1, 0:NS], xin[0:NS, QT, P * k:P * (k + 1)],
                             ident(NS)).then_inc(xt_ready, 1)

            def halves(hf):
                return slice(HALF * hf, HALF * (hf + 1))

            def product(slot, cols, hi, lo, ks, out, part=slice(None)):
                work = [(hf, k, pas) for hf in range(2) for k in range(len(ks)) for pas in range(3)]
                for hf, k, pas in work[part]:
                    w = (w_hi, w_hi, w_lo)[pas]
                    x = (hi, lo, hi)[pas]
                    last = k == len(ks) - 1 and pas == 2
                    mm = pe.matmul(out[hf], w[:, slot, cols(k)], x[:, ks[k], halves(hf)],
                                   start=(k == 0 and pas == 0), stop=last)
                    if last:
                        mm.then_inc(half_done, 1)

            def cols(k):
                return slice(P * k, P * (k + 1))

            def in_unit(u, c):
                if c == 0:
                    pe.wait_ge(lo_done, u + 1)
                    if u:
                        pe.wait_ge(acc_act, u)
                if c == 4 and u:
                    pe.wait_ge(acc_dve, u)
                product(u % RING, cols, h_hi, h_lo, range(KT), [acc[:, hf, 0:HALF] for hf in range(2)],
                        slice(6 * c, 6 * (c + 1)))

            pe.wait_ge(h_ready, KT)
            pe.wait_ge(res_ready, 2 * KT)
            for u in range(3):
                for c in range(8):
                    in_unit(u, c)
            pe.wait_ge(bias_ready, H + 3)

            def scores(n):
                i, s, t, h, L = item(n)
                b = n % 2
                if n >= 2:
                    pe.wait_ge(p_written, n - 1)
                q = z_q[i % 2][:, h, P * t:P * (t + 1)]
                out = s_bank[b]
                if i < PAIRS:
                    pe.matmul(out[:, 0:L], sid_r[:, 2 * i + h, :], dist_r[:, SEQ - L:SEQ], start=True, stop=False)
                    pe.matmul(out[:, 0:L], q, z_kv[i % 2][:, 0, 0:L], start=False, stop=True).then_inc(s_ready, 1)
                else:
                    pe.matmul(out[:, 0:L], q, z_kv[i % 2][:, 0, 0:L], start=True, stop=False)
                    pe.matmul(out[:, L - P:L], id_r[:, :], below_r[:, :], start=False, stop=True).then_inc(s_ready, 1)

            def turn_probs(n):
                i, s, t, h, L = item(n)
                pe.wait_ge(p_scaled, n + 1)
                if n >= 2:
                    pe.wait_ge(pt_read, n - 1)
                for kb in range(t + 1):
                    mm = pe.transpose(pt_bank(n)[:, P * kb:P * (kb + 1)], prob[:, n % 3, P * kb:P * (kb + 1)], ident(P))
                mm.then_inc(pt_ready, 1)

            def values(n):
                i, s, t, h, L = item(n)
                pe.wait_ge(pt_read, n + 1)
                if t == 0:
                    pe.wait_ge(kv_act, 2 * i + 2)
                    if i:
                        pe.wait_ge(m_ready, i)
                for kb in range(t + 1):
                    for hh in range(2):
                        r = slice(HD * hh, HD * (hh + 1))
                        mm = pe.matmul(o_bank[r, P * t:P * (t + 1)], v_tok[i % 2][:, kb, r],
                                       prob_t[hh][:, t * (t + 1) // 2 + kb, :], start=(kb == 0), stop=(kb == t))
                mm.then_inc(o_ready, 1)

            def turn_kv(i, s):
                src = z_kv[i % 2]
                if s == 0:
                    pe.wait_ge(acc_act, 3 * i + 3)
                    pe.wait_ge(acc_dve, 3 * i + 3)
                    if i:
                        pe.wait_ge(s_read, i)
                else:
                    pe.wait_ge(kv_act, 2 * i + s)
                if s < 2:
                    for t in range(QT):
                        mm = pe.transpose(acc[:, 3, P * t:P * (t + 1)], src[:, s, P * t:P * (t + 1)], ident(P))
                else:
                    for w in range(2):
                        mm = pe.transpose(acc[0:NS, 3, P * w:P * (w + 1)], src[:, w, SEQ:T], ident(P))
                mm.then_inc(kv_t, 1)

            fill = [(u, c) for u in range(3, IN_UNITS) for c in range(8)]
            for n in range(ITEMS + 4):
                i, s = divmod(n, 8)
                if n < ITEMS:
                    if s == 0:
                        pe.wait_ge(acc_act, 3 * i + 2)
                        pe.wait_ge(acc_dve, 3 * i + 2)
                    scores(n)
                for uc in fill[3 * n:3 * n + 1]:
                    in_unit(*uc)
                if 2 <= n < ITEMS + 2:
                    turn_probs(n - 2)
                for uc in fill[3 * n + 1:3 * n + 2]:
                    in_unit(*uc)
                if n >= 4 and n % 2 == 0:
                    values(n - 3)
                if n < ITEMS and s < 3:
                    turn_kv(i, s)
                for uc in fill[3 * n + 2:3 * n + 3]:
                    in_unit(*uc)

            pe.wait_ge(gelu_done, 1)
            pe.wait_ge(acc_act, IN_UNITS)
            pe.wait_ge(acc_dve, IN_UNITS)
            for t in range(QT):
                for ct in range(2):
                    mm = pe.transpose(acc[:, t // 2, W_C * (t % 2) + P * ct:W_C * (t % 2) + P * (ct + 1)],
                                      z_c[:, 2 + ct, P * t:P * (t + 1)], ident(P))
            mm.then_inc(vt_ready, 1)

            def page(q):
                n, pg = divmod(q, 2)
                pe.wait_ge(kp_loaded[n % 2], 16 * PAGES * (n // 2 + 1))
                if q >= 3:
                    pe.wait_ge(kt_dve if q % 2 == 0 else kt_act, (q - 3) // 2 + 1)
                for p in range(PAIRS):
                    mm = pe.transpose(page_bank(q)[:, P * p:P * (p + 1)], k_pg[:, n % 2, pg, P * p:P * (p + 1)], ident(P))
                mm.then_inc(kt_pe, 1)

            def s_scores(gi):
                y, grp = divmod(gi, 2)
                pe.wait_ge(kt_act, 4 * (gi + 1))
                pe.wait_ge(kt_dve, 4 * (gi + 1))
                if gi == 0:
                    pe.wait_ge(sb_ready, 2)
                    pe.wait_ge(z_copied, 6)
                if gi:
                    pe.wait_ge(sp_written, gi)
                pe.matmul(t_bank[:, 0:SK], id_r[:, :], sb_r[:, gi, :], start=True, stop=False)
                for new in range(2):
                    for p in range(PAIRS):
                        for b4 in range(4):
                            out = t_bank[32 * b4:32 * (b4 + 1), PAST:SK] if new else t_bank[32 * b4:32 * (b4 + 1), 0:PAST]
                            keys = k_new[y][:, p, :] if new else k_t[:, b4, p, :]
                            mm = pe.matmul(out, qbd[y][:, 4 * grp + b4, p, :], keys, start=False,
                                           stop=(new == 1 and p == PAIRS - 1), tile_position=(0, 32 * b4))
                mm.then_inc(sc_pe, 1)

            def turn_s_probs(g):
                pe.wait_ge(sp_written, g + 1)
                if g >= 2:
                    pe.wait_ge(s_scaled, g + 1)
                if g:
                    pe.wait_ge(ot_lo, g)
                pe.transpose(o_bank[:, 0:P], s_prob[:, 0:P], ident(P))
                pe.transpose(o_bank[:, P:2 * P], s_prob[:, P:2 * P], ident(P))
                pe.transpose(o_bank[0:NS, 2 * P:3 * P], s_prob[:, 2 * P:SK], ident(P)).then_inc(st_pe, 1)

            def s_values(g):
                y = g // 2
                pe.wait_ge(st_act, 2 * (g + 1))
                if g:
                    pe.wait_ge(om_done, g)
                for pg in range(PAGES + 1):
                    for b4 in range(4):
                        if pg == 0:
                            pe.wait_ge(vp_loaded[b4], 16 * PAGES * (g + 1))
                        r = slice(32 * b4, 32 * (b4 + 1))
                        if pg < PAGES:
                            pe.matmul(acc[r, 2, 0:W_ATT], s_pt[:, pg, r], v_pg[:, b4, pg, :], start=(pg == 0),
                                      stop=False, tile_position=(0, 32 * b4))
                        else:
                            mm = pe.matmul(acc[r, 2, 0:W_ATT], s_pt[0:NS, 2, r], kv_new[y][:, 1, :], start=False,
                                           stop=True, tile_position=(0, 32 * b4))
                mm.then_inc(pv_pe, 1)

            def s_pick(g):
                pe.wait_ge(om_done, g + 1)
                for p in range(PAIRS):
                    mm = pe.matmul(o_bank[:, 16 * p:16 * (p + 1)], s_om[:, P * p:P * (p + 1)], c_("s_pick"),
                                   start=True, stop=True)
                mm.then_inc(ot_pe, 1)

            for gi in range(5):
                for j in range(8):
                    if gi < 4:
                        page(8 * gi + j)
                    if gi == 0 and j == 1:
                        pe.wait_ge(vt_read, 1)
                        for ct in range(2):
                            mm = pe.transpose(acc[0:NS, 0, P * ct:P * (ct + 1)], z_c[:, 2 + ct, SEQ:T], ident(P))
                        mm.then_inc(vt_ready, 1)
                    if gi == 1 and j == 0:
                        pe.wait_ge(v_chain, 8)
                        pe.wait_ge(vt_read, 3)
                        pe.wait_ge(wsp_ready, 2 * GROUPS)
                        for jj in range(2):
                            for ch in range(QT):
                                for g2 in range(2):
                                    g = 2 * jj + g2
                                    mm = pe.matmul(acc[HD * g2:HD * (g2 + 1), jj, CHUNK * ch:CHUNK * (ch + 1)],
                                                   vt[:, ch, HD * g:HD * (g + 1)], wsp[:, g, :], start=True, stop=True)
                            mm.then_inc(mix_ready, 1)
                    if gi == 2 and j == 0:
                        pe.wait_ge(mix_dve, 4)
                        for jj in range(2):
                            for g2 in range(2):
                                g = 2 * jj + g2
                                mm = pe.matmul(acc[HD * g2:HD * (g2 + 1), 0, NS * jj:NS * (jj + 1)],
                                               vt[0:NS, QT, HD * g:HD * (g + 1)], wbd[:, g, :], start=True, stop=True)
                        mm.then_inc(mix_ready, 1)
                    if gi and j == 2:
                        turn_s_probs(gi - 1)
                    if gi and j == 4:
                        s_values(gi - 1)
                    if gi and j == 6:
                        s_pick(gi - 1)
                if gi < 4:
                    s_scores(gi)

            pe.wait_ge(ot_lo, 4)
            pe.wait_ge(mix_lo, 1)

            def out_unit(m):
                u = IN_UNITS + m
                pe.wait_ge(lo_done, u + 1)
                if m >= 2:
                    pe.wait_ge(acc_dve, dve_reads(u - 1))
                b = 2 * (u % 2)
                product(u % RING, cols, m_hi, m_lo, range(KT), [acc[:, b + hf, 0:HALF] for hf in range(2)])

            def mean_step(k):
                pe.wait_ge(acc_dve, dve_reads(IN_UNITS + k + 1))
                for hf in range(2):
                    mm = pe.matmul(s_bank[hf][:, 0:HALF], c_("mean"), res[:, k, halves(hf)],
                                   start=(k == 0), stop=(k == KT - 1))
                if k == KT - 1:
                    mm.then_inc(mean_pe, 1)
            for m in range(KT):
                out_unit(m)
                if m:
                    mean_step(m - 1)
            mean_step(KT - 1)
            for k in range(KT):
                pe.wait_ge(sq_done, k + 1)
                for hf, bank in enumerate((t_bank, o_bank)):
                    mm = pe.matmul(bank[:, 0:HALF], c_("mean"), sq[:, k % 2, halves(hf)],
                                   start=(k == 0), stop=(k == KT - 1))
                mm.then_inc(sq_pe, 1)

            pe.wait_ge(h1_lo, KT)

            def segment(kind, par, prev, c):
                first = (0, 2) if prev == "down" else (1, 1)
                if kind == "up":
                    for j in range(UPS):
                        pe.wait_ge(lo_done, c["unit"] + (j + 1))
                        a, d = (j - 1, j - 1) if j else (-first[0], -first[1])
                        pe.wait_ge(acc_act, c["act"] + a)
                        pe.wait_ge(acc_dve, c["dve"] + d)
                        b = 2 * (j % 2)
                        product((FF0 + j) % RING, cols, h_hi, h_lo, range(KT),
                                [acc[:, b + hf, 0:HALF] for hf in range(2)])
                else:
                    pe.wait_ge(hid_lo, (c["down"] + 1) * FG)
                    for j in range(FG):
                        pe.wait_ge(lo_done, c["unit"] + (j + 1))
                        for mj in range(2):
                            m = 2 * j + mj
                            a, d = (0, 2 * (m - 1)) if m else (-first[0], -first[1])
                            pe.wait_ge(acc_act, c["act"] + a)
                            pe.wait_ge(acc_dve, c["dve"] + d)
                            b = 2 * (m % 2)
                            product((FF0 + j) % RING, lambda f: slice(2 * P * f + P * mj, 2 * P * f + P * (mj + 1)),
                                    m_hi, m_lo, [FG * par + f for f in range(FG)],
                                    [acc[:, b + hf, 0:HALF] for hf in range(2)])
            mlp(pe, segment)

            pe.wait_ge(acc_dve, DVE0 + NG * (UPS + 2 * DOWNS))
            for t in range(QT + 1):
                r = rows[t]
                banks = y_banks(t)
                if t == QT:
                    pe.wait_ge(yt_read, 2)
                for m in range(KT):
                    mm = pe.transpose(banks[m // 4][0:r, P * (m % 4):P * (m % 4 + 1)], res[:, m, P * t:P * t + r], ident(P))
                mm.then_inc(yt_pe, 1)


def constants():
    c = np.zeros((P, CONSTS), np.float32)
    s = np.zeros((P, S_CONSTS), np.float32)

    def put(name, a):
        to, where = (c, CONST) if name in CONST else (s, S_CONST)
        at, n = where[name]
        to[:a.shape[0], at:at + n] = a
    i = np.arange(P)[:, None]
    put("ident", np.eye(P))
    j = np.arange(SEQ)[None, :] - (SEQ - P)
    put("dist", np.where(j <= i, j - i, NEG))
    j = np.arange(P)[None, :]
    put("below_neg", np.where(j < i, 0.0, NEG))
    put("upto", i <= j)
    b, hq = i // 32, i % 32
    h, q = hq // NQ, hq % NQ
    slope = np.array(SLOPES + [0.0, 0.0])[h]
    key = np.arange(SK)[None, :]
    new = key - PAST
    rel = new % NQ - q
    for grp in range(2):
        at = np.arange(grp * SK, (grp + 1) * SK)
        own = (new >= 0) & (new // NQ == 4 * grp + b)
        for name, a in (("s_bias", np.where(key < PAST, slope * (new - q), np.where(own & (rel <= 0), slope * rel, NEG))),
                        ("s_neg", np.where((key < PAST) | (own & (rel < 0)), 0.0, NEG))):
            s[:, S_CONST[name][0] + at] = a
    put("mean", np.full((P, P), 1.0 / D_MODEL))
    put("s_head", (np.arange(W_ATT)[None, :] // HD == h))
    bb = np.arange(16)[None, :]
    put("s_pick", (bb // NQ == b) & (bb % NQ == q) & (h < H))
    a, d = np.arange(NS)[:, None], np.arange(NS)[None, :]
    put("s_chunk", (a // NQ == d // NQ) & (a % NQ <= d % NQ))
    return c, s


def split_units(w_in, w_out, w_ff1, w_ff2):
    def columns(w, at, n=P):
        return w[:, at:at + n].reshape(-1, P, n).transpose(1, 0, 2).reshape(P, -1)
    units = []
    for y in range(2):
        for p in range(PAIRS):
            units += [columns(w_in, (3 * y + s) * W_ATT + P * p) for s in range(3)]
    units += [columns(w_in, 6 * W_ATT + P * j) for j in C_TILE]
    units += [columns(w_out, P * m) for m in range(OUT_UNITS)]

    def up(g):
        return [columns(w_ff1, P * (FG * g + j)) for j in range(FG)]

    def down(g):
        rows = w_ff2[P * FG * g:P * FG * (g + 1)]
        return [columns(rows, 2 * P * j, 2 * P) for j in range(FG)]
    units += up(0)
    for g in range(1, NG):
        units += up(g) + down(g - 1)
    return np.stack(units + down(NG - 1))


_OUTS = [("y_prompt", (1, SEQ, D_MODEL)), ("y_sample", (NB, NQ, D_MODEL)),
         ("k_a_prompt", (1, 1, SEQ, H, HD)), ("v_a_prompt", (1, 1, SEQ, H, HD)),
         ("k_b_prompt", (1, 1, SEQ, H, HD)), ("v_b_prompt", (1, 1, SEQ, H, HD)),
         ("k_a_sample", (1, NB, NQ, H, HD)), ("v_a_sample", (1, NB, NQ, H, HD)),
         ("k_b_sample", (1, NB, NQ, H, HD)), ("v_b_sample", (1, NB, NQ, H, HD)),
         ("v_c_sample", (1, NB, NQ, W_C))]


def kernel(x_prompt, x_sample, cache_k_a, cache_v_a, cache_k_b, cache_v_b, page_table, ln_in_g,
           ln_in_b, w_in, w_out, w_spatial, b_spatial, ln_c_g, ln_c_b, ln1_g, ln1_b, w_ff1, w_ff2,
           ln2_g, ln2_b):
    import concourse.bacc as bacc
    from concourse.bass_utils import run_bass_kernel_spmd

    a = {k: np.asarray(v) for k, v in locals().items()
         if k not in ("bacc", "run_bass_kernel_spmd")}
    arrays = {
        "x_prompt": a["x_prompt"], "x_sample": a["x_sample"],
        "weights": split_units(a["w_in"][0], a["w_out"][0], a["w_ff1"][0], a["w_ff2"][0]),
        "cache_k_a": a["cache_k_a"], "cache_v_a": a["cache_v_a"],
        "cache_k_b": a["cache_k_b"], "cache_v_b": a["cache_v_b"],
        "page_table": a["page_table"],
        "ln_cols": np.stack([v.reshape(KT, P).T for v in
                             (a["ln_in_g"], a["ln_in_b"], a["ln1_g"][0], a["ln1_b"][0])], axis=1),
        "w_spatial": a["w_spatial"][0].transpose(2, 0, 1),
        "b_spatial": a["b_spatial"][0],
        "lnc_g": a["ln_c_g"].reshape(1, W_C), "lnc_b": a["ln_c_b"].reshape(1, W_C),
        "ln2_g": a["ln2_g"].reshape(1, D_MODEL), "ln2_b": a["ln2_b"].reshape(1, D_MODEL),
        "consts": constants()[0], "s_consts": constants()[1],
    }
    nc = bacc.Bacc("TRN2", target_bir_lowering=False, num_devices=1)
    args = []
    for name, v in arrays.items():
        arrays[name] = v = np.ascontiguousarray(v)
        args.append(nc.dram_tensor(name, v.shape, mybir.dt.from_np(v.dtype), kind="ExternalInput").ap())
    for name, shape in _OUTS:
        args.append(nc.dram_tensor(name, shape, F32, kind="ExternalOutput").ap())
    hybrid_layer(nc, *args)
    r = run_bass_kernel_spmd(nc, [arrays], core_ids=[0]).results[0]
    return tuple(r[name] for name, _ in _OUTS)
```

```python
from contextlib import ExitStack

import numpy as np

import concourse.bass as bass
from concourse import mybir

ALU = mybir.AluOpType
ACT = mybir.ActivationFunctionType
AX_X = mybir.AxisListType.X
F32 = mybir.dt.float32
F32R = mybir.dt.float32r
I32 = mybir.dt.int32

P = 128
D_MODEL = 1024
KT = D_MODEL // P
SEQ = 512
NB = 8
NQ = 4
NS = NB * NQ
T = SEQ + NS
HALF = T // 2
QT = SEQ // P
HD = 64
H = 6
PAIRS = H // 2
W_ATT = H * HD
GROUPS = 4
W_C = GROUPS * HD
PAST = 256
PAGE = 128
PAGES = PAST // PAGE
CHUNK = 128
D_FF = 4 * D_MODEL
SCALE = HD ** -0.5
ALPHA = 2 ** 0.25
EPS = 1e-5
MOBA_BLOCK = 256
MOBA_TOPK = 3
assert max(SEQ, PAST + NQ) <= 2 * MOBA_BLOCK and MOBA_TOPK >= 2
SLOPES = [0.25, 0.0625, 0.015625, 0.00390625, 0.5, 0.125]
NEG = -1e30
SK = PAST + NS

IN_UNITS = 22
OUT_UNITS = D_MODEL // P
FG = 4
NG = D_FF // (P * FG)
FF_UNITS = 2 * NG * FG
UNITS = IN_UNITS + OUT_UNITS + FF_UNITS
STAGE = 2
RING = 4
ITEMS = 2 * PAIRS * QT * 2
K_RING = 7
X_ORDER = (QT, *range(QT))
C_TILE = (2, 3, 0, 1)

def _pack(*sizes):
    at, out = 0, {}
    for name, cols in sizes:
        out[name] = (at, cols)
        at += cols
    return out, at


CONST, CONSTS = _pack(("ident", P), ("below_neg", P), ("upto", P), ("mean", P))
S_CONST, S_CONSTS = _pack(("s_bias", 2 * SK), ("s_neg", 2 * SK), ("s_head", W_ATT),
                          ("s_pick", 16), ("s_chunk", NS))


def hybrid_layer(nc, x_prompt, x_sample, weights, cache_k_a, cache_v_a, cache_k_b, cache_v_b,
                 page_table, ln_cols, w_spatial, b_spatial, lnc_g, lnc_b, ln2_g, ln2_b, consts, s_consts,
                 y_prompt, y_sample, k_a_prompt, v_a_prompt, k_b_prompt, v_b_prompt,
                 k_a_sample, v_a_sample, k_b_sample, v_b_sample, v_c_sample):
    n_pool = cache_k_a.shape[0]
    key_pages = (cache_k_a, cache_k_b)
    value_pages = [c.rearrange("l n p h d -> (l n) p (h d)") for c in (cache_v_a, cache_v_b)]
    x_rows = [x_prompt[0, t * P:(t + 1) * P, :] for t in range(QT)]
    x_rows.append(x_sample.rearrange("b t d -> (b t) d"))
    kv_prompt = [[o.rearrange("l b (t p) h d -> p (l b t) (h d)", p=P) for o in kv]
                 for kv in ((k_a_prompt, v_a_prompt), (k_b_prompt, v_b_prompt))]
    kv_sample = [[o.rearrange("l b t h d -> (l b t) (h d)") for o in kv]
                 for kv in ((k_a_sample, v_a_sample), (k_b_sample, v_b_sample))]
    rows = [P] * QT + [NS]

    with ExitStack() as ctx:
        def sb(name, shape, dt=F32, to=None):
            return (to or ctx).enter_context(nc.sbuf_tensor(name, shape, dt))

        def sem(name):
            return ctx.enter_context(nc.semaphore(name))

        cst = sb("cst", [P, CONSTS])
        h_hi = sb("h_hi", [P, KT, T], F32R)
        h_lo = sb("h_lo", [P, KT, T], F32R)
        m_hi = sb("m_hi", [P, KT, T], F32R)
        m_lo = sb("m_lo", [P, KT, T], F32R)
        w_raw = sb("w_raw", [P, STAGE, KT * P])
        w_hi = sb("w_hi", [P, RING, KT * P], F32R)
        w_lo = sb("w_lo", [P, RING, KT * P], F32R)
        lnp = sb("lnp", [P, 4, KT])
        eps = sb("eps", [P, 1])
        warm = sb("warm", [P, 1])
        qbd = [sb(f"qbd{y}", [P, NB, PAIRS, 32]) for y in range(2)]
        dist_r = sb("dist_r", [P, SEQ], F32R)
        sid_r = sb("sid_r", [P, H, P], F32R)
        id_r = sb("id_r", [P, P], F32R)
        below_r = sb("below_r", [P, P], F32R)

        early = ExitStack()
        s_cst = sb("s_cst", [P, S_CONSTS], to=early)
        sb_r = sb("sb_r", [P, 4, SK], F32R, to=early)
        k_t0 = sb("k_t0", [P, 2, PAGES, PAIRS, PAGE], to=early)
        ptab = sb("ptab", [1, NB * PAGES], I32, to=early)
        early.close()
        res = sb("res", [P, KT, T])

        ph = ExitStack()
        xin = sb("xin", [P, QT + 1, D_MODEL], to=ph)
        x_n = sb("x_n", [P, KT, T], to=ph)
        dist = sb("dist", [P, SEQ], to=ph)
        x_st = sb("x_st", [P, QT + 1, 12], to=ph)
        x_mv = sb("x_mv", [P, QT + 1, 2], to=ph)
        x_sd = sb("x_sd", [P, QT + 1], to=ph)
        x_rs = sb("x_rs", [P, QT + 1], to=ph)
        x_sh = sb("x_sh", [P, QT + 1], to=ph)
        ph.close()

        after_x = ExitStack()
        z_c = sb("z_c", [P, 4, T], to=after_x)
        k_new = [sb(f"k_new{y}", [P, PAIRS, NS], to=after_x) for y in range(2)]
        kv_new = [sb(f"kv_new{y}", [NS, 2, W_ATT], to=after_x) for y in range(2)]

        pr = ExitStack()
        k_tok = [sb(f"k_tok{j}", [P, QT, P], to=pr) for j in range(2)]
        v_tok = [sb(f"v_tok{j}", [P, QT, P], to=pr) for j in range(2)]
        keep = sb("keep", [P, 2, SEQ], to=pr)
        left = sb("left", [P, 2, SEQ], to=pr)
        prob = sb("prob", [P, 3, SEQ], to=pr)
        prob_t = [sb(f"prob_t{h}", [P, QT * (QT + 1) // 2, P], to=pr) for h in range(2)]
        mx = sb("mx", [P, 2], to=pr)
        nmx = sb("nmx", [P, 2], to=pr)
        rsum = sb("rsum", [P, 2], to=pr)
        rinv = sb("rinv", [P, 2], to=pr)
        z_q, z_kv = [], []
        for j in range(2):
            z_q.append(sb(f"z_q{j}", [P, 2, T], to=pr))
            z_kv.append(sb(f"z_kv{j}", [P, 2, T], to=pr))
        pr.close()

        sa = ExitStack()
        vt = sb("vt", [P, QT + 1, W_C], to=sa)
        vsq = sb("vsq", [P, QT + 1, W_C], to=sa)
        v_s = sb("v_s", [P, 4, (QT + 1) * GROUPS], to=sa)
        lnc = sb("lnc", [P, 2, W_C], to=sa)
        wsp = sb("wsp", [P, GROUPS, CHUNK], to=sa)
        wbd = sb("wbd", [NS, GROUPS, NS], to=sa)
        bsp = sb("bsp", [P, 2, CHUNK], to=sa)
        v_pg = sb("v_pg", [P, 4, PAGES, W_ATT], to=sa)
        sw = [sb(f"sw{j}", [P, SK], to=sa) for j in range(2)]
        s_prob = sb("s_prob", [P, SK], to=sa)
        s_pt = sb("s_pt", [P, 3, P], to=sa)
        s_om = sb("s_om", [P, W_ATT], to=sa)
        s_st = sb("s_st", [P, 8], to=sa)
        k_t = sb("k_t", [P, K_RING - 2, PAGES, PAIRS, PAGE], to=sa)
        sa.close()
        after_x.close()

        ff = ExitStack()
        mean_b = sb("mean_b", [P, T], to=ff)
        sd_b = sb("sd_b", [P, T], to=ff)
        rstd_b = sb("rstd_b", [P, T], to=ff)
        sq = sb("sq", [P, KT, HALF], to=ff)
        r_sum = sb("r_sum", [P, T], to=ff)
        sq_sum = sb("sq_sum", [P, T], to=ff)
        relu = sb("relu", [P, FG, T], to=ff)
        hid = sb("hid", [P, 2, T], to=ff)
        wo = ExitStack()
        wo_hi = sb("wo_hi", [P, OUT_UNITS - RING, KT * P], F32R, to=wo)
        wo_lo = sb("wo_lo", [P, OUT_UNITS - RING, KT * P], F32R, to=wo)
        wo.close()
        ln2 = sb("ln2", [P, 2, D_MODEL], to=ff)
        y_n = sb("y_n", [P, QT + 1, D_MODEL], to=ff)
        y_st = sb("y_st", [P, QT + 1, 12], to=ff)
        y_mv = sb("y_mv", [P, QT + 1, 2], to=ff)
        y_sd = sb("y_sd", [P, QT + 1], to=ff)
        y_rs = sb("y_rs", [P, QT + 1], to=ff)
        y_sh = sb("y_sh", [P, QT + 1], to=ff)
        ff.close()

        acc = ctx.enter_context(nc.psum_tensor("acc", [P, 4, 512], F32))
        s_bank = [ctx.enter_context(nc.psum_tensor(f"s_bank{j}", [P, 512], F32)) for j in range(2)]
        t_bank = ctx.enter_context(nc.psum_tensor("t_bank", [P, 512], F32))
        o_bank = ctx.enter_context(nc.psum_tensor("o_bank", [P, 512], F32))

        def c_(name, r=P, lo=0, hi=None):
            where, t = (CONST, cst) if name in CONST else (S_CONST, s_cst)
            at, n = where[name]
            return t[0:r, at + lo:at + (n if hi is None else hi)]

        def ident(r):
            return c_("ident", r, 0, r)

        x_loaded = [sem(f"x_loaded{t}") for t in range(QT + 1)]
        const_loaded = sem("const_loaded")
        x_rec, xn_even, xn_odd, hi_even, hi_odd, h_even, h_odd = (
            sem(n) for n in ("x_rec", "xn_even", "xn_odd", "hi_even", "hi_odd", "h_even", "h_odd"))
        const2_loaded, s_const_loaded = sem("const2_loaded"), sem("s_const_loaded")
        bias_ready, sb_ready = sem("bias_ready"), sem("sb_ready")
        vt_zero, wbd_zero, max_ready, s_scaled, stream = (sem(n) for n in ("vt_zero", "wbd_zero", "max_ready", "s_scaled", "stream"))
        w_loaded = [sem(f"w_loaded{j}") for j in range(STAGE)]
        hi_done, lo_done = sem("hi_done"), sem("lo_done")
        half_done = sem("half_done")
        acc_act, acc_dve = sem("acc_act"), sem("acc_dve")
        x_stat, x_std, x_norm, x_norm_dve = (sem(n) for n in ("x_stat", "x_std", "x_norm", "x_norm_dve"))
        xt_ready, res_ready, hhi_ready, h_ready = sem("xt_ready"), sem("res_ready"), sem("hhi_ready"), sem("h_ready")
        init = sem("init")
        z_copied, q_copied = sem("z_copied"), sem("q_copied")
        kv_t, kv_act, kv_dve = sem("kv_t"), sem("kv_act"), sem("kv_dve")
        kv_out = [sem(f"kv_out{y}") for y in range(2)]
        s_ready, s_read = sem("s_ready"), sem("s_read")
        st1, st2, st3, st4 = sem("st1"), sem("st2"), sem("st3"), sem("st4")
        softplus_e, softplus = sem("softplus_e"), sem("softplus")
        d1, d2, d3, d4, d5 = sem("d1"), sem("d2"), sem("d3"), sem("d4"), sem("d5")
        p_written, p_scaled, p_sum = sem("p_written"), sem("p_scaled"), sem("p_sum")
        pt_ready, pt_read = sem("pt_ready"), sem("pt_read")
        o_ready, mhi_ready, m_ready = sem("o_ready"), sem("mhi_ready"), sem("m_ready")
        gelu_done, vt_ready, vt_read, v_chain, v_sq = sem("gelu_done"), sem("vt_ready"), sem("vt_read"), sem("v_chain"), sem("v_sq")
        mix_ready, mix_dve, mix_hi, mix_lo = sem("mix_ready"), sem("mix_dve"), sem("mix_hi"), sem("mix_lo")
        wsp_ready, g_loaded = sem("wsp_ready"), sem("g_loaded")
        pt_loaded = sem("pt_loaded")
        kp_loaded = [sem(f"kp_loaded{j}") for j in range(K_RING)]
        vp_loaded = [sem(f"vp_loaded{j}") for j in range(4)]
        kt_pe, kt_act, kt_dve, sc_pe = sem("kt_pe"), sem("kt_act"), sem("kt_dve"), sem("sc_pe")
        tail_done = sem("tail_done")
        ss_read, e1, e2, e3, sp_written = sem("ss_read"), sem("e1"), sem("e2"), sem("e3"), sem("sp_written")
        st_pe, st_act, pv_pe, om_done, ot_pe, ot_hi, ot_lo = (sem(n) for n in ("st_pe", "st_act", "pv_pe", "om_done", "ot_pe", "ot_hi", "ot_lo"))
        r_ready, mean_pe, mean_sb, cent, sq_done, sq_pe, std_done, rstd_done = (sem(n) for n in ("r_ready", "mean_pe", "mean_sb", "cent", "sq_done", "sq_pe", "std_done", "rstd_done"))
        nrm, r_sums, sq_sums, h1_hi, h1_lo, res_a = (sem(n) for n in ("nrm", "r_sums", "sq_sums", "h1_hi", "h1_lo", "res_a"))
        relu_act, relu_dve, sq_h, hid_hi, hid_lo = (sem(n) for n in ("relu_act", "relu_dve", "sq_h", "hid_hi", "hid_lo"))
        yt_pe, yt_read, y_c, y_std, y_nrm, y_g, y_b, ln2_loaded = (sem(n) for n in ("yt_pe", "yt_read", "y_c", "y_std", "y_nrm", "y_g", "y_b", "ln2_loaded"))
        y_out, y_b2, head_sq, head_hi = sem("y_out"), sem("y_b2"), sem("head_sq"), sem("head_hi")
        out_s = sem("out_s")
        d0, e4, y_rec = sem("d0"), sem("e4"), sem("y_rec")

        def x_rows_sb(t):
            return xin[0:rows[t], t, :]

        def xt_banks(k):
            a, b = ((acc[:, 2, :], acc[:, 3, :]), (t_bank[:, :], o_bank[:, :]))[k % 2]
            return a[:, 0:SEQ], b[:, 0:NS]

        def out_bank(q):
            return acc[:, (q + 2) % 4, 0:HALF]

        def item(n):
            i, s = divmod(n, 8)
            return i, s, s // 2, s % 2, P * (s // 2 + 1)

        def pt_bank(n):
            return t_bank[:, :] if n % 2 == 0 else acc[:, 2, :]

        def y_banks(t):
            return ((s_bank[0][:, :], s_bank[1][:, :]), (t_bank[:, :], o_bank[:, :]),
                    (acc[:, 0, :], acc[:, 1, :]), (acc[:, 2, :], acc[:, 3, :]))[t % 4]

        def keys_of(n):
            return k_t0[:, n % K_RING] if n % K_RING < 2 else k_t[:, n % K_RING - 2]

        def halves(hf):
            return slice(HALF * hf, HALF * (hf + 1))

        block = ctx.enter_context(nc.Block())

        MLP_HEAD = [("up", 0), ("up", 1), ("down", 0)]
        MLP_BODY = [("up", 2), ("down", 1), ("up", 3), ("down", 2)]
        MLP_ROUNDS = (NG - 2) // 2
        MLP_TAIL = [("last", NG - 1)]
        UPS, DOWNS = FG, KT
        FF0 = IN_UNITS + OUT_UNITS

        def act_reads(n):
            return min(n, IN_UNITS)

        def dve_reads(n):
            return min(n, IN_UNITS) + 2 * max(0, n - IN_UNITS)

        OUT_ORDER = [(0, m) for m in range(RING)] + [(1, 0)] + [(0, m) for m in range(RING, KT)] \
            + [(1, m) for m in range(1, KT)]
        ACT0, DVE0 = act_reads(FF0), dve_reads(FF0)
        DVE_END = DVE0 + NG * (UPS + 2 * DOWNS)

        def mlp(eng, segment):
            up = {"unit": FG, "tile": UPS, "act": UPS, "dve": UPS, "up": 1, "down": 0}
            down = {"unit": FG, "tile": DOWNS, "act": 0, "dve": 2 * DOWNS, "up": 0, "down": 1}
            before = [None]

            def run(c, segments):
                for kind, g in segments:
                    segment(kind, g % 2, before[0], c)
                    before[0] = kind
                    c = {k: c[k] + (up if kind == "up" else down)[k] for k in c}
                return c

            c = run({"unit": FF0, "tile": FF0, "act": ACT0, "dve": DVE0, "up": 0, "down": 0}, MLP_HEAD)
            with eng.Fori(0, MLP_ROUNDS) as i:
                run({k: i * (2 * up[k] + 2 * down[k]) + c[k] for k in c}, MLP_BODY)
            run({k: c[k] + MLP_ROUNDS * (2 * up[k] + 2 * down[k]) for k in c}, MLP_TAIL)

        @block.sync
        def _(sp):
            at, n = CONST["ident"]
            for t in X_ORDER[:2]:
                sp.dma_start(x_rows_sb(t), x_rows[t]).then_inc(x_loaded[t], 16)
            sp.dma_start(cst[:, at:at + n], consts[:, at:at + n]).then_inc(const_loaded, 16)
            sp.dma_start(lnp[:, :, :], ln_cols).then_inc(const_loaded, 16)
            for t in X_ORDER[2:]:
                sp.dma_start(x_rows_sb(t), x_rows[t]).then_inc(x_loaded[t], 16)

            def load_unit(u, slot, count):
                if count is not None:
                    sp.wait_ge(lo_done, count)
                sp.dma_start(w_raw[:, slot, :], weights[u]).then_inc(w_loaded[slot], 16)

            def load_first(u):
                load_unit(u, u % STAGE, u - STAGE + 1 if u >= STAGE else None)

            def load_keys(n):
                y, b = divmod(n, NB)
                for pg in range(PAGES):
                    sp.dma_start(keys_of(n)[:, pg], key_pages[y][pages[PAGES * b + pg]]).then_inc(kp_loaded[n % K_RING], 16)

            for u in range(STAGE):
                load_first(u)
            sp.dma_start(cst[:, at + n:CONSTS], consts[:, at + n:CONSTS]).then_inc(const2_loaded, 16)
            sp.dma_start(dist[:, :], consts[:, CONSTS:CONSTS + SEQ]).then_inc(const2_loaded, 16)
            sp.dma_start(ptab[:, :], page_table.rearrange("(a b) p -> a (b p)", a=1)).then_inc(pt_loaded, 16)
            for u in range(STAGE, 8):
                load_first(u)
            sp.dma_start(s_cst[:, :], s_consts).then_inc(s_const_loaded, 16)
            sp.wait_ge(pt_loaded, 16)
            pages = [sp.value_load(ptab[0:1, n:n + 1], min_val=0, max_val=n_pool - 1)
                     for n in range(NB * PAGES)]
            for n in range(2):
                load_keys(n)
            for u in range(8, IN_UNITS + 1):
                load_first(u)
            sp.wait_ge(p_written, 8 * (2 * PAIRS - 1))
            sp.wait_ge(kv_t, 3 * (2 * PAIRS - 1))
            sp.wait_ge(z_copied, 2 * PAIRS - 1)
            for n in range(2, 4):
                load_keys(n)
            for u in range(IN_UNITS + 1, IN_UNITS + RING):
                load_first(u)

            sp.wait_ge(p_written, ITEMS)
            sp.wait_ge(kv_t, 3 * 2 * PAIRS)
            sp.wait_ge(z_copied, 2 * PAIRS)
            for n in range(4, K_RING):
                load_keys(n)
            sp.wait_ge(m_ready, 6)
            sp.wait_ge(kv_out[0], 16 * 6)
            sp.wait_ge(kv_out[1], 16 * 6)
            loaded = K_RING
            for gi in range(4):
                y, grp = divmod(gi, 2)
                if gi:
                    sp.wait_ge(pv_pe, gi)
                for b4 in range(4):
                    for pg in range(PAGES):
                        src = value_pages[y][pages[PAGES * (4 * grp + b4) + pg]]
                        sp.dma_start(v_pg[:, b4, pg, :], src).then_inc(vp_loaded[b4], 16)
                ahead = min(2 * NB, 4 * gi + 12)
                for n in range(loaded, ahead):
                    if n >= K_RING:
                        sp.wait_ge(sc_pe, (n - K_RING) // 4 + 1)
                    load_keys(n)
                loaded = max(loaded, ahead)
            for u in range(IN_UNITS + RING, FF0):
                load_first(u)

            def segment(kind, par, prev, c):
                for j in range(FG):
                    load_unit(c["unit"] + j, (FF0 + j) % STAGE, c["unit"] + (j - STAGE + 1))
            mlp(sp, segment)
            for j, row in enumerate((ln2_g, ln2_b)):
                sp.dma_start(ln2[:, j, :], row.to_broadcast([P, D_MODEL])).then_inc(ln2_loaded, 16)
            for t in range(QT + 1):
                dst = y_prompt[0, P * t:P * (t + 1), :] if t < QT else y_sample.rearrange("b t d -> (b t) d")
                for j, done in ((1, y_b2), (0, y_b)):
                    sp.wait_ge(done, t + 1)
                    sp.dma_start(dst[:, 512 * j:512 * (j + 1)],
                                 y_n[0:rows[t], t, 512 * j:512 * (j + 1)]).then_inc(y_out, 16)
            sp.wait_ge(y_out, 16 * 2 * (QT + 1))
            for j in range(2):
                sp.wait_ge(kv_out[j], 16 * 6)
            sp.wait_ge(out_s, 16 * 5)

        @block.gpsimd
        def _(pool):
            def lo_part(slot, stage, u):
                pool.wait_ge(hi_done, u + 1)
                pool.tensor_tensor(w_lo[:, slot, :], w_raw[:, stage, :],
                                   w_hi[:, slot, :].bitcast(F32), ALU.subtract).then_inc(lo_done, 1)

            pool.memset(eps[:, :], EPS).then_inc(init, 1)
            for j in range(2):
                pool.memset(z_q[j][:, :, :], 0.0).then_inc(init, 1)
            for y in range(2):
                pool.memset(qbd[y][:, :, :, :], 0.0).then_inc(init, 1)
            lo_part(0, 0, 0)
            for k in range(0, KT, 2):
                pool.wait_ge(hi_even, k // 2 + 1)
                pool.tensor_tensor(h_lo[:, k, :], x_n[:, k, :], h_hi[:, k, :].bitcast(F32),
                                   ALU.subtract).then_inc(h_even, 1)
                if k == 0:
                    lo_part(1, 1 % STAGE, 1)
            lo_part(2, 2 % STAGE, 2)
            pool.wait_ge(const2_loaded, 32)
            pool.tensor_copy(dist_r[:, :], dist[:, :]).then_inc(bias_ready, 1)
            for h in range(H):
                pool.tensor_scalar(sid_r[:, h, :], c_("ident"), SLOPES[h], None, ALU.mult).then_inc(bias_ready, 1)
            lo_part(3, 3 % STAGE, 3)
            pool.tensor_copy(id_r[:, :], c_("ident")).then_inc(bias_ready, 1)
            pool.tensor_copy(below_r[:, :], c_("below_neg")).then_inc(bias_ready, 1)

            def keep_samples(i):
                y, p = divmod(i, PAIRS)
                pool.wait_ge(acc_act, 3 * i + 3)
                pool.wait_ge(acc_dve, 3 * i + 3)
                for h in range(2):
                    r = slice(HD * h, HD * (h + 1))
                    pool.tensor_copy(qbd[y][r, :, p, 8 * p + NQ * h:8 * p + NQ * (h + 1)],
                                     z_q[i % 2][r, h, SEQ:T].rearrange("d (b q) -> d b q", q=NQ)).then_inc(q_copied, 1)
                    pool.wait_ge(q_copied, 2 * i + h + 1)
                pool.tensor_copy(k_new[y][:, p, :], z_kv[i % 2][:, 0, SEQ:T]).then_inc(z_copied, 1)

            for u in range(4, IN_UNITS + RING):
                lo_part(u % RING, u % STAGE, u)
                if u in (10, 12):
                    pool.wait_ge(s_const_loaded, 16)
                    a = 2 * ((u - 10) // 2)
                    pool.tensor_copy(sb_r[:, a:a + 2, :],
                                     c_("s_bias" if a == 0 else "s_neg").rearrange("p (g k) -> p g k", k=SK)).then_inc(sb_ready, 1)
                if u >= 7 and (u - 7) % 3 == 0 and (u - 7) // 3 < 6:
                    pool.wait_ge(lo_done, u + 1)
                    keep_samples((u - 7) // 3)
            pool.wait_ge(m_ready, 6)
            pool.wait_ge(kv_out[0], 16 * 6)
            pool.wait_ge(kv_out[1], 16 * 6)
            for j, row in enumerate((lnc_g, lnc_b)):
                pool.dma_start(lnc[:, j, :], row.to_broadcast([P, W_C])).then_inc(g_loaded, 16)
            pool.dma_start(wsp[:, :, :], w_spatial).then_inc(g_loaded, 16)
            for g in range(GROUPS):
                j, g2 = divmod(g, 2)
                pool.dma_start(bsp[HD * g2:HD * (g2 + 1), j, :],
                               b_spatial[g:g + 1, :].to_broadcast([HD, CHUNK])).then_inc(g_loaded, 16)
            pool.wait_ge(wbd_zero, 1)
            for b in range(NB):
                pool.dma_start(wbd[NQ * b:NQ * (b + 1), :, NQ * b:NQ * (b + 1)],
                               w_spatial[0:NQ, :, 0:NQ]).then_inc(g_loaded, 16)
            pool.wait_ge(g_loaded, 16 * (3 + GROUPS + NB))
            for g in range(GROUPS):
                pool.tensor_tensor(wsp[:, g, :], wsp[:, g, :], c_("upto"), ALU.mult).then_inc(wsp_ready, 1)
                pool.tensor_tensor(wbd[:, g, :], wbd[:, g, :], c_("s_chunk", NS), ALU.mult).then_inc(wsp_ready, 1)
            for u in range(IN_UNITS + RING, FF0):
                pool.wait_ge(hi_done, u + 1)
                pool.tensor_tensor(wo_lo[:, u - IN_UNITS - RING, :], w_raw[:, u % STAGE, :],
                                   wo_hi[:, u - IN_UNITS - RING, :].bitcast(F32), ALU.subtract).then_inc(lo_done, 1)
            for u in range(FF0, FF0 + RING):
                lo_part(u % RING, u % STAGE, u)
            pool.wait_ge(h1_lo, 2 * KT)
            for k in range(KT):
                pool.tensor_scalar(res[:, k, :], res[:, k, :], lnp[:, 3, k:k + 1], ALPHA, ALU.add,
                                   ALU.mult).then_inc(res_a, 1)

            first = [True]

            def segment(kind, par, prev, c):
                if first[0]:
                    first[0] = False
                    return
                for j in range(FG):
                    lo_part((FF0 + j) % RING, (FF0 + j) % STAGE, c["unit"] + j)
            mlp(pool, segment)

            pool.wait_ge(ln2_loaded, 32)
            for t in range(QT + 1):
                r = rows[t]
                pool.wait_ge(yt_read, 2 * t + 2)
                pool.tensor_tensor(y_n[0:r, t, 0:512], y_n[0:r, t, 0:512], ln2[0:r, 0, 0:512], ALU.mult).then_inc(y_g, 1)
                pool.wait_ge(y_g, t + 1)
                pool.tensor_tensor(y_n[0:r, t, 0:512], y_n[0:r, t, 0:512], ln2[0:r, 1, 0:512], ALU.add).then_inc(y_b, 1)

        @block.scalar
        def _(act):
            def hi_part(slot, stage, u, used, loaded):
                if used is not None:
                    act.wait_ge(half_done, used)
                act.wait_ge(w_loaded[stage], loaded)
                act.activation(w_hi[:, slot, :], w_raw[:, stage, :], ACT.Copy).then_inc(hi_done, 1)

            def hi_unit(u):
                hi_part(u % RING, u % STAGE, u, 2 * (u - RING + 1) if u >= RING else None, 16 * (u // STAGE + 1))

            act.wait_ge(init, 1)
            act.activation(warm[:, :], eps[:, :], ACT.Sqrt)
            for o in range(QT + 2):
                if o <= QT:
                    t = X_ORDER[o]
                    r = rows[t]
                    act.wait_ge(x_stat, 3 * (o + 1))
                    act.activation(x_sd[0:r, t:t + 1], x_mv[0:r, t, 1:2], ACT.Sqrt, bias=eps[0:r, 0:1]).then_inc(x_std, 1)
                if o == QT + 1:
                    hi_unit(0)
                elif o:
                    t = X_ORDER[o - 1]
                    r = rows[t]
                    act.wait_ge(x_rec, 2 * o)
                    act.activation(xin[0:r, t, :], xin[0:r, t, :], ACT.Identity, bias=x_sh[0:r, t:t + 1],
                                   scale=x_rs[0:r, t:t + 1]).then_inc(x_norm, 1)
            act.wait_ge(const_loaded, 32)
            for k in range(1, KT, 2):
                act.wait_ge(xt_ready, k + 1)
                for dst, src in zip((slice(0, SEQ), slice(SEQ, T)), xt_banks(k)):
                    act.activation(x_n[:, k, dst], src, ACT.Identity, bias=lnp[:, 1, k:k + 1],
                                   scale=lnp[:, 0, k:k + 1]).then_inc(xn_odd, 1)
                act.wait_ge(xn_odd, k + 1)
                act.activation(h_hi[:, k, :], x_n[:, k, :], ACT.Copy).then_inc(hi_odd, 1)
                if k == 1:
                    hi_unit(1)
            hi_unit(2)
            hi_unit(3)
            act.wait_ge(init, 5)

            def read_half(u):
                i, j = divmod(u, 3)
                act.wait_ge(half_done, 2 * u + 1)
                src, scale = acc[:, 0, 0:HALF], 1.0
                if u >= 18:
                    act.activation(z_c[:, C_TILE[u - 18], 0:HALF], src, ACT.Copy).then_inc(acc_act, 1)
                    return
                if i >= 2 and j == 0:
                    act.wait_ge(z_copied, i - 1)
                if j == 0:
                    for h in range(2):
                        r = slice(HD * h, HD * (h + 1))
                        op = act.activation(z_q[i % 2][r, h, 0:HALF], acc[r, 0, 0:HALF], ACT.Copy, scale=SCALE)
                    op.then_inc(acc_act, 1)
                else:
                    act.activation(z_kv[i % 2][:, j - 1, 0:HALF], src, ACT.Copy).then_inc(acc_act, 1)

            for u in range(3):
                read_half(u)
                hi_unit(u + RING)

            def probs(n):
                i, s, t, h, L = item(n)
                b = n % 2
                if i < PAIRS:
                    act.wait_ge(max_ready, n + 1)
                else:
                    act.wait_ge(s_ready, n + 1)
                    act.wait_ge(p_scaled, n - 1)
                    act.activation(keep[:, b, 0:L], s_bank[b][:, 0:L], ACT.Sigmoid, scale=-1.0)
                if n >= 3:
                    act.wait_ge(pt_ready, n - 2)
                if i < PAIRS:
                    act.activation(prob[:, n % 3, 0:L], s_bank[b][:, 0:L], ACT.Exp, bias=nmx[:, b:b + 1],
                                   accum_out=rsum[:, b:b + 1]).then_inc(p_written, 1)
                else:
                    act.activation(prob[:, n % 3, 0:L], s_bank[b][:, 0:L], ACT.Sigmoid).then_inc(p_written, 1)

            def keep_turned(n):
                i, s, t, h, L = item(n)
                act.wait_ge(pt_ready, n + 1)
                act.activation(prob_t[h][:, t * (t + 1) // 2:(t + 1) * (t + 2) // 2, :],
                               pt_bank(n)[:, 0:L].rearrange("p (k q) -> p k q", q=P), ACT.Copy).then_inc(pt_read, 1)

            for n in range(ITEMS + 4):
                i, s = divmod(n, 8)
                if n < ITEMS:
                    probs(n)
                if n < ITEMS and s < 2:
                    act.wait_ge(kv_t, 3 * i + s + 1)
                    if i >= 2:
                        act.wait_ge(kv_out[i % 2], 32 * (i // 2))
                    y, p = divmod(i, PAIRS)
                    dst = (k_tok, v_tok)[s][i % 2]
                    act.activation(dst[:, :, :], acc[:, 3, :], ACT.Copy).then_inc(kv_act, 1)
                    act.wait_ge(kv_act, 2 * i + s + 1)
                    act.dma_start(kv_prompt[y][s][:, :, P * p:P * (p + 1)], dst[:, :, :]).then_inc(kv_out[i % 2], 16)
                if 2 <= n < ITEMS + 2:
                    keep_turned(n - 2)
                if i >= 1 and s == 3:
                    act.wait_ge(o_ready, 4 * i)
                    act.activation(m_hi[:, i - 1, 0:SEQ], o_bank[:, :], ACT.Copy).then_inc(mhi_ready, 1)
                if n == ITEMS + 1:
                    act.wait_ge(acc_act, 20)
                    act.wait_ge(acc_dve, 20)
                    act.activation(z_c[:, 2:4, :], z_c[:, 2:4, :], ACT.Gelu_apprx_tanh).then_inc(gelu_done, 1)
                if n < ITEMS:
                    if s in (1, 3, 6):
                        read_half(3 * (i + 1) + (1, 3, 6).index(s))
                    if s in (2, 5, 7):
                        u = 3 * (i + 1) + (2, 5, 7).index(s)
                        hi_unit(u + RING)
            read_half(21)
            hi_unit(21 + RING)

            def s_softmax(g):
                if g:
                    act.wait_ge(st_pe, g)
                if g < 2:
                    act.wait_ge(e2, g + 1)
                    act.activation(s_prob[:, :], t_bank[:, 0:SK], ACT.Exp, bias=s_st[:, 4 * g + 1:4 * g + 2],
                                   accum_out=s_st[:, 4 * g + 2:4 * g + 3]).then_inc(sp_written, 1)
                else:
                    act.wait_ge(sc_pe, g + 1)
                    act.wait_ge(s_scaled, g)
                    act.activation(sw[0][:, :], t_bank[:, 0:SK], ACT.Sigmoid, scale=-1.0)
                    act.activation(s_prob[:, :], t_bank[:, 0:SK], ACT.Sigmoid).then_inc(sp_written, 1)

            act.wait_ge(m_ready, 6)
            act.wait_ge(vt_zero, 1)
            act.wait_ge(vt_ready, 1)
            for j in range(2):
                act.activation(vt[:, 2 * j:2 * j + 2, :], acc[:, j, :], ACT.Copy).then_inc(vt_read, 1)
            act.wait_ge(vt_ready, 2)
            act.activation(vt[0:NS, QT, :], acc[0:NS, 0, 0:W_C], ACT.Copy).then_inc(vt_read, 1)
            act.wait_ge(acc_act, IN_UNITS)
            act.wait_ge(acc_dve, IN_UNITS)
            act.activation(z_c[:, 0:2, :], z_c[:, 0:2, :], ACT.Gelu_apprx_tanh).then_inc(gelu_done, 1)
            s_softmax(0)
            act.wait_ge(v_chain, 3)
            act.activation(vsq[:, :, :], vt[:, :, :], ACT.Square).then_inc(v_sq, 1)
            act.wait_ge(v_chain, 4)
            act.activation(v_s[:, 2, :], v_s[:, 1, :], ACT.Sqrt, bias=eps[:, 0:1], scale=1.0 / HD).then_inc(v_sq, 1)

            for gi in range(1, 5):
                g = gi - 1
                y, grp = divmod(g, 2)
                act.wait_ge(st_pe, g + 1)
                act.activation(s_pt[:, 0:2, :], o_bank[:, 0:2 * P], ACT.Copy).then_inc(st_act, 1)
                act.activation(s_pt[0:NS, 2, :], o_bank[0:NS, 2 * P:3 * P], ACT.Copy).then_inc(st_act, 1)
                if gi == 4:
                    act.wait_ge(v_chain, 8)
                    act.dma_start(v_c_sample.rearrange("l b t c -> (l b t) c"), vt[0:NS, QT, :]).then_inc(out_s, 16)
                    act.wait_ge(s_read, 6)
                    for yy in range(2):
                        for w in range(2):
                            act.dma_start(kv_sample[yy][w], kv_new[yy][:, w, :]).then_inc(out_s, 16)
                if g < 3:
                    s_softmax(g + 1)
                if g == 2:
                    act.wait_ge(mix_dve, 4)
                    act.activation(m_hi[:, 6:8, 0:SEQ], z_c[:, 0:2, 0:SEQ], ACT.Copy).then_inc(mix_hi, 1)
                act.wait_ge(ot_pe, g + 1)
                act.activation(m_hi[:, 3 * y:3 * y + 3, SEQ + 16 * grp:SEQ + 16 * (grp + 1)],
                               s_bank[1][:, 0:48].rearrange("p (t c) -> p t c", c=16), ACT.Copy).then_inc(ot_hi, 1)
                if gi == 3:
                    act.wait_ge(mix_dve, 8)
                    act.activation(m_hi[:, 6:8, SEQ:T], z_c[:, 0:2, SEQ:T], ACT.Copy).then_inc(mix_hi, 1)

            act.wait_ge(ot_lo, 4)
            act.wait_ge(mix_lo, 2)
            act.wait_ge(out_s, 16 * 5)
            for u in range(IN_UNITS + RING, FF0):
                act.wait_ge(w_loaded[u % STAGE], 16 * (u // STAGE + 1))
                act.activation(wo_hi[:, u - IN_UNITS - RING, :], w_raw[:, u % STAGE, :], ACT.Copy).then_inc(hi_done, 1)

            def hi_ff(j):
                u = FF0 + j
                hi_part(u % RING, u % STAGE, u, 2 * IN_UNITS + OUT_ORDER.index((1, j)) + 1, 16 * (u // STAGE + 1))

            def relu_half(j, c):
                act.wait_ge(half_done, 2 * c["tile"] + j + 1)
                act.activation(relu[:, j, 0:HALF], acc[:, 2 * (j % 2), 0:HALF], ACT.Relu).then_inc(acc_act, 1)

            def mean_copy(hf):
                act.wait_ge(mean_pe, hf + 1)
                act.activation(mean_b[:, halves(hf)], s_bank[hf][:, 0:HALF], ACT.Copy).then_inc(mean_sb, 1)

            def squares(hf):
                for k in range(KT):
                    act.wait_ge(cent, KT * hf + k + 1)
                    if hf:
                        act.wait_ge(sq_sums, KT - 1)
                    act.activation(sq[:, k, :], res[:, k, halves(hf)], ACT.Square).then_inc(sq_done, 1)

            def std(hf):
                act.wait_ge(sq_pe, hf + 1)
                act.activation(sd_b[:, halves(hf)], (t_bank, o_bank)[hf][:, 0:HALF], ACT.Sqrt,
                               bias=eps[:, 0:1]).then_inc(std_done, 1)

            def affine(hf):
                for k in range(KT):
                    act.wait_ge(nrm, KT * hf + k + 1)
                    act.activation(h_hi[:, k, halves(hf)], res[:, k, halves(hf)], ACT.Identity,
                                   bias=lnp[:, 3, k:k + 1]).then_inc(h1_hi, 1)

            mean_copy(0)
            squares(0)
            std(0)
            hi_ff(0)
            hi_ff(1)
            affine(0)
            hi_ff(2)
            hi_ff(3)

            def segment(kind, par, prev, c):
                if prev is None:
                    mean_copy(1)
                    relu_half(0, c)
                    squares(1)
                    relu_half(1, c)
                    std(1)
                    relu_half(2, c)
                    affine(1)
                    relu_half(3, c)
                for j in range(FG):
                    if kind == "up" and prev is not None:
                        act.wait_ge(half_done, (c["tile"] + j) * 2 + 1)
                        act.wait_ge(sq_h, c["up"] * FG + (j - 3))
                        act.activation(relu[:, j, 0:HALF], acc[:, 2 * (j % 2), 0:HALF],
                                       ACT.Relu).then_inc(acc_act, 1)
                    u = c["unit"] + j
                    if kind == "last":
                        continue
                    if isinstance(u, int) and u + RING >= UNITS:
                        continue
                    used = j + 1 + UPS if prev is None else 2 * (j + 1) if kind == "up" else 4 * (j + 1)
                    hi_part((FF0 + j) % RING, (FF0 + j) % STAGE, u + RING, c["tile"] * 2 + used,
                            c["unit"] * (16 // STAGE) + 16 * ((j + RING) // STAGE + 1))
            mlp(act, segment)

            for t in range(QT + 1):
                r = rows[t]
                act.wait_ge(y_c, 3 * (t + 1))
                act.activation(y_sd[0:r, t:t + 1], y_mv[0:r, t, 1:2], ACT.Sqrt, bias=eps[0:r, 0:1]).then_inc(y_std, 1)
                act.wait_ge(y_rec, 2 * (t + 1))
                for j in (1, 0):
                    act.activation(y_n[0:r, t, 512 * j:512 * (j + 1)], y_banks(t)[j][0:r, :], ACT.Identity,
                                   bias=y_sh[0:r, t:t + 1], scale=y_rs[0:r, t:t + 1]).then_inc(yt_read, 1)

        @block.vector
        def _(dve):
            def x_scale(o):
                t = X_ORDER[o]
                r = rows[t]
                dve.wait_ge(x_std, o + 1)
                dve.reciprocal(x_rs[0:r, t:t + 1], x_sd[0:r, t:t + 1]).then_inc(x_rec, 1)
                dve.wait_ge(x_rec, 2 * o + 1)
                dve.scalar_tensor_tensor(x_sh[0:r, t:t + 1], x_mv[0:r, t, 0:1], -1.0, x_rs[0:r, t:t + 1],
                                         ALU.mult, ALU.mult).then_inc(x_rec, 1)

            for o, t in enumerate(X_ORDER):
                r = rows[t]
                dve.wait_ge(x_loaded[t], 16)
                for j in range(2):
                    dve.bn_stats(x_st[0:r, t, 6 * j:6 * j + 6],
                                 xin[0:r, t, 512 * j:512 * (j + 1)]).then_inc(x_stat, 1)
                dve.wait_ge(x_stat, 3 * o + 2)
                dve.bn_aggr(x_mv[0:r, t, :], x_st[0:r, t, :]).then_inc(x_stat, 1)
                if o:
                    x_scale(o - 1)
            x_scale(QT)
            dve.wait_ge(x_rec, 2 * (QT + 1))
            t = X_ORDER[QT]
            dve.tensor_scalar(xin[:, t, :], xin[:, t, :], x_rs[:, t:t + 1], x_sh[:, t:t + 1], ALU.mult,
                              ALU.add).then_inc(x_norm_dve, 1)
            dve.wait_ge(const_loaded, 32)

            def x_odd(k):
                dve.wait_ge(hi_odd, (k + 1) // 2)
                dve.tensor_tensor(h_lo[:, k, :], x_n[:, k, :], h_hi[:, k, :].bitcast(F32),
                                  ALU.subtract).then_inc(h_odd, 1)
            for k in range(0, KT, 2):
                dve.wait_ge(xt_ready, k + 1)
                for dst, src in zip((slice(0, SEQ), slice(SEQ, T)), xt_banks(k)):
                    dve.tensor_scalar(x_n[:, k, dst], src, lnp[:, 0, k:k + 1], lnp[:, 1, k:k + 1],
                                      ALU.mult, ALU.add).then_inc(xn_even, 1)
                dve.wait_ge(xn_even, k + 2)
                dve.tensor_copy(h_hi[:, k, :], x_n[:, k, :]).then_inc(hi_even, 1)
                if k >= 2:
                    x_odd(k - 1)
            x_odd(KT - 1)
            dve.wait_ge(init, 5)

            def read_half(u):
                i, j = divmod(u, 3)
                dve.wait_ge(half_done, 2 * u + 2)
                src = acc[:, 1, 0:HALF]
                if u >= 18:
                    dve.tensor_copy(z_c[:, C_TILE[u - 18], HALF:T], src).then_inc(acc_dve, 1)
                    return
                if i >= 2 and j == 0:
                    dve.wait_ge(z_copied, i - 1)
                if j == 0:
                    for h in range(2):
                        r = slice(HD * h, HD * (h + 1))
                        op = dve.tensor_scalar(z_q[i % 2][r, h, HALF:T], acc[r, 1, 0:HALF], SCALE, None, ALU.mult)
                    op.then_inc(acc_dve, 1)
                else:
                    dve.tensor_copy(z_kv[i % 2][:, j - 1, HALF:T], src).then_inc(acc_dve, 1)

            for u in range(3):
                read_half(u)

            def row_max(n):
                i, s, t, h, L = item(n)
                b = n % 2
                dve.wait_ge(s_ready, n + 1)
                dve.tensor_reduce(mx[:, b:b + 1], s_bank[b][:, 0:L], AX_X, ALU.max).then_inc(d1, 1)
                dve.wait_ge(d1, n + 1)
                dve.tensor_scalar(nmx[:, b:b + 1], mx[:, b:b + 1], -1.0, None, ALU.mult).then_inc(max_ready, 1)

            def normalise(n):
                i, s, t, h, L = item(n)
                b = n % 2
                dve.wait_ge(p_written, n + 1)
                dve.reciprocal(rinv[:, b:b + 1], rsum[:, b:b + 1]).then_inc(d2, 1)
                dve.wait_ge(d2, n + 1)
                dve.tensor_scalar(prob[:, n % 3, 0:L], prob[:, n % 3, 0:L], rinv[:, b:b + 1], None,
                                  ALU.mult).then_inc(p_scaled, 1)

            def stick(n):
                i, s, t, h, L = item(n)
                b = n % 2
                dve.wait_ge(p_written, n + 1)
                back = keep[:, b, 0:L][:, ::-1]
                dve.tensor_tensor_scan(left[:, b, 0:L][:, ::-1], back, back, 1.0, ALU.mult, ALU.min).then_inc(d3, 1)
                dve.wait_ge(d3, n - 8 * PAIRS + 1)
                dve.tensor_tensor(prob[:, n % 3, 0:L - 1], prob[:, n % 3, 0:L - 1], left[:, b, 1:L],
                                  ALU.mult).then_inc(p_scaled, 1)

            dve.wait_ge(const2_loaded, 32)
            for n in range(ITEMS + 4):
                i, s = divmod(n, 8)
                if n < 8 * PAIRS:
                    row_max(n)
                if 1 <= n <= ITEMS:
                    normalise(n - 1) if n - 1 < 8 * PAIRS else stick(n - 1)
                if n < ITEMS and s == 2:
                    y, p = divmod(i, PAIRS)
                    dve.wait_ge(kv_t, 3 * i + 3)
                    dve.tensor_copy(kv_new[y][:, :, P * p:P * (p + 1)],
                                    acc[0:NS, 3, 0:2 * P].rearrange("t (w c) -> t w c", w=2)).then_inc(s_read, 1)
                if i >= 1 and s == 3:
                    dve.wait_ge(mhi_ready, i)
                    dve.tensor_tensor(m_lo[:, i - 1, 0:SEQ], o_bank[:, :], m_hi[:, i - 1, 0:SEQ].bitcast(F32),
                                      ALU.subtract).then_inc(m_ready, 1)
                if n < ITEMS and s in (2, 5, 7):
                    read_half(3 * (i + 1) + (2, 5, 7).index(s))
            read_half(21)

            dve.wait_ge(kv_out[0], 16 * 6)
            dve.wait_ge(kv_out[1], 16 * 6)
            dve.memset(vt[:, QT, :], 0.0).then_inc(vt_zero, 1)
            dve.memset(wbd[:, :, :], 0.0).then_inc(wbd_zero, 1)
            def bc(j):
                return v_s[:, j, :].rearrange("p (a o) -> p a o", o=1).to_broadcast([P, (QT + 1) * GROUPS, HD])
            def s_max(g):
                dve.wait_ge(sc_pe, g + 1)
                at = 4 * g
                dve.tensor_reduce(s_st[:, at:at + 1], t_bank[:, 0:SK], AX_X, ALU.max).then_inc(e1, 1)
                dve.wait_ge(e1, g + 1)
                dve.tensor_scalar(s_st[:, at + 1:at + 2], s_st[:, at:at + 1], -1.0, None, ALU.mult).then_inc(e2, 1)

            def s_scale(g):
                dve.wait_ge(sp_written, g + 1)
                if g < 2:
                    dve.reciprocal(s_st[:, 4 * g + 3:4 * g + 4], s_st[:, 4 * g + 2:4 * g + 3]).then_inc(s_scaled, 1)
                else:
                    back = sw[0][:, ::-1]
                    dve.tensor_tensor_scan(sw[1][:, ::-1], back, back, 1.0, ALU.mult, ALU.min).then_inc(e4, 1)
                    dve.wait_ge(e4, g - 1)
                    dve.tensor_tensor(s_prob[:, 0:SK - 1], s_prob[:, 0:SK - 1], sw[1][:, 1:SK], ALU.mult).then_inc(s_scaled, 1)

            vg = vt[:, :, :].rearrange("p t (g d) -> p (t g) d", d=HD)
            vall = vsq[:, :, :].rearrange("p t (g d) -> p (t g) d", d=HD)
            dve.wait_ge(vt_read, 3)
            dve.tensor_reduce(v_s[:, 0, :], vg, AX_X, ALU.add).then_inc(v_chain, 1)
            dve.wait_ge(v_chain, 1)
            dve.tensor_scalar(v_s[:, 1, :], v_s[:, 0, :], 1.0 / HD, None, ALU.mult).then_inc(v_chain, 1)
            dve.wait_ge(v_chain, 2)
            dve.tensor_tensor(vg, vg, bc(1), ALU.subtract).then_inc(v_chain, 1)
            s_max(0)
            dve.wait_ge(v_sq, 1)
            dve.tensor_reduce(v_s[:, 1, :], vall, AX_X, ALU.add).then_inc(v_chain, 1)
            dve.wait_ge(v_sq, 2)
            dve.reciprocal(v_s[:, 3, :], v_s[:, 2, :]).then_inc(v_chain, 1)
            dve.wait_ge(v_chain, 5)
            dve.tensor_tensor(vg, vg, bc(3), ALU.mult).then_inc(v_chain, 1)
            tmp = vsq[:, :, :].rearrange("p t c -> p (t c)")

            def mix(j, cols, src, at, parts, width):
                done = 2 * (j + (2 if at >= 2 * SEQ else 0))
                n = parts * width
                tj = tmp[:, at:at + n].rearrange("p (c t) -> p c t", t=width)
                row = bsp[:, j, 0:width].rearrange("p (o t) -> p o t", o=1).to_broadcast([P, parts, width])
                dve.tensor_tensor(tj, src.rearrange("p (c t) -> p c t", t=width), row, ALU.add).then_inc(mix_dve, 1)
                dve.wait_ge(mix_dve, done + 1)
                dve.tensor_tensor(z_c[:, j, cols], z_c[:, j, cols], tmp[:, at:at + n], ALU.mult).then_inc(mix_dve, 1)

            def mix_rest(count, cols):
                dve.wait_ge(mix_hi, count)
                dve.tensor_tensor(m_lo[:, 6:8, cols], z_c[:, 0:2, cols], m_hi[:, 6:8, cols].bitcast(F32),
                                  ALU.subtract).then_inc(mix_lo, 1)

            for gi in range(1, 5):
                g = gi - 1
                y, grp = divmod(g, 2)
                if g == 0:
                    s_scale(0)
                    s_max(1)
                if g < 3:
                    s_scale(g + 1)
                if g == 2:
                    mix_rest(1, slice(0, SEQ))
                dve.wait_ge(pv_pe, g + 1)
                dve.wait_ge(s_scaled, g + 1)
                dve.scalar_tensor_tensor(s_om[:, :], s_bank[0][:, 0:W_ATT], s_st[:, 4 * g + 3:4 * g + 4] if y == 0 else 1.0,
                                         c_("s_head"), ALU.mult, ALU.mult).then_inc(om_done, 1)
                dve.wait_ge(ot_hi, g + 1)
                dst = slice(SEQ + 16 * grp, SEQ + 16 * (grp + 1))
                dve.tensor_tensor(m_lo[:, 3 * y:3 * y + 3, dst], s_bank[1][:, 0:48].rearrange("p (t c) -> p t c", c=16),
                                  m_hi[:, 3 * y:3 * y + 3, dst].bitcast(F32), ALU.subtract).then_inc(ot_lo, 1)
                if gi == 1:
                    dve.wait_ge(g_loaded, 16 * (3 + GROUPS + NB))
                    for j, op in enumerate((ALU.mult, ALU.add)):
                        dve.wait_ge(v_chain, 6 + j)
                        row = lnc[:, j, :].rearrange("p (o c) -> p o c", o=1).to_broadcast([P, QT + 1, W_C])
                        dve.tensor_tensor(vt[:, :, :], vt[:, :, :], row, op).then_inc(v_chain, 1)
                if gi == 2:
                    dve.wait_ge(gelu_done, 2)
                    for j in range(2):
                        dve.wait_ge(mix_ready, j + 1)
                        mix(j, slice(0, SEQ), acc[:, j, :], SEQ * j, QT, CHUNK)
                if gi == 3:
                    dve.wait_ge(mix_ready, 3)
                    for j in range(2):
                        mix(j, slice(SEQ, T), s_bank[1][:, 64 + NS * j:64 + NS * (j + 1)], 2 * SEQ + NS * j, NB, NQ)
                if gi == 3:
                    mix_rest(2, slice(SEQ, T))

            def centre(hf, ks):
                dve.wait_ge(mean_sb, hf + 1)
                for k in ks:
                    dve.tensor_tensor(res[:, k, halves(hf)], res[:, k, halves(hf)], mean_b[:, halves(hf)],
                                      ALU.subtract).then_inc(cent, 1)

            def normed(hf, k):
                dve.scalar_tensor_tensor(res[:, k, halves(hf)], res[:, k, halves(hf)], lnp[:, 2, k:k + 1],
                                         rstd_b[:, halves(hf)], ALU.mult, ALU.mult).then_inc(nrm, 1)

            def h1_rest(hf, k):
                dve.wait_ge(h1_hi, KT * hf + k + 1)
                dve.scalar_tensor_tensor(h_lo[:, k, halves(hf)], res[:, k, halves(hf)], lnp[:, 3, k:k + 1],
                                         h_hi[:, k, halves(hf)].bitcast(F32), ALU.add, ALU.subtract).then_inc(h1_lo, 1)

            def res_part(hf):
                return lambda k: res[:, k, halves(hf)]

            def sq_part(k):
                return sq[:, k, :]

            def add_up(total, part, hf, k, counter):
                if k == 0:
                    return
                if k > 1:
                    dve.wait_ge(counter, (KT - 1) * hf + k - 1)
                first = part(0) if k == 1 else total[:, halves(hf)]
                dve.tensor_tensor(total[:, halves(hf)], first, part(k), ALU.add).then_inc(counter, 1)

            dve.wait_ge(out_s, 16 * 5)
            dve.wait_ge(ot_lo, 4)
            for q, (hf, m) in enumerate(OUT_ORDER):
                if hf == 0:
                    dve.tensor_tensor(res[:, m, :], h_hi[:, m, :].bitcast(F32), h_lo[:, m, :].bitcast(F32),
                                      ALU.add).then_inc(stream, 1)
                    dve.wait_ge(stream, m + 1)
                dve.wait_ge(half_done, 2 * IN_UNITS + q + 1)
                dve.scalar_tensor_tensor(res[:, m, halves(hf)], res[:, m, halves(hf)], ALPHA,
                                         out_bank(q), ALU.mult, ALU.add).then_inc(acc_dve, 1)
                dve.wait_ge(acc_dve, IN_UNITS + q + 1)
                add_up(r_sum, res_part(hf), hf, m, r_sums)
                if q == KT + 1:
                    centre(0, range(KT))
                if q == KT + 2:
                    for k in range(KT):
                        dve.wait_ge(sq_done, k + 1)
                        add_up(sq_sum, sq_part, 0, k, sq_sums)
                if q == KT + 4:
                    dve.wait_ge(std_done, 1)
                    dve.reciprocal(rstd_b[:, halves(0)], sd_b[:, halves(0)]).then_inc(rstd_done, 1)
                    dve.wait_ge(rstd_done, 1)
                    for k in range(KT):
                        normed(0, k)
                if q == KT + 6:
                    for k in range(KT):
                        h1_rest(0, k)
            for k in range(KT + 2):
                if k < KT:
                    centre(1, range(k, k + 1))
                if k >= 2:
                    dve.wait_ge(sq_done, KT + k - 1)
                    add_up(sq_sum, sq_part, 1, k - 2, sq_sums)
            dve.wait_ge(std_done, 2)
            dve.reciprocal(rstd_b[:, halves(1)], sd_b[:, halves(1)]).then_inc(rstd_done, 1)
            dve.wait_ge(rstd_done, 2)
            for k in range(KT + 2):
                if k < KT:
                    normed(1, k)
                if k >= 2:
                    h1_rest(1, k - 2)

            def up_tile(j, par, cols, sq_sem, sq_count, hi_sem, hi_count):
                dve.tensor_tensor(hid[:, j % 2, cols], relu[:, j, cols], relu[:, j, cols], ALU.mult).then_inc(sq_sem, 1)
                dve.wait_ge(sq_sem, sq_count)
                dve.tensor_copy(m_hi[:, FG * par + j, cols], hid[:, j % 2, cols]).then_inc(hi_sem, 1)
                dve.wait_ge(hi_sem, hi_count)
                return dve.tensor_tensor(m_lo[:, FG * par + j, cols], hid[:, j % 2, cols],
                                         m_hi[:, FG * par + j, cols].bitcast(F32), ALU.subtract)

            def norm2_stats(t):
                r = rows[t]
                dve.wait_ge(yt_pe, t + 1)
                for j in range(2):
                    dve.bn_stats(y_st[0:r, t, 6 * j:6 * j + 6], y_banks(t)[j][0:r, :]).then_inc(y_c, 1)
                dve.wait_ge(y_c, 3 * t + 2)
                dve.bn_aggr(y_mv[0:r, t, :], y_st[0:r, t, :]).then_inc(y_c, 1)

            def norm2_scale(t):
                r = rows[t]
                dve.wait_ge(y_std, t + 1)
                dve.reciprocal(y_rs[0:r, t:t + 1], y_sd[0:r, t:t + 1]).then_inc(y_rec, 1)
                dve.wait_ge(y_rec, 2 * t + 1)
                dve.scalar_tensor_tensor(y_sh[0:r, t:t + 1], y_mv[0:r, t, 0:1], -1.0, y_rs[0:r, t:t + 1],
                                         ALU.mult, ALU.mult).then_inc(y_rec, 1)

            def norm2_affine(t):
                r = rows[t]
                y = y_n[0:r, t, 512:1024]
                dve.wait_ge(yt_read, 2 * t + 1)
                dve.tensor_tensor(y, y, ln2[0:r, 0, 512:1024], ALU.mult).then_inc(y_nrm, 1)
                dve.wait_ge(y_nrm, t + 1)
                dve.tensor_tensor(y, y, ln2[0:r, 1, 512:1024], ALU.add).then_inc(y_b2, 1)

            def segment(kind, par, prev, c):
                if kind == "up" and prev is None:
                    def first_half(j):
                        dve.wait_ge(acc_act, c["act"] + j + 1)
                        up_tile(j, par, halves(0), head_sq, j + 1, head_hi, j + 1)

                    first_half(0)
                    first_half(1)
                    for j in range(UPS):
                        dve.wait_ge(half_done, 2 * c["tile"] + UPS + j + 1)
                        dve.tensor_scalar(relu[:, j, halves(1)], acc[:, 2 * (j % 2) + 1, 0:HALF], 0.0, None,
                                          ALU.max).then_inc(acc_dve, 1)
                        if j < 2:
                            first_half(j + 2)
                        dve.wait_ge(acc_dve, c["dve"] + j + 1)
                        up_tile(j, par, halves(1), sq_h, j + 1, hid_hi, j + 1).then_inc(hid_lo, 1)
                elif kind == "up":
                    for j in range(UPS):
                        done = c["up"] * FG + (j + 1)
                        dve.wait_ge(half_done, (c["tile"] + j) * 2 + 2)
                        dve.tensor_scalar(relu[:, j, HALF:T], acc[:, 2 * (j % 2) + 1, 0:HALF], 0.0, None,
                                          ALU.max).then_inc(acc_dve, 1)
                        dve.wait_ge(acc_act, c["act"] + (j + 1))
                        dve.wait_ge(acc_dve, c["dve"] + (j + 1))
                        up_tile(j, par, slice(0, T), sq_h, done, hid_hi, done).then_inc(hid_lo, 1)
                elif kind == "down":
                    for m in range(DOWNS):
                        for hf in range(2):
                            dve.wait_ge(half_done, (c["tile"] + m) * 2 + (hf + 1))
                            if m == 0 and hf == 0:
                                dve.wait_ge(res_a, KT)
                            dve.tensor_tensor(res[:, m, halves(hf)], res[:, m, halves(hf)],
                                              acc[:, 2 * (m % 2) + hf, 0:HALF], ALU.add).then_inc(acc_dve, 1)
                else:
                    for q in range(2 * DOWNS):
                        hf, m = divmod(q, DOWNS)
                        dve.wait_ge(half_done, c["tile"] * 2 + q + 1)
                        dve.tensor_tensor(res[:, m, halves(hf)], res[:, m, halves(hf)],
                                          acc[:, q % 4, 0:HALF], ALU.add).then_inc(acc_dve, 1)
                        for at, step, t in ((10, norm2_stats, 0), (11, norm2_scale, 0), (12, norm2_stats, 1),
                                            (13, norm2_scale, 1), (14, norm2_affine, 0)):
                            if q == at:
                                if q == 14:
                                    dve.wait_ge(ln2_loaded, 32)
                                step(t)
            mlp(dve, segment)

            norm2_affine(1)
            norm2_stats(2)
            norm2_scale(2)
            norm2_stats(3)
            norm2_scale(3)
            norm2_affine(2)
            norm2_stats(4)
            norm2_scale(4)
            norm2_affine(3)
            norm2_affine(4)

        @block.tensor
        def _(pe):
            def turn_x(k):
                if k >= 2:
                    pe.wait_ge((xn_even, xn_odd)[k % 2], 2 * (k // 2))
                main, rest = xt_banks(k)
                for t in range(QT):
                    if k == 0:
                        pe.wait_ge(*((x_norm, X_ORDER.index(t) + 1) if t != X_ORDER[-1] else (x_norm_dve, 1)))
                    pe.transpose(main[:, P * t:P * (t + 1)], xin[:, t, P * k:P * (k + 1)], ident(P))
                pe.transpose(rest, xin[0:NS, QT, P * k:P * (k + 1)], ident(NS)).then_inc(xt_ready, 1)

            pe.wait_ge(const_loaded, 32)
            for k in range(6):
                turn_x(k)

            def product(wh, wl, slot, cols, hi, lo, ks, out, hf, part=slice(None)):
                work = [(k, pas) for k in range(len(ks)) for pas in range(3)]
                for k, pas in work[part]:
                    w = (wh, wh, wl)[pas]
                    x = (hi, lo, hi)[pas]
                    last = k == len(ks) - 1 and pas == 2
                    mm = pe.matmul(out, w[:, slot, cols(k)], x[:, ks[k], halves(hf)],
                                   start=(k == 0 and pas == 0), stop=last)
                    if last:
                        mm.then_inc(half_done, 1)

            def cols(k):
                return slice(P * k, P * (k + 1))

            def in_unit(u, c):
                if c == 0:
                    pe.wait_ge(lo_done, u + 1)
                    if u:
                        pe.wait_ge(acc_act, u)
                if c == 4 and u:
                    pe.wait_ge(acc_dve, u)
                hf = c // 4
                product(w_hi, w_lo, u % RING, cols, h_hi, h_lo, range(KT), acc[:, hf, 0:HALF], hf,
                        slice(6 * (c % 4), 6 * (c % 4 + 1)))

            for u in range(3):
                for c in range(8):
                    if u == 0 and c < 4:
                        pe.wait_ge(h_even, c + 1)
                        pe.wait_ge(h_odd, c + 1)
                    in_unit(u, c)
                    if u == 0 and c == 0:
                        turn_x(6)
                        turn_x(7)
            pe.wait_ge(bias_ready, H + 3)

            def scores(n):
                i, s, t, h, L = item(n)
                b = n % 2
                if n >= 2:
                    pe.wait_ge(p_written, n - 1)
                q = z_q[i % 2][:, h, P * t:P * (t + 1)]
                out = s_bank[b]
                if i < PAIRS:
                    pe.matmul(out[:, 0:L], sid_r[:, 2 * i + h, :], dist_r[:, SEQ - L:SEQ], start=True, stop=False)
                    pe.matmul(out[:, 0:L], q, z_kv[i % 2][:, 0, 0:L], start=False, stop=True).then_inc(s_ready, 1)
                else:
                    pe.matmul(out[:, 0:L], q, z_kv[i % 2][:, 0, 0:L], start=True, stop=False)
                    pe.matmul(out[:, L - P:L], id_r[:, :], below_r[:, :], start=False, stop=True).then_inc(s_ready, 1)

            def turn_probs(n):
                i, s, t, h, L = item(n)
                pe.wait_ge(p_scaled, n + 1)
                if n >= 2:
                    pe.wait_ge(pt_read, n - 1)
                for kb in range(t + 1):
                    mm = pe.transpose(pt_bank(n)[:, P * kb:P * (kb + 1)], prob[:, n % 3, P * kb:P * (kb + 1)], ident(P))
                mm.then_inc(pt_ready, 1)

            def values(n):
                i, s, t, h, L = item(n)
                pe.wait_ge(pt_read, n + 1)
                if t == 0:
                    pe.wait_ge(kv_act, 2 * i + 2)
                    if i:
                        pe.wait_ge(m_ready, i)
                for kb in range(t + 1):
                    for hh in range(2):
                        r = slice(HD * hh, HD * (hh + 1))
                        mm = pe.matmul(o_bank[r, P * t:P * (t + 1)], v_tok[i % 2][:, kb, r],
                                       prob_t[hh][:, t * (t + 1) // 2 + kb, :], start=(kb == 0), stop=(kb == t))
                mm.then_inc(o_ready, 1)

            def turn_kv(i, s):
                src = z_kv[i % 2]
                if s == 0:
                    pe.wait_ge(acc_act, 3 * i + 3)
                    pe.wait_ge(acc_dve, 3 * i + 3)
                    if i:
                        pe.wait_ge(s_read, i)
                else:
                    pe.wait_ge(kv_act, 2 * i + s)
                if s < 2:
                    for t in range(QT):
                        mm = pe.transpose(acc[:, 3, P * t:P * (t + 1)], src[:, s, P * t:P * (t + 1)], ident(P))
                else:
                    for w in range(2):
                        mm = pe.transpose(acc[0:NS, 3, P * w:P * (w + 1)], src[:, w, SEQ:T], ident(P))
                mm.then_inc(kv_t, 1)

            fill = [(u, c) for u in range(3, IN_UNITS) for c in range(8)]
            for n in range(ITEMS + 4):
                i, s = divmod(n, 8)
                if n < ITEMS:
                    if s == 0:
                        pe.wait_ge(acc_act, 3 * i + 2)
                        pe.wait_ge(acc_dve, 3 * i + 2)
                    scores(n)
                for uc in fill[3 * n:3 * n + 1]:
                    in_unit(*uc)
                if 2 <= n < ITEMS + 2:
                    turn_probs(n - 2)
                for uc in fill[3 * n + 1:3 * n + 2]:
                    in_unit(*uc)
                if n >= 4 and n % 2 == 0:
                    values(n - 3)
                if n < ITEMS and s < 3:
                    turn_kv(i, s)
                for uc in fill[3 * n + 2:3 * n + 3]:
                    in_unit(*uc)

            def out_half(q, ks=range(KT)):
                hf, m = OUT_ORDER[q]
                if ks[0] == 0:
                    pe.wait_ge(lo_done, IN_UNITS + m + 1)
                    if q >= 4:
                        pe.wait_ge(acc_dve, IN_UNITS + q - 3)
                wh, wl, slot = (w_hi, w_lo, (IN_UNITS + m) % RING) if m < RING else (wo_hi, wo_lo, m - RING)
                product(wh, wl, slot, cols, m_hi, m_lo, range(KT), out_bank(q), hf,
                        slice(3 * ks[0], 3 * (ks[-1] + 1)))

            def over_partitions(hf, bank, total, ready, done):
                pe.wait_ge(ready, (KT - 1) * (hf + 1))
                pe.matmul(bank[:, 0:HALF], c_("mean"), total[:, halves(hf)], start=True, stop=True).then_inc(done, 1)

            def mean_step(hf):
                over_partitions(hf, s_bank[hf], r_sum, r_sums, mean_pe)

            def var_step(hf):
                over_partitions(hf, (t_bank, o_bank)[hf], sq_sum, sq_sums, sq_pe)

            pe.wait_ge(m_ready, 5)
            out_half(0, range(0, 3))
            pe.wait_ge(m_ready, 6)
            pe.wait_ge(gelu_done, 1)
            pe.wait_ge(acc_act, IN_UNITS)
            pe.wait_ge(acc_dve, IN_UNITS)
            for t in range(QT):
                for ct in range(2):
                    mm = pe.transpose(acc[:, t // 2, W_C * (t % 2) + P * ct:W_C * (t % 2) + P * (ct + 1)],
                                      z_c[:, 2 + ct, P * t:P * (t + 1)], ident(P))
            mm.then_inc(vt_ready, 1)

            def s_scores(gi):
                y, grp = divmod(gi, 2)
                for n in range(4 * gi, 4 * gi + 4):
                    pe.wait_ge(kp_loaded[n % K_RING], 16 * PAGES * (n // K_RING + 1))
                if gi == 0:
                    pe.wait_ge(sb_ready, 2)
                    pe.wait_ge(z_copied, 6)
                if gi:
                    pe.wait_ge(sp_written, gi)
                pe.matmul(t_bank[:, 0:SK], id_r[:, :], sb_r[:, gi, :], start=True, stop=False)
                for new in range(2):
                    for p in range(PAIRS):
                        for b4 in range(4):
                            out = t_bank[32 * b4:32 * (b4 + 1), PAST:SK] if new else t_bank[32 * b4:32 * (b4 + 1), 0:PAST]
                            keys = k_new[y][:, p, :] if new else keys_of(4 * gi + b4)[:, :, p, :]
                            mm = pe.matmul(out, qbd[y][:, 4 * grp + b4, p, :], keys, start=False,
                                           stop=(new == 1 and p == PAIRS - 1), tile_position=(0, 32 * b4))
                mm.then_inc(sc_pe, 1)

            def turn_s_probs(g):
                pe.wait_ge(sp_written, g + 1)
                if g >= 2:
                    pe.wait_ge(s_scaled, g + 1)
                if g:
                    pe.wait_ge(st_act, 2 * g)
                pe.transpose(o_bank[:, 0:P], s_prob[:, 0:P], ident(P))
                pe.transpose(o_bank[:, P:2 * P], s_prob[:, P:2 * P], ident(P))
                pe.transpose(o_bank[0:NS, 2 * P:3 * P], s_prob[:, 2 * P:SK], ident(P)).then_inc(st_pe, 1)

            def s_values(g):
                y = g // 2
                pe.wait_ge(st_act, 2 * (g + 1))
                if g:
                    pe.wait_ge(om_done, g)
                for pg in range(PAGES + 1):
                    for b4 in range(4):
                        if pg == 0:
                            pe.wait_ge(vp_loaded[b4], 16 * PAGES * (g + 1))
                        r = slice(32 * b4, 32 * (b4 + 1))
                        if pg < PAGES:
                            pe.matmul(s_bank[0][r, 0:W_ATT], s_pt[:, pg, r], v_pg[:, b4, pg, :], start=(pg == 0),
                                      stop=False, tile_position=(0, 32 * b4))
                        else:
                            mm = pe.matmul(s_bank[0][r, 0:W_ATT], s_pt[0:NS, 2, r], kv_new[y][:, 1, :], start=False,
                                           stop=True, tile_position=(0, 32 * b4))
                mm.then_inc(pv_pe, 1)

            def s_pick(g):
                pe.wait_ge(om_done, g + 1)
                if g:
                    pe.wait_ge(ot_lo, g)
                if g == 3:
                    pe.wait_ge(mix_dve, 8)
                for p in range(PAIRS):
                    mm = pe.matmul(s_bank[1][:, 16 * p:16 * (p + 1)], s_om[:, P * p:P * (p + 1)], c_("s_pick"),
                                   start=True, stop=True)
                mm.then_inc(ot_pe, 1)

            def mix_rows():
                pe.wait_ge(v_chain, 8)
                pe.wait_ge(vt_read, 3)
                pe.wait_ge(wsp_ready, 2 * GROUPS)
                for j in range(2):
                    for ch in range(QT):
                        for g2 in range(2):
                            g = 2 * j + g2
                            mm = pe.matmul(acc[HD * g2:HD * (g2 + 1), j, CHUNK * ch:CHUNK * (ch + 1)],
                                           vt[:, ch, HD * g:HD * (g + 1)], wsp[:, g, :], start=True, stop=True)
                    mm.then_inc(mix_ready, 1)

            def mix_samples():
                pe.wait_ge(vt_read, 3)
                pe.wait_ge(ot_lo, 3)
                for j in range(2):
                    for g2 in range(2):
                        g = 2 * j + g2
                        mm = pe.matmul(s_bank[1][HD * g2:HD * (g2 + 1), 64 + NS * j:64 + NS * (j + 1)],
                                       vt[0:NS, QT, HD * g:HD * (g + 1)], wbd[:, g, :], start=True, stop=True)
                mm.then_inc(mix_ready, 1)

            out_half(0, range(3, 6))
            pe.wait_ge(vt_read, 1)
            for ct in range(2):
                mm = pe.transpose(acc[0:NS, 0, P * ct:P * (ct + 1)], z_c[:, 2 + ct, SEQ:T], ident(P))
            mm.then_inc(vt_ready, 1)
            s_scores(0)
            out_half(1, range(0, 4))
            turn_s_probs(0)
            out_half(1, range(4, 6))
            for g in range(3):
                s_scores(g + 1)
                s_values(g)
                if g == 1:
                    mix_rows()
                turn_s_probs(g + 1)
                if g == 2:
                    pe.wait_ge(mix_dve, 4)
                    out_half(2, range(0, 4))
                    pe.wait_ge(mix_lo, 1)
                    out_half(0, range(6, KT))
                s_pick(g)
            out_half(1, range(6, KT))
            mix_samples()
            out_half(2, range(4, KT))
            s_values(3)
            out_half(3, range(0, 4))
            s_pick(3)
            out_half(3, range(4, KT))
            pe.wait_ge(ot_lo, 4)
            pe.wait_ge(mix_lo, 2)
            for q in range(4, 2 * KT):
                if q == KT + 4:
                    out_half(q, range(0, 4))
                    var_step(0)
                    out_half(q, range(4, KT))
                else:
                    out_half(q)
                if q == KT + 1:
                    mean_step(0)

            def up_half(j, hf, part=slice(None)):
                product(w_hi, w_lo, (FF0 + j) % RING, cols, h_hi, h_lo, range(KT),
                        acc[:, 2 * (j % 2) + hf, 0:HALF], hf, part)

            def down_half(j, mj, par, out, hf):
                product(w_hi, w_lo, (FF0 + j) % RING, lambda f: slice(2 * P * f + P * mj, 2 * P * f + P * (mj + 1)),
                        m_hi, m_lo, [FG * par + f for f in range(FG)], out, hf)

            def segment(kind, par, prev, c):
                first = (0, 2) if prev == "down" else (1, 1)
                if kind == "up" and prev is None:
                    for hf in range(2):
                        for j in range(UPS):
                            if hf == 0:
                                pe.wait_ge(lo_done, c["unit"] + j + 1)
                            if j < 2:
                                pe.wait_ge(acc_dve, c["dve"] - (1 if j + hf == 0 else 0))
                            else:
                                pe.wait_ge(*((acc_act, c["act"] + j - 1) if hf == 0 else (acc_dve, c["dve"] + j - 1)))
                            if j == 0:
                                for kk in range(KT):
                                    pe.wait_ge(h1_lo, KT * hf + kk + 1)
                                    up_half(j, hf, slice(3 * kk, 3 * kk + 3))
                                    if hf == 0 and kk == 5:
                                        mean_step(1)
                            elif hf == 0 and j == 2:
                                up_half(j, hf, slice(0, 18))
                                var_step(1)
                                up_half(j, hf, slice(18, 24))
                            else:
                                up_half(j, hf)
                elif kind == "up":
                    for j in range(UPS):
                        pe.wait_ge(lo_done, c["unit"] + (j + 1))
                        a, d = (j - 1, j - 1) if j else (-first[0], -first[1])
                        pe.wait_ge(acc_act, c["act"] + a)
                        pe.wait_ge(acc_dve, c["dve"] + d)
                        for hf in range(2):
                            up_half(j, hf)
                elif kind == "down":
                    pe.wait_ge(hid_lo, (c["down"] + 1) * FG)
                    for j in range(FG):
                        pe.wait_ge(lo_done, c["unit"] + (j + 1))
                        for mj in range(2):
                            m = 2 * j + mj
                            a, d = (0, 2 * (m - 1)) if m else (-first[0], -first[1])
                            pe.wait_ge(acc_act, c["act"] + a)
                            pe.wait_ge(acc_dve, c["dve"] + d)
                            for hf in range(2):
                                down_half(j, mj, par, acc[:, 2 * (m % 2) + hf, 0:HALF], hf)
                else:
                    pe.wait_ge(hid_lo, (c["down"] + 1) * FG)
                    for q in range(2 * DOWNS):
                        hf, m = divmod(q, DOWNS)
                        if hf == 0 and m % 2 == 0:
                            pe.wait_ge(lo_done, c["unit"] + m // 2 + 1)
                        pe.wait_ge(acc_dve, c["dve"] + (q - 3 if q >= 4 else 0 if q >= 2 else -2))
                        down_half(m // 2, m % 2, par, acc[:, q % 4, 0:HALF], hf)
                        if q in (9, 11):
                            turn_stream((q - 9) // 2)

            def turn_stream(t):
                r = rows[t]
                if t == 0:
                    pe.wait_ge(acc_dve, DVE_END - DOWNS)
                if t == 2:
                    pe.wait_ge(acc_dve, DVE_END)
                if t == QT:
                    pe.wait_ge(yt_read, 2)
                for m in range(KT):
                    mm = pe.transpose(y_banks(t)[m // 4][0:r, P * (m % 4):P * (m % 4 + 1)],
                                      res[:, m, P * t:P * t + r], ident(P))
                mm.then_inc(yt_pe, 1)
            mlp(pe, segment)
            for t in range(2, QT + 1):
                turn_stream(t)


def constants():
    c = np.zeros((P, CONSTS + SEQ), np.float32)
    s = np.zeros((P, S_CONSTS), np.float32)

    def put(name, a):
        to, where = (c, CONST) if name in CONST else (s, S_CONST)
        at, n = where[name]
        to[:a.shape[0], at:at + n] = a
    i = np.arange(P)[:, None]
    put("ident", np.eye(P))
    j = np.arange(SEQ)[None, :] - (SEQ - P)
    c[:, CONSTS:] = np.where(j <= i, j - i, NEG)
    j = np.arange(P)[None, :]
    put("below_neg", np.where(j < i, 0.0, NEG))
    put("upto", i <= j)
    b, hq = i // 32, i % 32
    h, q = hq // NQ, hq % NQ
    slope = np.array(SLOPES + [0.0, 0.0])[h]
    key = np.arange(SK)[None, :]
    new = key - PAST
    rel = new % NQ - q
    for grp in range(2):
        at = np.arange(grp * SK, (grp + 1) * SK)
        own = (new >= 0) & (new // NQ == 4 * grp + b)
        for name, a in (("s_bias", np.where(key < PAST, slope * (new - q), np.where(own & (rel <= 0), slope * rel, NEG))),
                        ("s_neg", np.where((key < PAST) | (own & (rel < 0)), 0.0, NEG))):
            s[:, S_CONST[name][0] + at] = a
    put("mean", np.full((P, P), 1.0 / D_MODEL))
    put("s_head", (np.arange(W_ATT)[None, :] // HD == h))
    bb = np.arange(16)[None, :]
    put("s_pick", (bb // NQ == b) & (bb % NQ == q) & (h < H))
    a, d = np.arange(NS)[:, None], np.arange(NS)[None, :]
    put("s_chunk", (a // NQ == d // NQ) & (a % NQ <= d % NQ))
    return c, s


def split_units(w_in, w_out, w_ff1, w_ff2):
    def columns(w, at, n=P):
        return w[:, at:at + n].reshape(-1, P, n).transpose(1, 0, 2).reshape(P, -1)
    units = []
    for y in range(2):
        for p in range(PAIRS):
            units += [columns(w_in, (3 * y + s) * W_ATT + P * p) for s in range(3)]
    units += [columns(w_in, 6 * W_ATT + P * j) for j in C_TILE]
    units += [columns(w_out, P * m) for m in range(OUT_UNITS)]

    def up(g):
        return [columns(w_ff1, P * (FG * g + j)) for j in range(FG)]

    def down(g):
        rows = w_ff2[P * FG * g:P * FG * (g + 1)]
        return [columns(rows, 2 * P * j, 2 * P) for j in range(FG)]
    units += up(0)
    for g in range(1, NG):
        units += up(g) + down(g - 1)
    return np.stack(units + down(NG - 1))


def transposed_keys(cache):
    n = cache.shape[0] * cache.shape[1]
    return cache.reshape(n, PAGE, PAIRS, P).transpose(0, 3, 2, 1)


_OUTS = [("y_prompt", (1, SEQ, D_MODEL)), ("y_sample", (NB, NQ, D_MODEL)),
         ("k_a_prompt", (1, 1, SEQ, H, HD)), ("v_a_prompt", (1, 1, SEQ, H, HD)),
         ("k_b_prompt", (1, 1, SEQ, H, HD)), ("v_b_prompt", (1, 1, SEQ, H, HD)),
         ("k_a_sample", (1, NB, NQ, H, HD)), ("v_a_sample", (1, NB, NQ, H, HD)),
         ("k_b_sample", (1, NB, NQ, H, HD)), ("v_b_sample", (1, NB, NQ, H, HD)),
         ("v_c_sample", (1, NB, NQ, W_C))]


def kernel(x_prompt, x_sample, cache_k_a, cache_v_a, cache_k_b, cache_v_b, page_table, ln_in_g,
           ln_in_b, w_in, w_out, w_spatial, b_spatial, ln_c_g, ln_c_b, ln1_g, ln1_b, w_ff1, w_ff2,
           ln2_g, ln2_b):
    import concourse.bacc as bacc
    from concourse.bass_utils import run_bass_kernel_spmd

    a = {k: np.asarray(v) for k, v in locals().items()
         if k not in ("bacc", "run_bass_kernel_spmd")}
    arrays = {
        "x_prompt": a["x_prompt"], "x_sample": a["x_sample"],
        "weights": split_units(a["w_in"][0], a["w_out"][0], a["w_ff1"][0], a["w_ff2"][0]),
        "cache_k_a": transposed_keys(a["cache_k_a"]), "cache_v_a": a["cache_v_a"],
        "cache_k_b": transposed_keys(a["cache_k_b"]), "cache_v_b": a["cache_v_b"],
        "page_table": a["page_table"],
        "ln_cols": np.stack([v.reshape(KT, P).T for v in
                             (a["ln_in_g"], a["ln_in_b"], a["ln1_g"][0], a["ln1_b"][0])], axis=1),
        "w_spatial": a["w_spatial"][0].transpose(2, 0, 1),
        "b_spatial": a["b_spatial"][0],
        "lnc_g": a["ln_c_g"].reshape(1, W_C), "lnc_b": a["ln_c_b"].reshape(1, W_C),
        "ln2_g": a["ln2_g"].reshape(1, D_MODEL), "ln2_b": a["ln2_b"].reshape(1, D_MODEL),
        "consts": constants()[0], "s_consts": constants()[1],
    }
    nc = bacc.Bacc("TRN2", target_bir_lowering=False, num_devices=1)
    args = []
    for name, v in arrays.items():
        arrays[name] = v = np.ascontiguousarray(v)
        args.append(nc.dram_tensor(name, v.shape, mybir.dt.from_np(v.dtype), kind="ExternalInput").ap())
    for name, shape in _OUTS:
        args.append(nc.dram_tensor(name, shape, F32, kind="ExternalOutput").ap())
    hybrid_layer(nc, *args)
    r = run_bass_kernel_spmd(nc, [arrays], core_ids=[0]).results[0]
    return tuple(r[name] for name, _ in _OUTS)
```
